# Optimizing a Trainium2 kernel written in Bass

```python
import math
import jax, jax.numpy as jnp
from jax import lax
import numpy as np

D_MODEL = 1024
BATCH = 1
SEQ = 256
DEPTH = 2

N_MEM = 256
EPS = 1e-6

D_MIX = D_MODEL
D_CONV = D_MIX // 4
CONV_WIDTH = 31
SSD_HEAD_DIM = 64
D_SSD = D_MIX // 2
SSD_HEADS = D_SSD // SSD_HEAD_DIM
SSD_GROUPS = 2
SSD_STATE = 128
SSD_CONV = 4
SSD_CHUNK = 128
D_XBC = D_SSD + 2 * SSD_GROUPS * SSD_STATE
ATT_HEAD_DIM = 64
D_ATT = D_MIX // 4
ATT_HEADS = D_ATT // ATT_HEAD_DIM
IDX_HEADS = 8
IDX_DIM = 64
TOPK_MAX = 256
Q_BLOCK = 128
ROPE_THETA = 500000.0
ROT_DIM = ATT_HEAD_DIM // 4
D_IN = 2 * D_CONV + D_SSD + D_XBC + SSD_HEADS + 3 * D_ATT + IDX_HEADS * IDX_DIM + IDX_DIM + IDX_HEADS
MEM_HEADS = 4
MEM_HEAD_DIM = 64
D_MEMATT = MEM_HEADS * MEM_HEAD_DIM
D_FF = 2816
N_EXPERTS = 8
TOP_K = 2
MOE_BLOCK = 256
N_DENSE = (DEPTH + 1) // 2
N_MOE = DEPTH // 2

kernel_name = 'hybrid_conv_ssd_dsa_moe_block'

def rms_norm(x, g):
    xf = x.astype(jnp.float32)
    y = xf * lax.rsqrt(jnp.mean(xf * xf, axis=-1, keepdims=True) + EPS)
    return (y * g.astype(jnp.float32)).astype(x.dtype)

def layer_norm(x, g, b):
    xf = x.astype(jnp.float32)
    mu = jnp.mean(xf, axis=-1, keepdims=True)
    xc = xf - mu
    y = xc * lax.rsqrt(jnp.mean(xc * xc, axis=-1, keepdims=True) + EPS)
    return (y * g.astype(jnp.float32) + b.astype(jnp.float32)).astype(x.dtype)

def rope_tables(positions):
    inv = ROPE_THETA ** (-jnp.arange(0, ROT_DIM, 2, dtype=jnp.float32) / ROT_DIM)
    ang = positions.astype(jnp.float32)[..., None] * inv
    return jnp.cos(ang), jnp.sin(ang)

def partial_rope(x, cos, sin):
    half = ROT_DIM // 2
    c = cos[:, :, None, :]
    s = sin[:, :, None, :]
    xf = x.astype(jnp.float32)
    x1 = xf[..., :half]
    x2 = xf[..., half:ROT_DIM]
    out = jnp.concatenate([x1 * c - x2 * s, x2 * c + x1 * s, xf[..., ROT_DIM:]], axis=-1)
    return out.astype(x.dtype)

def causal_dwconv(x, w):
    k = w.shape[0]
    return lax.conv_general_dilated(
        x, w[:, None, :].astype(x.dtype), window_strides=(1,), padding=[(k - 1, 0)],
        dimension_numbers=('NWC', 'WIO', 'NWC'), feature_group_count=x.shape[-1])

def conformer_conv(u, dw_w, ln_g, ln_b, pw_w):
    h = u[..., :D_CONV] * jax.nn.sigmoid(u[..., D_CONV:])
    h = causal_dwconv(h, dw_w)
    h = jax.nn.silu(layer_norm(h, ln_g, ln_b))
    return h @ pw_w.astype(h.dtype)

def _segsum(a):
    cs = jnp.cumsum(a, axis=-1)
    seg = cs[..., :, None] - cs[..., None, :]
    t = a.shape[-1]
    mask = jnp.tril(jnp.ones((t, t), dtype=bool))
    return jnp.where(mask, seg, -jnp.inf)

def ssd_chunked(xd, a, bm, cm):
    b, s, h, p = xd.shape
    n = bm.shape[-1]
    c, l = s // SSD_CHUNK, SSD_CHUNK
    xd = xd.reshape(b, c, l, h, p)
    bm = bm.reshape(b, c, l, h, n)
    cm = cm.reshape(b, c, l, h, n)
    a = a.reshape(b, c, l, h).transpose(0, 3, 1, 2)
    a_cs = jnp.cumsum(a, axis=-1)
    decay_in = jnp.exp(_segsum(a))
    cb = jnp.einsum('bclhn,bcshn->bhcls', cm, bm) * decay_in
    y_diag = jnp.einsum('bhcls,bcshp->bclhp', cb, xd)
    decay_states = jnp.exp(a_cs[..., -1:] - a_cs).transpose(0, 2, 3, 1)
    states = jnp.einsum('bclhn,bclhp->bchpn', bm * decay_states[..., None], xd)
    states = jnp.concatenate([jnp.zeros_like(states[:, :1]), states], axis=1)
    decay_chunk = jnp.exp(_segsum(jnp.pad(a_cs[..., -1], ((0, 0), (0, 0), (1, 0)))))
    states = jnp.einsum('bhzc,bchpn->bzhpn', decay_chunk, states)[:, :-1]
    y_off = jnp.einsum('bclhn,bchpn->bclhp', cm, states) * jnp.exp(a_cs).transpose(0, 2, 3, 1)[..., None]
    return (y_diag + y_off).reshape(b, s, h, p)

def ssd_mixer(z, xbc, dt_raw, conv_w, conv_b, dt_bias, a_log, d_skip, norm_g):
    b, s, _ = xbc.shape
    xbc = jax.nn.silu(causal_dwconv(xbc, conv_w) + conv_b.astype(xbc.dtype))
    xs = xbc[..., :D_SSD].reshape(b, s, SSD_HEADS, SSD_HEAD_DIM).astype(jnp.float32)
    bc = xbc[..., D_SSD:].reshape(b, s, 2, SSD_GROUPS, SSD_STATE).astype(jnp.float32)
    rep = SSD_HEADS // SSD_GROUPS
    bm = jnp.repeat(bc[:, :, 0], rep, axis=2)
    cm = jnp.repeat(bc[:, :, 1], rep, axis=2)
    dt = jax.nn.softplus(dt_raw.astype(jnp.float32) + dt_bias.astype(jnp.float32))
    a = -jnp.exp(a_log.astype(jnp.float32))
    y = ssd_chunked(xs * dt[..., None], dt * a, bm, cm)
    y = y + xs * d_skip.astype(jnp.float32)[:, None]
    y = y.reshape(b, s, D_SSD) * jax.nn.silu(z.astype(jnp.float32))
    y = rms_norm(y.reshape(b, s, SSD_GROUPS, D_SSD // SSD_GROUPS),
                 norm_g.reshape(SSD_GROUPS, D_SSD // SSD_GROUPS)).reshape(b, s, D_SSD)
    return y.astype(z.dtype)

def dsa_attention(q, k, v, q_idx, k_idx, w_idx, cos, sin, q_g, k_g):
    b, s, _ = q.shape
    q = partial_rope(rms_norm(q.reshape(b, s, ATT_HEADS, ATT_HEAD_DIM), q_g), cos, sin)
    k = partial_rope(rms_norm(k.reshape(b, s, ATT_HEADS, ATT_HEAD_DIM), k_g), cos, sin)
    v = v.reshape(b, s, ATT_HEADS, ATT_HEAD_DIM)
    q_idx = partial_rope(q_idx.reshape(b, s, IDX_HEADS, IDX_DIM), cos, sin).astype(jnp.float32)
    k_idx = partial_rope(k_idx[:, :, None, :], cos, sin)[:, :, 0].astype(jnp.float32)
    w = w_idx.astype(jnp.float32) * (IDX_HEADS ** -0.5 * IDX_DIM ** -0.5)
    kv = jnp.concatenate([k, v], axis=-1)
    k_sel = min(TOPK_MAX, s // 4)
    nb = s // Q_BLOCK
    key_pos = jnp.arange(s)

    def to_blocks(t):
        return jnp.moveaxis(t.reshape((b, nb, Q_BLOCK) + t.shape[2:]), 1, 0)

    def block(args):
        qb, qib, wb, start = args
        qpos = start + jnp.arange(Q_BLOCK)
        logits = jnp.einsum('bthd,bsd->bths', qib, k_idx)
        score = jnp.einsum('bth,bths->bts', wb, jax.nn.relu(logits))
        score = jnp.where((key_pos[None, :] <= qpos[:, None])[None], score, -jnp.inf)
        _, idx = lax.top_k(score, k_sel)
        valid = idx <= qpos[None, :, None]
        kv_sel = jax.vmap(lambda kvb, ib: kvb[ib])(kv, idx)
        k_s = kv_sel[..., :ATT_HEAD_DIM]
        v_s = kv_sel[..., ATT_HEAD_DIM:]
        att = jnp.einsum('bthd,btkhd->bhtk', qb.astype(jnp.float32), k_s.astype(jnp.float32)) * (ATT_HEAD_DIM ** -0.5)
        att = jnp.where(valid[:, None], att, -jnp.inf)
        p = jax.nn.softmax(att, axis=-1)
        return jnp.einsum('bhtk,btkhd->bthd', p.astype(v_s.dtype), v_s)

    starts = jnp.arange(nb, dtype=jnp.int32) * Q_BLOCK
    out = lax.map(block, (to_blocks(q), to_blocks(q_idx), to_blocks(w), starts))
    return jnp.moveaxis(out, 0, 1).reshape(b, s, D_ATT)

def memory_cross_attention(h, m, w_q, w_kv, q_g, k_g, w_o):
    b, s, _ = h.shape
    nm = m.shape[1]
    q = rms_norm((h @ w_q).reshape(b, s, MEM_HEADS, MEM_HEAD_DIM), q_g)
    kv = (m @ w_kv).reshape(b, nm, 2, MEM_HEADS, MEM_HEAD_DIM)
    k = rms_norm(kv[:, :, 0], k_g)
    v = kv[:, :, 1]
    att = jnp.einsum('bshd,bmhd->bhsm', q.astype(jnp.float32), k.astype(jnp.float32)) * (MEM_HEAD_DIM ** -0.5)
    p = jax.nn.softmax(att, axis=-1)
    o = jnp.einsum('bhsm,bmhd->bshd', p.astype(v.dtype), v).reshape(b, s, D_MEMATT)
    return o @ w_o

def swiglu(h, wg, wu, wd):
    return (jax.nn.silu(h @ wg) * (h @ wu)) @ wd

def moe_swiglu(h, w_router, w_gate, w_up, w_down):
    b, s, d = h.shape
    hf = h.reshape(b * s, d)
    logits = (hf @ w_router).astype(jnp.float32)
    top_v, top_i = lax.top_k(logits, TOP_K)
    gates = jax.nn.softmax(top_v, axis=-1)
    n_assign = hf.shape[0] * TOP_K
    expert_flat = top_i.reshape(-1)
    token_flat = jnp.arange(n_assign, dtype=jnp.int32) // TOP_K
    gate_flat = gates.reshape(-1)
    order = jnp.argsort(expert_flat)
    sorted_exp = expert_flat[order]
    counts = jnp.bincount(expert_flat, length=N_EXPERTS)
    starts = jnp.cumsum(counts) - counts
    padded = (counts + MOE_BLOCK - 1) // MOE_BLOCK * MOE_BLOCK
    padded_ends = jnp.cumsum(padded)
    padded_starts = padded_ends - padded
    dest = padded_starts[sorted_exp] + jnp.arange(n_assign, dtype=jnp.int32) - starts[sorted_exp]
    n_blocks = -(-n_assign // MOE_BLOCK) + N_EXPERTS
    n_slots = n_blocks * MOE_BLOCK
    slot_tok = jnp.zeros((n_slots,), jnp.int32).at[dest].set(token_flat[order])
    slot_gate = jnp.zeros((n_slots,), jnp.float32).at[dest].set(gate_flat[order])
    block_exp = jnp.minimum(
        jnp.searchsorted(padded_ends, jnp.arange(n_blocks, dtype=jnp.int32) * MOE_BLOCK, side='right'),
        N_EXPERTS - 1)

    def block(args):
        tok, g, e = args
        y = swiglu(hf[tok], w_gate[e], w_up[e], w_down[e])
        return y * g[:, None].astype(y.dtype)

    ys = lax.map(block, (slot_tok.reshape(n_blocks, MOE_BLOCK), slot_gate.reshape(n_blocks, MOE_BLOCK), block_exp))
    out = jnp.zeros_like(hf).at[slot_tok].add(ys.reshape(n_slots, d))
    return out.reshape(b, s, d)

def setup_inputs(seed: int = 0) -> dict:
    key = jax.random.key(seed)
    ks = iter(jax.random.split(key, 40))
    f32 = jnp.float32

    def nrm(shape, scale):
        return jax.random.normal(next(ks), shape, f32) * scale

    def gain(shape):
        return 1.0 + 0.02 * jax.random.normal(next(ks), shape, f32)

    x = nrm((BATCH, SEQ, D_MODEL), 1.0)
    mem = nrm((BATCH, N_MEM, D_MODEL), 1.0)
    positions = (jax.random.randint(next(ks), (BATCH, 1), 0, 4096, dtype=jnp.int32)
                 + jnp.arange(SEQ, dtype=jnp.int32)[None, :])
    mix_norm_g = gain((DEPTH, D_MODEL))
    w_in = nrm((DEPTH, D_MODEL, D_IN), D_MODEL ** -0.5)
    conv_dw_w = nrm((DEPTH, CONV_WIDTH, D_CONV), CONV_WIDTH ** -0.5)
    conv_ln_g = gain((DEPTH, D_CONV))
    conv_ln_b = nrm((DEPTH, D_CONV), 0.02)
    conv_pw_w = nrm((DEPTH, D_CONV, D_CONV), D_CONV ** -0.5)
    ssd_conv_w = nrm((DEPTH, SSD_CONV, D_XBC), SSD_CONV ** -0.5)
    ssd_conv_b = nrm((DEPTH, D_XBC), 0.02)
    u = jax.random.uniform(next(ks), (DEPTH, SSD_HEADS), f32)
    dt0 = jnp.exp(u * (math.log(0.1) - math.log(0.001)) + math.log(0.001))
    ssd_dt_bias = dt0 + jnp.log(-jnp.expm1(-dt0))
    ssd_a_log = jnp.log(jax.random.uniform(next(ks), (DEPTH, SSD_HEADS), f32, 1.0, 16.0))
    ssd_d = gain((DEPTH, SSD_HEADS))
    ssd_norm_g = gain((DEPTH, D_SSD))
    att_q_norm_g = gain((DEPTH, ATT_HEAD_DIM))
    att_k_norm_g = gain((DEPTH, ATT_HEAD_DIM))
    w_out = nrm((DEPTH, D_MIX, D_MODEL), D_MIX ** -0.5)
    memx_norm_g = gain((DEPTH, D_MODEL))
    mem_norm_g = gain((DEPTH, D_MODEL))
    memx_w_q = nrm((DEPTH, D_MODEL, D_MEMATT), D_MODEL ** -0.5)
    memx_w_kv = nrm((DEPTH, D_MODEL, 2 * D_MEMATT), D_MODEL ** -0.5)
    memx_q_norm_g = gain((DEPTH, MEM_HEAD_DIM))
    memx_k_norm_g = gain((DEPTH, MEM_HEAD_DIM))
    memx_w_o = nrm((DEPTH, D_MEMATT, D_MODEL), D_MEMATT ** -0.5)
    ffn_norm_g = gain((DEPTH, D_MODEL))
    ffn_w_gate = nrm((N_DENSE, D_MODEL, D_FF), D_MODEL ** -0.5)
    ffn_w_up = nrm((N_DENSE, D_MODEL, D_FF), D_MODEL ** -0.5)
    ffn_w_down = nrm((N_DENSE, D_FF, D_MODEL), D_FF ** -0.5)
    moe_w_router = nrm((N_MOE, D_MODEL, N_EXPERTS), D_MODEL ** -0.5)
    moe_w_gate = nrm((N_MOE, N_EXPERTS, D_MODEL, D_FF), D_MODEL ** -0.5)
    moe_w_up = nrm((N_MOE, N_EXPERTS, D_MODEL, D_FF), D_MODEL ** -0.5)
    moe_w_down = nrm((N_MOE, N_EXPERTS, D_FF, D_MODEL), D_FF ** -0.5)
    return {'x': x, 'mem': mem, 'positions': positions, 'mix_norm_g': mix_norm_g, 'w_in': w_in,
            'conv_dw_w': conv_dw_w, 'conv_ln_g': conv_ln_g, 'conv_ln_b': conv_ln_b, 'conv_pw_w': conv_pw_w,
            'ssd_conv_w': ssd_conv_w, 'ssd_conv_b': ssd_conv_b, 'ssd_dt_bias': ssd_dt_bias,
            'ssd_a_log': ssd_a_log, 'ssd_d': ssd_d, 'ssd_norm_g': ssd_norm_g,
            'att_q_norm_g': att_q_norm_g, 'att_k_norm_g': att_k_norm_g, 'w_out': w_out,
            'memx_norm_g': memx_norm_g, 'mem_norm_g': mem_norm_g, 'memx_w_q': memx_w_q,
            'memx_w_kv': memx_w_kv, 'memx_q_norm_g': memx_q_norm_g, 'memx_k_norm_g': memx_k_norm_g,
            'memx_w_o': memx_w_o, 'ffn_norm_g': ffn_norm_g, 'ffn_w_gate': ffn_w_gate,
            'ffn_w_up': ffn_w_up, 'ffn_w_down': ffn_w_down, 'moe_w_router': moe_w_router,
            'moe_w_gate': moe_w_gate, 'moe_w_up': moe_w_up, 'moe_w_down': moe_w_down}

def reference(x, mem, positions, mix_norm_g, w_in, conv_dw_w, conv_ln_g, conv_ln_b, conv_pw_w,
              ssd_conv_w, ssd_conv_b, ssd_dt_bias, ssd_a_log, ssd_d, ssd_norm_g,
              att_q_norm_g, att_k_norm_g, w_out, memx_norm_g, mem_norm_g, memx_w_q, memx_w_kv,
              memx_q_norm_g, memx_k_norm_g, memx_w_o, ffn_norm_g, ffn_w_gate, ffn_w_up, ffn_w_down,
              moe_w_router, moe_w_gate, moe_w_up, moe_w_down):
    cos, sin = rope_tables(positions)
    sizes = [2 * D_CONV, D_SSD, D_XBC, SSD_HEADS, D_ATT, D_ATT, D_ATT, IDX_HEADS * IDX_DIM, IDX_DIM, IDX_HEADS]
    for i in range(DEPTH):
        h = rms_norm(x, mix_norm_g[i])
        u = h @ w_in[i].astype(h.dtype)
        parts = []
        off = 0
        for sz in sizes:
            parts.append(u[..., off:off + sz])
            off += sz
        u_conv, z, xbc, dt_raw, q, k, v, q_idx, k_idx, w_idx = parts
        y_conv = conformer_conv(u_conv, conv_dw_w[i], conv_ln_g[i], conv_ln_b[i], conv_pw_w[i])
        y_ssd = ssd_mixer(z, xbc, dt_raw, ssd_conv_w[i], ssd_conv_b[i], ssd_dt_bias[i],
                          ssd_a_log[i], ssd_d[i], ssd_norm_g[i])
        y_att = dsa_attention(q, k, v, q_idx, k_idx, w_idx, cos, sin, att_q_norm_g[i], att_k_norm_g[i])
        y_mix = jnp.concatenate([y_conv.astype(x.dtype), y_ssd.astype(x.dtype), y_att.astype(x.dtype)], axis=-1)
        x = x + (y_mix @ w_out[i].astype(x.dtype)).astype(x.dtype)
        h = rms_norm(x, memx_norm_g[i])
        m = rms_norm(mem, mem_norm_g[i])
        x = x + memory_cross_attention(h, m, memx_w_q[i], memx_w_kv[i], memx_q_norm_g[i],
                                       memx_k_norm_g[i], memx_w_o[i]).astype(x.dtype)
        h = rms_norm(x, ffn_norm_g[i])
        j = i // 2
        if i % 2 == 0:
            y = swiglu(h, ffn_w_gate[j], ffn_w_up[j], ffn_w_down[j])
        else:
            y = moe_swiglu(h, moe_w_router[j], moe_w_gate[j], moe_w_up[j], moe_w_down[j])
        x = x + y.astype(x.dtype)
    return x


_drawn_inputs = setup_inputs


def setup_inputs(seed=0):
    import zlib

    import numpy as np

    out = dict(_drawn_inputs(seed))
    spreads = {}
    factors = {'conv_ln_g': 3.707,
     'conv_ln_b': 2.709,
     'att_q_norm_g': 8.0,
     'att_k_norm_g': 6.148,
     'memx_norm_g': 6.428,
     'mem_norm_g': 8.0,
     'memx_q_norm_g': 8.0,
     'memx_k_norm_g': 8.0,
     'ffn_norm_g': 3.41}
    for name, (base, spread) in spreads.items():
        noise = np.random.default_rng([zlib.crc32(name.encode()), seed]).standard_normal(out[name].shape)
        drawn = base * np.exp(spread * noise) if base else spread * noise
        out[name] = __import__('jax').numpy.asarray(drawn.astype(out[name].dtype))
    for name, factor in factors.items():
        out[name] = (out[name] * factor).astype(out[name].dtype)
    return out
```

```python
from contextlib import ExitStack

import concourse.bass as bass
from concourse import mybir

F32 = mybir.dt.float32
I32 = mybir.dt.int32
ALU = mybir.AluOpType
ACT = mybir.ActivationFunctionType
AX_X = mybir.AxisListType.X

P = 128
SEQ, D_MODEL, DEPTH = 256, 1024, 2
NT = SEQ // P
KT = D_MODEL // P
D_CONV, CONV_W = 256, 31
D_SSD, SSD_H, SSD_P, SSD_CONV = 512, 8, 64, 4
D_ATT, ATT_H, HD = 256, 4, 64
IDX_H = 8
TOPK = 64
ROPE_THETA, ROT = 500000.0, 16
MEM_H = 4
D_FF, N_EXP = 2816, 8
FT = D_FF // P
EPS = 1e-6

WSLOTS = 8
SLOT = 3 * KT * P
MIX_ITEMS = 16
WIDE = SLOT // KT
LOOP_SLOTS = 7
ROUNDS = FT // LOOP_SLOTS
BLOCK = 128
MAX_OVER = (2 * SEQ - 1) // (BLOCK + 1)

U_V, U_QI, U_KI, U_W, U_DT, U_N = 512, 768, 1280, 1344, 1352, 1360
U_HEADS = 21

COLS = {}
_n = 0
for _name, _w in (("mix_g", KT), ("memx_g", KT), ("mem_g", KT), ("conv_w", 2 * CONV_W), ("ln_g", 2),
                  ("ln_b", 2), ("ssd_w", KT * SSD_CONV), ("ssd_b", KT), ("ssd_g", 4),
                  ("mq_g", 1), ("mk_g", 1)):
    COLS[_name] = _n
    _n += _w
N_COLS = _n
R_QK, R_DTB, R_ALOG, R_D, N_ROWS = 0, 128, 136, 144, 152

MASKED = -1e30
TAKEN = -3e38
PAD = -3e38
PICKED = -2e38


TWO_PI = 6.283185307179586
TURN_PARTS = (6.28125, 0.0019350051879882812, 3.0199159819567e-07)
ROUND_BIG = 12582912.0
DEBUG = False

RAISES = {
    "a_full": 71, "a_free": 71, "v_full": 28, "v_free": 28, "dve_step": 213, "act_step": 17,
    "x_ready": 2, "rstd_ready": 3, "h_ready": 6, "xbc_conv": 4, "xc_ready": 4, "a_ready": 2,
    "m_ready": 2, "score_used": 8, "att_ready": 4, "exp_ready": 4, "p_ready": 4, "mem_ready": 2,
    "hn_ss": 2, "hn_rstd": 2, "hn_ready": 2,
    "place_ready": 2, "hc_full": 2, "hc_ready": 2, "gu_full": FT, "silu_ready": FT, "act_ready": FT,
    "yc_ready": 2, "sc_full": 4, "x_added": 4,
}
A_SEG, A_INDEX, A_KV, A_MQ = 26, 31, 47, 60


class Signal:

    def __init__(self, sem, name, per, start=0):
        self.sem, self.name, self.per, self.start, self.n = sem, name, per, start, 0

    def count(self, lap):
        return self.n - lap * self.per

    def up(self):
        self.n += 1
        return self.sem, 1

    def __call__(self, lap, k):
        return self.sem, lap * self.per + (self.start + k)


def index_head(pair, j):
    return 4 * (pair // 2) + pair % 2 + 2 * j


def trunk_kernel(nc, x_in, mem_in, pos_in, cols_in, rows_in, ffn_g_in, router_in, wmix, wffn, out):
    with ExitStack() as ctx:
        def sb(name, shape, dt=F32):
            return ctx.enter_context(nc.sbuf_tensor(name, shape, dt))

        signals = []

        def signal(name, start=0):
            s = Signal(ctx.enter_context(nc.semaphore(name)), name, RAISES.get(name, 1), start)
            signals.append(s)
            return s

        W = sb("W", [P, WSLOTS, SLOT])
        X = sb("X", [P, NT, D_MODEL])
        HT = sb("HT", [P, KT, SEQ])
        H = sb("H", [P, NT, D_MODEL])
        U = sb("U", [P, NT, U_N])
        XR_LM = sb("XR_LM", [P, KT * (SEQ + 3)])
        XR = XR_LM[:, :].rearrange("p (k s) -> p k s", k=KT)
        XC = sb("XC", [P, KT, SEQ])
        LM = XR_LM[:, 0:NT * SSD_H * P].rearrange("p (t h l) -> p t h l", t=NT, h=SSD_H)
        Z = sb("Z", [P, NT, D_SSD])
        hpad = sb("hpad", [P, 2, SEQ + CONV_W - 1])
        cacc = sb("cacc", [P, 2, SEQ])
        ctmp = sb("ctmp", [P, 2, SEQ])
        xd = sb("xd", [P, NT, D_SSD])
        ysk = sb("ysk", [P, NT, D_SSD])
        xdd = sb("xdd", [P, D_SSD])
        btok = sb("btok", [P, 2, P])
        st = sb("st", [P, 2, 256])
        qkT = sb("qkT", [P, 4, SEQ])
        qiT = sb("qiT", [P, 4, SEQ])
        kiT = sb("kiT", [P, SEQ])
        kk = sb("kk", [P, NT, P])
        score = sb("score", [P, NT, SEQ])
        rl = sb("rl", [P, 2, 2, SEQ])
        abias = sb("abias", [P, NT, SEQ])
        prob = sb("prob", [P, 4, SEQ])
        pT = sb("pT", [P, 2, 4, P])
        RN = NT * U_HEADS * 8
        TA = H[:, :, :].rearrange("p t (h l) -> p t h l", h=SSD_H)
        YT = HT
        MT = XC
        kvt = LM[:, 0, :, :].rearrange("p h l -> p (h l)").rearrange("p (t n) -> p t n", t=NT)
        KTm = LM[:, 1, 0:4, :].rearrange("p h l -> p (h l)").rearrange("p (t n) -> p t n", t=2)
        mq = LM[:, 1, 4:8, :].rearrange("p h l -> p (h l)").rearrange("p (t n) -> p t n", t=NT)
        mqT = st
        rt = [t[:, :, :].rearrange("p c s -> p (c s)")[:, i * RN:(i + 1) * RN]
              .rearrange("p (t h d) -> p t h d", t=NT, h=U_HEADS) for t in (qkT, qiT) for i in range(2)]
        oT = xdd[:, :].rearrange("p (t n) -> p t n", t=2)
        junk = rl[:, :, :, :].rearrange("p a b s -> p (a b s)")
        hcT = U[:, 0, 0:1024].rearrange("p (c j) -> p c j", c=KT)
        yc = U[:, 1, 0:1024]
        sg = U[:, 0, 1024:1280].rearrange("p (b j) -> p b j", b=2)
        aT = U[:, 1, 1024:1280].rearrange("p (b j) -> p b j", b=2)
        PM = qiT[:, 0, :].rearrange("p (t j) -> p t j", t=NT)
        PG = qiT[:, 1, :].rearrange("p (t j) -> p t j", t=NT)
        PGT = qiT[:, 2, :].rearrange("p (t j) -> p t j", t=NT)

        ident = sb("ident", [P, P])
        tri = sb("tri", [P, P])
        tri_s = sb("tri_s", [P, P])
        ones = sb("ones", [P, P])
        neg_ssd = sb("neg_ssd", [P, P])
        neg_att = sb("neg_att", [P, P])
        iota_j = sb("iota_j", [P, P])
        cols = sb("cols", [P, N_COLS])
        rows = sb("rows", [P, N_ROWS])
        ffn_g2 = sb("ffn_g2", [P, DEPTH, KT])
        ffn_g = sb("ffn_g", [P, KT])
        wr = sb("wr", [P, KT, N_EXP])
        pos_i = sb("pos_i", [P, NT], I32)
        pos_f = sb("pos_f", [P, NT])
        ang = sb("ang", [P, NT, 8])
        kay = sb("kay", [P, NT, 8])
        cs_ = sb("cs_", [P, NT, 8])
        sn_ = sb("sn_", [P, NT, 8])
        inv = sb("inv", [P, 8])
        eps = sb("eps", [P, 1])
        one = sb("one", [P, 1])
        ss = sb("ss", [P, 32])
        rs = sb("rs", [P, 32])
        dts = sb("dts", [P, 6, NT, SSD_H])
        anum = sb("anum", [P, SSD_H])
        zeros = sb("zeros", [P, 512], mybir.dt.bfloat16)
        cum = sb("cum", [P, NT, 2, SSD_H])
        ecum = sb("ecum", [P, 2, SSD_H])
        m8 = sb("m8", [P, NT, 8])
        nmx = sb("nmx", [P, 4])
        psm = sb("psm", [P, 4])
        prs = sb("prs", [P, 4])
        rin = sb("rin", [P, NT, 16])
        tr = sb("tr", [P, NT, 8])
        mr = sb("mr", [P, NT, 16])
        rmask = sb("rmask", [P, NT, N_EXP])
        rel = sb("rel", [P, NT, N_EXP])
        rsc = sb("rsc", [P, 4, NT])
        gate = sb("gate", [P, NT, N_EXP])
        posm = sb("posm", [P, NT, N_EXP])
        cnt = sb("cnt", [P, 4, N_EXP])
        oh = sb("oh", [P, MAX_OVER, N_EXP])
        rtmp = sb("rtmp", [P, 5 * MAX_OVER, N_EXP])
        NB = N_EXP + MAX_OVER
        BT = sb("BT", [P, NT, NB])
        GT = sb("GT", [P, NT, NB])
        BT0 = sb("BT0", [P, NT, NB])
        flags = sb("flags", [P, DEPTH])
        flag = sb("flag", [P, 1])
        tabf = sb("tabf", [P, 8])
        erow = sb("erow", [P, N_EXP])
        tabi = sb("tabi", [P, 8], I32)

        PA = [ctx.enter_context(nc.psum_tensor(f"PA{i}", [P, 512], F32)) for i in range(4)]
        PV = [ctx.enter_context(nc.psum_tensor(f"PV{i}", [P, 512], F32)) for i in range(4)]

        slot_full = [ctx.enter_context(nc.semaphore(f"slot_full{s}")) for s in range(WSLOTS)]
        slot_free = [ctx.enter_context(nc.semaphore(f"slot_free{s}")) for s in range(WSLOTS)]
        in_x = ctx.enter_context(nc.semaphore("in_x"))
        in_small = ctx.enter_context(nc.semaphore("in_small"))
        in_params = ctx.enter_context(nc.semaphore("in_params"))
        in_mem = ctx.enter_context(nc.semaphore("in_mem"))
        out_done = ctx.enter_context(nc.semaphore("out_done"))
        const_ready = ctx.enter_context(nc.semaphore("const_ready"))
        trig_step = ctx.enter_context(nc.semaphore("trig_step"))
        trig_act = ctx.enter_context(nc.semaphore("trig_act"))
        a_full, a_free = signal("a_full"), signal("a_free")
        v_full, v_free = signal("v_full"), signal("v_free")
        dve_step = signal("dve_step")
        act_step = signal("act_step")
        x_ready = signal("x_ready")
        rstd_ready = signal("rstd_ready")
        h_ready = signal("h_ready")
        xr_ready = signal("xr_ready")
        xbc_conv = signal("xbc_conv")
        xc_ready = signal("xc_ready")
        conv_acc = signal("conv_acc")
        conv_centred = signal("conv_centred")
        conv_rstd = signal("conv_rstd")
        conv_norm = signal("conv_norm")
        conv_aff = signal("conv_aff")
        conv_exp = signal("conv_exp")
        conv_out = signal("conv_out")
        qk_ss, qk_rstd = signal("qk_ss"), signal("qk_rstd")
        dt_in = signal("dt_in")
        dt_log = signal("dt_log")
        rope_ready = signal("rope_ready")
        a_ready = signal("a_ready")
        xdd_ready = signal("xdd_ready")
        cum_ready = signal("cum_ready")
        ecum_ready = signal("ecum_ready")
        m_ready = signal("m_ready")
        score_used = signal("score_used")
        att_ready = signal("att_ready")
        exp_ready = signal("exp_ready")
        p_ready = signal("p_ready")
        y_ss, y_rstd = signal("y_ss"), signal("y_rstd")
        y_ready = signal("y_ready")
        mem_rstd = signal("mem_rstd")
        mem_ready = signal("mem_ready")
        hn_ss, hn_rstd = signal("hn_ss"), signal("hn_rstd")
        hn_ready = signal("hn_ready")
        ffn_g_ready = signal("ffn_g_ready")
        top2_ready = signal("top2_ready")
        top2_exp = signal("top2_exp")
        mask_ready = signal("mask_ready")
        table_ready = signal("table_ready")
        place_ready = signal("place_ready")
        hc_full, hc_ready = signal("hc_full"), signal("hc_ready")
        pgt_full, pgt_ready = signal("pgt_full"), signal("pgt_ready")
        gu_full = signal("gu_full")
        silu_ready = signal("silu_ready")
        act_ready = signal("act_ready", start=1)
        yc_ready = signal("yc_ready")
        sc_full, x_added = signal("sc_full"), signal("x_added", start=1)

        block = ctx.enter_context(nc.Block())

        released = {}

        def first_block(L):
            return L * NT

        def blocks_fixed(L):
            return N_EXP if L % 2 else NT

        def slot_loads(L, s, item=None, g=None, r=0):
            a_block = ROUNDS if s < LOOP_SLOTS else 1
            if g is None:
                return L * (MIX_ITEMS // WSLOTS) + first_block(L) * a_block + item // WSLOTS
            return (L + 1) * (MIX_ITEMS // WSLOTS) + g * a_block + r

        def chunk_reads(s, g, r=0):
            return 1 + g * (ROUNDS if s < LOOP_SLOTS else 1) + r

        def pe_layer(pe, L):
            na, nv = [0], [0]

            def a_bank():
                na[0] += 1
                if na[0] > 4:
                    pe.wait_ge(*a_free(L, na[0] - 4))
                return PA[(na[0] - 1) % 4]

            def v_bank():
                nv[0] += 1
                if nv[0] > 4:
                    pe.wait_ge(*v_free(L, nv[0] - 4))
                return PV[(nv[0] - 1) % 4]

            def a_taken():
                pe.wait_ge(*a_free(L, na[0]))

            def arrived(item):
                s = item % WSLOTS
                pe.wait_ge(slot_full[s], (slot_loads(L, s, item=item) + 1) * 16)
                return W[:, s, :]

            def k_tiles(view, width, at=0):
                return view[:, at:at + KT * width].rearrange("p (k n) -> p k n", k=KT)

            def transposes(tiles, src):
                for at in range(0, len(tiles), 2):
                    bank = a_bank()
                    for j, tile in enumerate(tiles[at:at + 2]):
                        for tt in range(NT):
                            last = pe.transpose(bank[:, j * SEQ + tt * P:j * SEQ + (tt + 1) * P],
                                                src(tile, tt), ident[:, :])
                    last.then_inc(*a_full.up())

            def accumulate(dst, pairs):
                for i, (lhsT, rhs) in enumerate(pairs):
                    last = pe.matmul(dst, lhsT, rhs, start=(i == 0), stop=(i == len(pairs) - 1))
                return last

            def tokens_by(dst, act, view, tt):
                return accumulate(dst, [(act[:, k, tt * P:(tt + 1) * P], view[:, k, :]) for k in range(KT)])

            pe.wait_ge(*h_ready(L, NT))
            transposes(list(range(KT)), lambda c, tt: H[:, tt, c * P:(c + 1) * P])
            a_taken()
            for tile in range(12):
                item = tile // 3
                view = k_tiles(arrived(item), WIDE)
                if tile % 2 == 0:
                    bank = a_bank()
                f = (tile % 3) * P
                last = accumulate(bank[:, (tile % 2) * SEQ:(tile % 2 + 1) * SEQ],
                                  [(view[:, k, f:f + P], HT[:, k, :]) for k in range(KT)])
                if tile % 2:
                    last.then_inc(*a_full.up())
                released[item] = a_full, na[0]
            for item in range(4, 8):
                width = WIDE if item < 7 else U_N - 3 * WIDE
                view = k_tiles(arrived(item), width)
                for tt in range(NT):
                    tokens_by(a_bank()[:, 0:width], HT, view, tt).then_inc(*a_full.up())
                released[item] = a_full, na[0]
            pe.wait_ge(*conv_acc(L, 1))
            accumulate(v_bank()[:, 0:SEQ], [(ones[:, :], cacc[:, j, :]) for j in range(2)]).then_inc(*v_full.up())
            z0, z1 = k_tiles(arrived(8), WIDE), k_tiles(arrived(9), P)
            for tt in range(NT):
                bank = a_bank()
                tokens_by(bank[:, 0:WIDE], HT, z0, tt)
                tokens_by(bank[:, WIDE:512], HT, z1, tt).then_inc(*a_full.up())
            released[8] = a_full, na[0]
            pe.wait_ge(*conv_centred(L, 1))
            accumulate(a_bank()[:, 0:SEQ], [(ones[:, :], ctmp[:, j, :]) for j in range(2)]).then_inc(*a_full.up())
            pe.wait_ge(*xc_ready(L, 4))
            for tt in range(NT):
                bank = v_bank()
                for j in range(4):
                    last = pe.transpose(bank[:, j * P:(j + 1) * P], XC[:, j, tt * P:(tt + 1) * P], ident[:, :])
                last.then_inc(*v_full.up())
            bank = a_bank()
            for j in range(2):
                last = pe.transpose(bank[:, j * P:(j + 1) * P], XC[:, 4 + j, 0:P], ident[:, :])
            last.then_inc(*a_full.up())
            b_group = na[0]
            pe.wait_ge(*a_ready(L, 1))
            bank = v_bank()
            for tt in range(NT):
                pe.matmul(bank[:, tt * 16:tt * 16 + 8], tri[:, :], dts[:, 4, tt, :], start=True, stop=True)
                last = pe.matmul(bank[:, tt * 16 + 8:tt * 16 + 16], ones[:, :], dts[:, 4, tt, :],
                                 start=True, stop=True)
            last.then_inc(*v_full.up())
            pe.wait_ge(*a_ready(L, 2))
            for tt in range(NT):
                for half in range(2):
                    bank = a_bank()
                    hs = slice(half * 4, half * 4 + 4)
                    pe.matmul(bank[:, :], ones[:, :], TA[:, tt, hs, :], start=True, stop=False)
                    pe.matmul(bank[:, :], tri[:, :], dts[:, 5, tt, hs].unsqueeze(2).to_broadcast([P, 4, P]),
                              start=False, stop=False)
                    pe.matmul(bank[:, :], ident[:, :], neg_ssd[:, :].unsqueeze(1).to_broadcast([P, 4, P]),
                              start=False, stop=True).then_inc(*a_full.up())
            released["TA"] = a_full, na[0]
            bank = v_bank()
            for tt in range(NT):
                for g in range(2):
                    o = (tt * 2 + g) * P
                    last = pe.matmul(bank[:, o:o + P], XC[:, 4 + g, tt * P:(tt + 1) * P],
                                     XC[:, 6 + g, tt * P:(tt + 1) * P], start=True, stop=True)
            last.then_inc(*v_full.up())
            pe.wait_ge(*rope_ready(L, 1))
            transposes([0, 1, 2, 3], lambda c, tt: U[:, tt, U_QI + c * P:U_QI + (c + 1) * P])
            transposes([0], lambda c, tt: kk[:, tt, :])
            index_group = na[0]
            transposes([0, 1, 2, 3], lambda c, tt: U[:, tt, c * P:(c + 1) * P])
            pe.wait_ge(*a_free(L, index_group))
            for tt in range(NT):
                keys = P * (tt + 1)
                for pair in range(IDX_H // 2):
                    bank = a_bank()
                    r = slice(HD * (pair % 2), HD * (pair % 2) + HD)
                    for j in range(2):
                        last = pe.matmul(bank[:, j * SEQ:j * SEQ + keys],
                                         qiT[r, index_head(pair, j) // 2, tt * P:(tt + 1) * P],
                                         kiT[r, 0:keys], start=True, stop=True)
                    last.then_inc(*a_full.up())
            pe.wait_ge(*conv_out(L, 1))
            pw = W[:, 9 % WSLOTS, KT * P:KT * P + 2 * D_CONV].rearrange("p (k n) -> p k n", k=2)
            bank = a_bank()
            for j in range(2):
                last = accumulate(bank[:, j * SEQ:(j + 1) * SEQ],
                                  [(pw[:, k, j * P:(j + 1) * P], ctmp[:, k, :]) for k in range(2)])
            last.then_inc(*a_full.up())
            released[9] = a_full, na[0]
            pe.wait_ge(*xdd_ready(L, 1))
            pe.wait_ge(*a_free(L, b_group))
            bank = a_bank()
            for g in range(2):
                last = pe.matmul(bank[:, g * SEQ:(g + 1) * SEQ], btok[:, g, :], xdd[:, g * SEQ:(g + 1) * SEQ],
                                 start=True, stop=True)
            last.then_inc(*a_full.up())
            for tt in range(NT):
                pe.wait_ge(*m_ready(L, tt + 1))
                bank = v_bank()
                for h in range(SSD_H):
                    last = pe.matmul(bank[:, h * SSD_P:(h + 1) * SSD_P], LM[:, tt, h, :],
                                     xd[:, tt, h * SSD_P:(h + 1) * SSD_P], start=True, stop=True)
                last.then_inc(*v_full.up())
            a_taken()
            bank = v_bank()
            for g in range(2):
                last = pe.matmul(bank[:, g * SEQ:(g + 1) * SEQ], XC[:, 6 + g, P:2 * P], st[:, g, :],
                                 start=True, stop=True)
            last.then_inc(*v_full.up())
            pe.wait_ge(*mem_ready(L, NT))
            transposes(list(range(KT)), lambda c, tt: H[:, tt, c * P:(c + 1) * P])
            a_taken()
            kv0, kv1 = k_tiles(arrived(10), WIDE), k_tiles(arrived(11), P)
            for tt in range(NT):
                bank = a_bank()
                tokens_by(bank[:, 0:WIDE], MT, kv0, tt)
                tokens_by(bank[:, WIDE:512], MT, kv1, tt).then_inc(*a_full.up())
            released[10] = released[11] = a_full, na[0]

            def att_logits(tt, qT, kT, keys):
                for odd in range(2):
                    bank = v_bank()
                    r = slice(HD * odd, HD * odd + HD)
                    for j in range(2):
                        last = pe.matmul(bank[:, j * keys:(j + 1) * keys], qT[r, j, tt * P:(tt + 1) * P],
                                         kT[r, j, 0:keys], start=True, stop=True)
                    last.then_inc(*v_full.up())

            def p_transposes(tiles):
                for s in range(tiles):
                    bank = a_bank()
                    for h in range(4):
                        last = pe.transpose(bank[:, h * P:(h + 1) * P], prob[:, h, s * P:(s + 1) * P], ident[:, :])
                    last.then_inc(*a_full.up())

            def weighted_values(tiles, v):
                bank = a_bank()
                for h in range(4):
                    r = HD * (h % 2)
                    last = accumulate(bank[r:r + HD, (h // 2) * P:(h // 2 + 1) * P],
                                      [(v(s, h), pT[:, s, h, :]) for s in range(tiles)])
                last.then_inc(*a_full.up())

            for tt in range(NT):
                att_logits(tt, qkT[:, 0:2, :], qkT[:, 2:4, :], P * (tt + 1))
                pe.wait_ge(*p_ready(L, tt + 1))
                p_transposes(tt + 1)
                a_taken()
                weighted_values(tt + 1, lambda s, h: U[:, s, U_V + h * HD:U_V + (h + 1) * HD])
            pe.wait_ge(*hn_ready(L, 1))
            transposes([0, 1], lambda c, tt: kvt[:, tt, c * P:(c + 1) * P])
            pe.wait_ge(*y_ready(L, 1))
            transposes([0, 1, 2, 3], lambda c, tt: ysk[:, tt, c * P:(c + 1) * P])
            a_taken()
            for item in range(12, 15):
                width = WIDE if item < 14 else D_MODEL - 2 * WIDE
                view = k_tiles(arrived(item), width)
                for tt in range(NT):
                    tokens_by(v_bank()[:, 0:width], YT, view, tt).then_inc(*v_full.up())
                released[item] = v_full, nv[0]
            pe.wait_ge(*h_ready(L, 2 * NT))
            transposes(list(range(KT)), lambda c, tt: H[:, tt, c * P:(c + 1) * P])
            a_taken()
            wq = k_tiles(arrived(15), D_ATT)
            bank = a_bank()
            for tt in range(NT):
                last = tokens_by(bank[:, tt * D_ATT:(tt + 1) * D_ATT], HT, wq, tt)
            last.then_inc(*a_full.up())
            pe.wait_ge(*hn_ready(L, 2))
            transposes([0, 1], lambda c, tt: mq[:, tt, c * P:(c + 1) * P])
            a_taken()
            for tt in range(NT):
                att_logits(tt, mqT, KTm, SEQ)
                pe.wait_ge(*p_ready(L, NT + tt + 1))
                p_transposes(2)
                a_taken()
                weighted_values(2, lambda s, h: kvt[:, s, D_ATT + h * HD:D_ATT + (h + 1) * HD])
            a_taken()
            wo = [W[:, 14 % WSLOTS, KT * 256:KT * 256 + D_MODEL], W[:, 15 % WSLOTS, KT * 256:KT * 256 + D_MODEL]]
            for half in range(2):
                for tt in range(NT):
                    accumulate(v_bank()[:, :], [(oT[:, k, tt * P:(tt + 1) * P],
                                                 wo[k][:, half * 512:(half + 1) * 512])
                                                for k in range(2)]).then_inc(*v_full.up())
            released[14] = released[15] = v_full, nv[0]
            pe.wait_ge(*h_ready(L, 3 * NT))
            transposes(list(range(KT)), lambda c, tt: H[:, tt, c * P:(c + 1) * P])
            a_taken()
            bank = v_bank()
            for tt in range(NT):
                last = tokens_by(bank[:, tt * N_EXP:(tt + 1) * N_EXP], HT, wr, tt)
            last.then_inc(*v_full.up())
            pe.wait_ge(*mask_ready(L, 1))
            bank = v_bank()
            accumulate(bank[:, 0:8], [(tri_s[:, :], rmask[:, 0, :])])
            accumulate(bank[:, 8:16], [(tri_s[:, :], rmask[:, 1, :]), (ones[:, :], rmask[:, 0, :])])
            accumulate(bank[:, 16:24], [(ones[:, :], rmask[:, tt, :]) for tt in range(NT)]).then_inc(*v_full.up())
            a_taken()
            pe.wait_ge(*v_free(L, nv[0]))
            pe.wait_ge(*table_ready(L, 1))
            more = pe.value_load(tabi[0:1, 0:1], min_val=1, max_val=MAX_OVER + 1)

            def gate_up(g, r, s, i):
                pe.wait_ge(slot_full[s], (slot_loads(L, s, g=g, r=r) + 1) * 16)
                wv = W[:, s, 0:2 * KT * P].rearrange("p (m k n) -> p m k n", m=2, k=KT)
                for m in range(2):
                    last = accumulate(PA[i % 2][:, m * P:(m + 1) * P],
                                      [(wv[:, m, k, :], hcT[:, k, :]) for k in range(KT)])
                last.then_inc(gu_full.sem, 1)

            def down(g, done, s, i, stop):
                pe.wait_ge(*act_ready(g, done))
                for half in range(2):
                    last = pe.matmul(PA[2 + half][:, :], aT[:, i % 2, :],
                                     W[:, s, (2 * KT + 4 * half) * P:(2 * KT + 4 * half + 4) * P],
                                     start=False, stop=stop, skip_group_check=True)
                return last

            with pe.Fori(0, blocks_fixed(L) - 1 + more) as b:
                g = first_block(L) + b
                pe.wait_ge(*place_ready(g, 2))
                for tt in range(NT):
                    last = pe.transpose(PA[0][:, 256 + tt * P:256 + (tt + 1) * P], PG[:, tt, :], ident[:, :])
                last.then_inc(pgt_full.sem, 1)
                for half in range(2):
                    for c in range(4):
                        k = half * 4 + c
                        last = accumulate(PV[half][:, c * P:(c + 1) * P],
                                          [(H[:, tt, k * P:(k + 1) * P], PM[:, tt, :]) for tt in range(NT)])
                    last.then_inc(hc_full.sem, 1)
                pe.wait_ge(*hc_ready(g, 2))
                pe.wait_ge(*pgt_ready(g, 1))
                for half in range(2):
                    pe.matmul(PA[2 + half][:, :], zeros[:, 0:P], zeros[:, :], start=True, stop=False,
                              skip_group_check=True)
                with pe.Fori(0, ROUNDS) as r:
                    for s in range(LOOP_SLOTS):
                        done = r * LOOP_SLOTS + s
                        if s == 0:
                            pe.wait_ge(*act_ready(g, done))
                        if s >= 2:
                            pe.wait_ge(*act_ready(g, done - 1))
                        gate_up(g, r, s, s)
                        if s:
                            down(g, done, s - 1, s - 1, False).then_inc(slot_free[s - 1], 1)
                    down(g, done + 1, s, s, False).then_inc(slot_free[s], 1)
                gate_up(g, 0, LOOP_SLOTS, 1)
                down(g, FT, LOOP_SLOTS, 1, True).then_inc(slot_free[LOOP_SLOTS], 1)
                pe.wait_ge(*yc_ready(g, 2))
                pe.wait_ge(*x_added(g, 0))
                for i in range(4):
                    tt, half = i % 2, i // 2
                    if i >= 2:
                        pe.wait_ge(*x_added(g, i - 1))
                    pe.matmul(PV[2 + i % 2][:, :], PGT[:, tt, :], yc[:, half * 512:(half + 1) * 512],
                              start=True, stop=True).then_inc(sc_full.sem, 1)

        @block.tensor
        def _(pe):
            pe.wait_ge(const_ready, 2)
            pe.wait_ge(in_small, 48)
            for L in range(DEPTH):
                pe_layer(pe, L)

        @block.sync
        def _(sp):
            sp.dma_start(X[:, :, :], x_in.rearrange("a (t p) d -> p (a t) d", p=P)).then_inc(in_x, 16)

            def chunk(g, r, s, expert, after=None):
                if after is not None:
                    sp.wait_ge(*after)
                sp.wait_ge(slot_free[s], chunk_reads(s, g, r))
                at = expert * FT + r * LOOP_SLOTS + s if s < LOOP_SLOTS else expert * FT + FT - 1
                sp.dma_start(W[:, s, :], wffn[bass.ds(at, 1), :, :].rearrange("a p n -> p (a n)")) \
                    .then_inc(slot_full[s], 16)

            def ffn_block(g, expert, rounds=(0, ROUNDS)):
                with sp.Fori(*rounds) as r:
                    for s in range(LOOP_SLOTS):
                        chunk(g, r, s, expert)

            for L in range(DEPTH):
                for item in range(MIX_ITEMS):
                    s = item % WSLOTS
                    if item >= WSLOTS:
                        done, k = released[item - WSLOTS]
                        sp.wait_ge(*done(L, k))
                    elif L:
                        sp.wait_ge(slot_free[s], chunk_reads(s, first_block(L)))
                    sp.dma_start(W[:, s, :], wmix[L * MIX_ITEMS + item]).then_inc(slot_full[s], 16)
                fixed = blocks_fixed(L)
                g0, moe = first_block(L), L % 2
                after = [done(L, k) for done, k in (released[WSLOTS + s] for s in range(WSLOTS))]
                for s in range(LOOP_SLOTS):
                    chunk(g0, 0, s, moe, after[s])
                ffn_block(g0, moe, (1, ROUNDS))
                chunk(g0, 0, LOOP_SLOTS, moe, after[LOOP_SLOTS])
                if fixed > 2:
                    with sp.Fori(1, fixed - 1) as b:
                        ffn_block(g0 + b, b + 1)
                        chunk(g0 + b, 0, LOOP_SLOTS, b + 1)
                sp.wait_ge(*table_ready(L, 1))
                more = sp.value_load(tabi[0:1, 0:1], min_val=1, max_val=MAX_OVER + 1)
                with sp.Fori(0, more) as j:
                    expert = sp.value_load(tabi[0:1, bass.ds(j + 1, 1)], min_val=0, max_val=N_EXP)
                    ffn_block(g0 + (fixed - 1) + j, expert)
                    chunk(g0 + (fixed - 1) + j, 0, LOOP_SLOTS, expert)
            sp.wait_ge(*x_added(first_block(DEPTH - 1) + (N_EXP - 1) + more, 0))
            sp.dma_start(out.rearrange("a (t p) d -> p (a t) d", p=P), X[:, :, :]).then_inc(out_done, 16)
            sp.wait_ge(out_done, 16)

        @block.gpsimd
        def _(pool):
            pool.dma_start(cols[:, :], cols_in[0]).then_inc(in_params, 16)
            pool.dma_start(rows[:, :], rows_in[0:1, :].to_broadcast([P, N_ROWS])).then_inc(in_params, 16)
            pool.dma_start(pos_i[:, :], pos_in).then_inc(in_small, 16)
            pool.dma_start(ffn_g2[:, :, :], ffn_g_in).then_inc(in_small, 16)
            pool.dma_start(wr[:, :, :], router_in).then_inc(in_small, 16)
            for s in range(WSLOTS):
                nc.gpsimd.memset(ss[:, s:s + 1], 0.0).then_inc(slot_free[s], 1)
            nc.gpsimd.memset(zeros[:, :], 0.0)
            nc.gpsimd.memset(ident[:, :], 0.0)
            nc.gpsimd.memset(tri[:, :], 1.0)
            nc.gpsimd.memset(tri_s[:, :], 1.0)
            nc.gpsimd.memset(ones[:, :], 1.0)
            nc.gpsimd.memset(neg_ssd[:, :], 0.0)
            nc.gpsimd.memset(neg_att[:, :], 0.0)
            nc.gpsimd.memset(hpad[:, :, :], 0.0)
            nc.gpsimd.memset(eps[:, :], EPS)
            nc.gpsimd.memset(one[:, :], 1.0)
            nc.gpsimd.memset(flags[:, 0:1], 0.0)
            nc.gpsimd.memset(flags[:, 1:2], 1.0).then_inc(const_ready, 1)
            pool.wait_ge(const_ready, 1)

            def cut(t, pattern, base, channel, op, fill):
                return nc.gpsimd.affine_select(out=t[:, :], in_=t[:, :], compare_op=op, fill=fill, base=base,
                                               pattern=pattern, channel_multiplier=channel)
            cut(ident, [[-1, P]], 0, 1, ALU.not_equal, 1.0)
            cut(tri, [[1, P]], 0, -1, ALU.is_ge, 0.0)
            cut(tri_s, [[1, P]], 0, -1, ALU.is_gt, 0.0)
            cut(neg_ssd, [[1, P]], 0, -1, ALU.is_ge, MASKED)
            cut(neg_att, [[-1, P]], 0, 1, ALU.is_ge, MASKED)
            nc.gpsimd.iota(iota_j[:, :], [[1, P]], base=0, channel_multiplier=0,
                           allow_small_or_imprecise_dtypes=True)
            nc.gpsimd.iota(erow[:, :], [[1, N_EXP]], base=1, channel_multiplier=0,
                           allow_small_or_imprecise_dtypes=True)
            nc.gpsimd.iota(BT0[:, :, :], [[P, NT], [-BLOCK, NB]], base=0, channel_multiplier=1,
                           allow_small_or_imprecise_dtypes=True).then_inc(const_ready, 1)
            for L in range(DEPTH):
                done, k = released["TA"]
                pool.wait_ge(*done(L, k))
                pool.dma_start(H[:, :, :], mem_in.rearrange("a (t p) d -> p (a t) d", p=P)).then_inc(in_mem, 16)
                if L + 1 < DEPTH:
                    pool.wait_ge(*x_ready(L, 2))
                    pool.dma_start(cols[:, :], cols_in[L + 1]).then_inc(in_params, 16)
                    pool.dma_start(rows[:, :], rows_in[L + 1:L + 2, :].to_broadcast([P, N_ROWS])) \
                        .then_inc(in_params, 16)

        def act_layer(act, L):
            act.wait_ge(in_params, 32 * (L + 1))
            na = [0]

            def step(ins):
                ins.then_inc(*act_step.up())
                act.wait_ge(*act_step(L, act_step.count(L)))

            def group():
                na[0] += 1
                act.wait_ge(*a_full(L, na[0]))
                return PA[(na[0] - 1) % 4]

            def col(name, at=0):
                return cols[:, COLS[name] + at:COLS[name] + at + 1]

            def copy(dst, src, scale=1.0):
                return act.activation(dst, src, ACT.Copy, scale=scale)

            def pair_of(bank):
                return bank[:, :].rearrange("p (j s) -> p j s", j=2)

            def copy_group(dst, src):
                copy(dst, src).then_inc(*a_free.up())

            def take_tiles(dst, tiles, gain):
                for at in range(0, tiles, 2):
                    bank = group()
                    for j in range(2):
                        last = copy(dst[:, at + j, :], bank[:, j * SEQ:(j + 1) * SEQ], gain(at + j))
                    last.then_inc(*a_free.up())

            def rstd(at, n, width, done):
                step(act.activation(rs[:, at:at + n], ss[:, at:at + n], ACT.Ln, bias=eps[:, :], scale=1.0 / width))
                act.activation(rs[:, at:at + n], rs[:, at:at + n], ACT.Exp, scale=-0.5).then_inc(*done.up())

            def squares(src, at):
                for tt in range(NT):
                    step(act.activation(junk, src[:, tt, :], ACT.Square, accum_out=ss[:, at + tt:at + tt + 1]))

            def softmax_exp(tt, keys, ready):
                act.wait_ge(*att_ready(L, ready))
                for h in range(4):
                    last = act.activation(prob[:, h, 0:keys], prob[:, h, 0:keys], ACT.Exp,
                                          bias=nmx[:, h:h + 1], accum_out=psm[:, h:h + 1])
                last.then_inc(*exp_ready.up())

            def take_p(tiles):
                for s in range(tiles):
                    copy_group(pT[:, s, :, :], group()[:, :].rearrange("p (h t) -> p h t", h=4))

            def take_o(dst, tt):
                copy_group(dst[:, :, tt * P:(tt + 1) * P], group()[:, 0:2 * P].rearrange("p (j t) -> p j t", j=2))

            if L == 0:
                act.wait_ge(in_x, 16)
            else:
                act.wait_ge(*x_added(first_block(L), 0))
            squares(X, 0)
            rstd(0, NT, D_MODEL, rstd_ready)
            take_tiles(HT, KT, lambda k: col("mix_g", k))
            for at in range(0, KT, 2):
                copy_group(XR[:, at:at + 2, 3:3 + SEQ], pair_of(group()))
            copy_group(hpad[:, :, CONV_W - 1:], pair_of(group()))
            act.activation(ctmp[:, :, :], pair_of(group()), ACT.Exp, scale=-1.0).then_inc(*a_free.up())
            for item in range(4, 8):
                width = WIDE if item < 7 else U_N - 3 * WIDE
                c0 = (item - 4) * WIDE
                for tt in range(NT):
                    copy_group(U[:, tt, c0:c0 + width], group()[:, 0:width])
            for at in range(0, KT, 2):
                act.wait_ge(*xbc_conv(L, at // 2 + 1))
                act.activation(XC[:, at:at + 2, :], XC[:, at:at + 2, :], ACT.Silu).then_inc(*xc_ready.up())
            for tt in range(NT):
                act.activation(Z[:, tt, :], group()[:, :], ACT.Silu).then_inc(*a_free.up())
            act.wait_ge(*dt_in(L, 1))
            step(act.activation(dts[:, 2, :, :], dts[:, 1, :, :], ACT.Exp, scale=-1.0))
            act.activation(anum[:, :], rows[:, R_ALOG:R_ALOG + SSD_H], ACT.Exp)
            act.activation(dts[:, 2, :, :], dts[:, 2, :, :], ACT.Ln, bias=one[:, :]).then_inc(*dt_log.up())
            act.wait_ge(*qk_ss(L, 1))
            rstd(2, 16, HD, qk_rstd)
            bank = group()
            act.activation(ctmp[:, 0, :], bank[:, 0:SEQ], ACT.Ln, bias=eps[:, :], scale=1.0 / D_CONV) \
                .then_inc(*a_free.up())
            act.wait_ge(*a_free(L, na[0]))
            act.activation(ctmp[:, 0, :], ctmp[:, 0, :], ACT.Exp, scale=-0.5).then_inc(*conv_rstd.up())
            copy_group(btok[:, :, :], group()[:, 0:2 * P].rearrange("p (g n) -> p g n", g=2))
            act.wait_ge(*cum_ready(L, 1))
            act.activation(ecum[:, :, :], ecum[:, :, :], ACT.Exp).then_inc(*ecum_ready.up())
            for tt in range(NT):
                for half in range(2):
                    act.activation(LM[:, tt, half * 4:half * 4 + 4, :],
                                   group()[:, :].rearrange("p (h l) -> p h l", h=4), ACT.Exp) \
                        .then_inc(*a_free.up())
            for at in (0, 2):
                copy_group(qiT[:, at:at + 2, :], pair_of(group()))
            copy_group(kiT[:, :], group()[:, 0:SEQ])
            for at in (0, 2):
                copy_group(qkT[:, at:at + 2, :], pair_of(group()))
            act.wait_ge(*conv_norm(L, 1))
            act.activation(ctmp[:, :, :], cacc[:, :, :], ACT.Exp, scale=-1.0).then_inc(*conv_exp.up())
            for n in range(NT * IDX_H // 2):
                keys = P * (n // (IDX_H // 2) + 1)
                bank = group()
                if n >= 2:
                    act.wait_ge(*score_used(L, n - 1))
                act.activation(rl[:, n % 2, :, 0:keys], pair_of(bank)[:, :, 0:keys], ACT.Relu) \
                    .then_inc(*a_free.up())
            copy_group(YT[:, 0:2, :], pair_of(group()))
            copy_group(st[:, :, :], pair_of(group()))
            act.wait_ge(in_mem, 16 * (L + 1))
            act.wait_ge(*score_used(L, NT * IDX_H // 2))
            squares(H, 18)
            rstd(18, NT, D_MODEL, mem_rstd)
            take_tiles(MT, KT, lambda k: col("mem_g", k))
            for tt in range(NT):
                copy_group(kvt[:, tt, :], group()[:, :])
            for tt in range(NT):
                softmax_exp(tt, P * (tt + 1), tt + 1)
                take_p(tt + 1)
                take_o(YT[:, 6:8, :], tt)
            act.wait_ge(*hn_ss(L, 1))
            rstd(20, NT * MEM_H, HD, hn_rstd)
            bank = group()
            copy(KTm[:, :, :], pair_of(bank), col("mk_g")).then_inc(*a_free.up())
            act.wait_ge(*y_ss(L, 1))
            rstd(28, 4, D_SSD // 2, y_rstd)
            take_tiles(YT[:, 2:6, :], 4, lambda c: col("ssd_g", c))
            act.wait_ge(*x_ready(L, 1))
            squares(X, 0)
            rstd(0, NT, D_MODEL, rstd_ready)
            take_tiles(HT, KT, lambda k: col("memx_g", k))
            copy_group(mq[:, :, :], pair_of(group()))
            act.wait_ge(*hn_ss(L, 2))
            rstd(20, NT * MEM_H, HD, hn_rstd)
            bank = group()
            copy(mqT[:, :, :], pair_of(bank), col("mq_g")).then_inc(*a_free.up())
            for tt in range(NT):
                softmax_exp(tt, SEQ, NT + tt + 1)
                take_p(2)
                take_o(oT, tt)
            act.wait_ge(*x_ready(L, 2))
            squares(X, 0)
            rstd(0, NT, D_MODEL, rstd_ready)
            act.wait_ge(*ffn_g_ready(L, 1))
            take_tiles(HT, KT, lambda k: ffn_g[:, k:k + 1])
            act.wait_ge(*top2_ready(L, 1))
            act.activation(rsc[:, 1, :], rsc[:, 0, :], ACT.Exp)
            act.activation(rel[:, :, :], rel[:, :, :], ACT.Exp).then_inc(*top2_exp.up())

            act.wait_ge(*table_ready(L, 1))
            more = act.value_load(tabi[0:1, 0:1], min_val=1, max_val=MAX_OVER + 1)

            def silu(g, done, i):
                act.wait_ge(*gu_full(g, done + 1))
                act.activation(sg[:, i % 2, :], PA[i % 2][:, 0:P], ACT.Silu).then_inc(silu_ready.sem, 1)

            with act.Fori(0, blocks_fixed(L) - 1 + more) as b:
                g = first_block(L) + b
                act.wait_ge(*pgt_full(g, 1))
                copy(PGT[:, :, :], PA[0][:, 256:512].rearrange("p (t j) -> p t j", t=NT)).then_inc(pgt_ready.sem, 1)
                with act.Fori(0, ROUNDS) as r:
                    for s in range(LOOP_SLOTS):
                        silu(g, r * LOOP_SLOTS + s, s)
                silu(g, FT - 1, 1)
                act.wait_ge(slot_free[LOOP_SLOTS], chunk_reads(LOOP_SLOTS, g) + 1)
                for half in range(2):
                    copy(yc[:, half * 512:(half + 1) * 512], PA[2 + half][:, :]).then_inc(yc_ready.sem, 1)

        @block.scalar
        def _(act):
            act.wait_ge(const_ready, 2)
            act.wait_ge(in_small, 48)
            act.wait_ge(trig_step, 1 + NT + 2 + len(TURN_PARTS))
            nc.scalar.activation(sn_[:, :, :], ang[:, :, :], ACT.Sin)
            nc.scalar.activation(kay[:, :, :], ang[:, :, :], ACT.Sin, scale=0.5).then_inc(trig_act, 1)
            for L in range(DEPTH):
                act_layer(act, L)

        def dve_layer(dve, L):
            dve.wait_ge(in_params, 32 * (L + 1))
            nv = [0]
            v = nc.vector

            def step(ins):
                ins.then_inc(*dve_step.up())
                dve.wait_ge(*dve_step(L, dve_step.count(L)))

            def note(ins):
                ins.then_inc(*dve_step.up())

            def group():
                nv[0] += 1
                dve.wait_ge(*v_full(L, nv[0]))
                return PV[(nv[0] - 1) % 4]

            def col(name, at=0, n=1):
                return cols[:, COLS[name] + at:COLS[name] + at + n]

            def along(ap, n):
                return ap.unsqueeze(len(ap.shape)).to_broadcast(list(ap.shape) + [n])

            def normalise(ready):
                dve.wait_ge(*rstd_ready(L, ready))
                for tt in range(NT):
                    v.tensor_scalar(H[:, tt, :], X[:, tt, :], rs[:, tt:tt + 1], None, ALU.mult) \
                        .then_inc(*h_ready.up())

            def head_squares(src, width, at, done):
                n = src.shape[2]
                tmp = prob[:, :, :].rearrange("p h s -> p (h s)")[:, 0:NT * n].rearrange("p (t n) -> p t n", t=NT)
                step(v.tensor_tensor(tmp, src, src, ALU.mult))
                v.tensor_reduce(ss[:, at:at + NT * n // width], tmp.rearrange("p t (h d) -> p (t h) d", d=width),
                                AX_X, ALU.add).then_inc(*done.up())

            def softmax_in(tt, keys, bias):
                for odd in range(2):
                    bank = group()
                    src = bank[:, 0:2 * keys].rearrange("p (h s) -> p h s", h=2)
                    dst = prob[:, :, :].rearrange("p (h o) s -> p o h s", o=2)[:, odd, :, 0:keys]
                    if bias is None:
                        v.tensor_scalar(dst, src, HD ** -0.5, None, ALU.mult).then_inc(*v_free.up())
                    else:
                        v.scalar_tensor_tensor(out=dst, in0=src, scalar=HD ** -0.5,
                                               in1=bias[:, 0:keys].unsqueeze(1).to_broadcast([P, 2, keys]),
                                               op0=ALU.mult, op1=ALU.add).then_inc(*v_free.up())
                dve.wait_ge(*v_free(L, nv[0]))
                v.tensor_reduce(nmx[:, :], prob[:, :, 0:keys], AX_X, ALU.max, negate=True).then_inc(*att_ready.up())

            def softmax_out(tt, keys, ready):
                dve.wait_ge(*exp_ready(L, ready))
                step(v.reciprocal(prs[:, :], psm[:, :]))
                v.tensor_tensor(prob[:, :, 0:keys], prob[:, :, 0:keys], along(prs[:, :], keys), ALU.mult) \
                    .then_inc(*p_ready.up())

            normalise(1)
            note(v.memset(XR[:, :, 0:3], 0.0))
            dve.wait_ge(*dve_step(L, dve_step.count(L)))
            for tile in range(KT):
                if tile % 2 == 0:
                    dve.wait_ge(*a_free(L, 4 + tile // 2 + 1))
            for at in range(0, KT, 2):
                for tap in range(SSD_CONV):
                    for tile in (at, at + 1):
                        w = col("ssd_w", tile * SSD_CONV + tap)
                        x = XR[:, tile, tap:tap + SEQ]
                        if tap == 0:
                            ins = v.tensor_scalar(XC[:, tile, :], x, w, col("ssd_b", tile), ALU.mult, ALU.add)
                        else:
                            ins = v.scalar_tensor_tensor(out=XC[:, tile, :], in0=x, scalar=w, in1=XC[:, tile, :],
                                                         op0=ALU.mult, op1=ALU.add)
                        if tap == SSD_CONV - 1 and tile % 2:
                            ins.then_inc(*xbc_conv.up())
                        else:
                            note(ins)
                    if tap < SSD_CONV - 1:
                        dve.wait_ge(*dve_step(L, dve_step.count(L)))
            dve.wait_ge(*a_free(L, 10))
            step(v.tensor_scalar(ctmp[:, :, :], ctmp[:, :, :], 1.0, None, ALU.add))
            step(v.reciprocal(ctmp[:, :, :], ctmp[:, :, :]))
            step(v.tensor_tensor(hpad[:, :, CONV_W - 1:], hpad[:, :, CONV_W - 1:], ctmp[:, :, :], ALU.mult))
            for tap in range(CONV_W):
                for j in range(2):
                    w = col("conv_w", j * CONV_W + tap)
                    x = hpad[:, j, tap:tap + SEQ]
                    if tap == 0:
                        ins = v.tensor_scalar(cacc[:, j, :], x, w, None, ALU.mult)
                    else:
                        dve.wait_ge(*dve_step(L, dve_step.count(L) - 1))
                        ins = v.scalar_tensor_tensor(out=cacc[:, j, :], in0=x, scalar=w, in1=cacc[:, j, :],
                                                     op0=ALU.mult, op1=ALU.add)
                    if tap == CONV_W - 1 and j == 1:
                        ins.then_inc(*conv_acc.up())
                    else:
                        note(ins)
            dve.wait_ge(*conv_acc(L, 1))
            bank = group()
            v.scalar_tensor_tensor(out=cacc[:, :, :], in0=bank[:, 0:SEQ].unsqueeze(1).to_broadcast([P, 2, SEQ]),
                                   scalar=-1.0 / D_CONV, in1=cacc[:, :, :], op0=ALU.mult, op1=ALU.add) \
                .then_inc(*v_free.up())
            dve.wait_ge(*v_free(L, nv[0]))
            v.tensor_tensor(ctmp[:, :, :], cacc[:, :, :], cacc[:, :, :], ALU.mult).then_inc(*conv_centred.up())
            dve.wait_ge(*a_free(L, 18))
            for tt in range(NT):
                step(v.tensor_tensor(dts[:, 0, tt, :], U[:, tt, U_DT:U_DT + SSD_H], rows[:, R_DTB:R_DTB + SSD_H],
                                     ALU.add))
            v.scalar_tensor_tensor(out=dts[:, 1, :, :], in0=dts[:, 0, :, :], scalar=-1.0, in1=dts[:, 0, :, :],
                                   op0=ALU.mult, op1=ALU.max).then_inc(*dt_in.up())
            head_squares(U[:, :, 0:2 * D_ATT], HD, 2, qk_ss)
            dve.wait_ge(*dt_log(L, 1))
            step(v.scalar_tensor_tensor(out=dts[:, 3, :, :], in0=dts[:, 0, :, :], scalar=0.0, in1=dts[:, 2, :, :],
                                        op0=ALU.max, op1=ALU.add))
            an = anum[:, :].unsqueeze(1).to_broadcast([P, NT, SSD_H])
            step(v.tensor_tensor(dts[:, 5, :, :], dts[:, 3, :, :], an, ALU.mult))
            v.tensor_scalar(dts[:, 4, :, :], dts[:, 5, :, :], -1.0, None, ALU.mult).then_inc(*a_ready.up())
            dve.wait_ge(*a_ready(L, 1))
            for tt in range(NT):
                ins = v.tensor_tensor(TA[:, tt, :, :], tri[:, :].unsqueeze(1).to_broadcast([P, SSD_H, P]),
                                      along(dts[:, 4, tt, :], P), ALU.mult)
            ins.then_inc(*a_ready.up())
            for tt in range(NT):
                bank = group()
                src = bank[:, :].rearrange("p (h d) -> p h d", h=SSD_H)
                note(v.tensor_tensor(xd[:, tt, :].rearrange("p (h d) -> p h d", h=SSD_H), src,
                                     along(dts[:, 3, tt, :], SSD_P), ALU.mult))
                v.tensor_tensor(ysk[:, tt, :].rearrange("p (h d) -> p h d", h=SSD_H), src,
                                along(rows[:, R_D:R_D + SSD_H], SSD_P), ALU.mult).then_inc(*v_free.up())
            bank = group()
            v.tensor_copy(cum[:, :, :, :], bank[:, 0:32].rearrange("p (t k h) -> p t k h", t=NT, k=2)) \
                .then_inc(*v_free.up())
            dve.wait_ge(*v_free(L, nv[0]))
            note(v.tensor_tensor(ecum[:, 0, :], cum[:, 0, 1, :], cum[:, 0, 0, :], ALU.subtract))
            v.tensor_copy(ecum[:, 1, :], cum[:, 1, 0, :]).then_inc(*cum_ready.up())
            dve.wait_ge(*qk_rstd(L, 1))
            qk = U[:, :, 0:2 * D_ATT]
            for tt in range(NT):
                step(v.tensor_tensor(qk[:, tt, :].rearrange("p (h d) -> p h d", d=HD),
                                     qk[:, tt, :].rearrange("p (h d) -> p h d", d=HD),
                                     along(rs[:, 2 + tt * 8:10 + tt * 8], HD), ALU.mult))
                gains = rows[:, R_QK:R_QK + 2 * HD].rearrange("p (m d) -> p m d", m=2).unsqueeze(2) \
                    .to_broadcast([P, 2, ATT_H, HD])
                step(v.tensor_tensor(qk[:, tt, :].rearrange("p (m h d) -> p m h d", m=2, d=HD),
                                     qk[:, tt, :].rearrange("p (m h d) -> p m h d", m=2, d=HD), gains, ALU.mult))
            heads = U[:, :, 0:U_HEADS * HD].rearrange("p t (h d) -> p t h d", d=HD)
            x1, x2 = heads[:, :, :, 0:8], heads[:, :, :, 8:16]
            c_, s_ = (t[:, :, :].unsqueeze(2).to_broadcast([P, NT, U_HEADS, 8]) for t in (cs_, sn_))
            for i, (x, y) in enumerate(((x1, c_), (x2, s_), (x2, c_), (x1, s_))):
                note(v.tensor_tensor(rt[i][:, :, :, :], x, y, ALU.mult))
            dve.wait_ge(*dve_step(L, dve_step.count(L)))
            for lo, hi in ((0, 2 * ATT_H), (3 * ATT_H, U_HEADS)):
                note(v.tensor_tensor(x1[:, :, lo:hi, :], rt[0][:, :, lo:hi, :], rt[1][:, :, lo:hi, :], ALU.subtract))
                note(v.tensor_tensor(x2[:, :, lo:hi, :], rt[2][:, :, lo:hi, :], rt[3][:, :, lo:hi, :], ALU.add))
            dve.wait_ge(*dve_step(L, dve_step.count(L)))
            note(v.tensor_scalar(U[:, :, U_W:U_W + IDX_H], U[:, :, U_W:U_W + IDX_H],
                                 IDX_H ** -0.5 * HD ** -0.5, None, ALU.mult))
            for j in range(2):
                ins = v.tensor_copy(kk[:, :, j * HD:(j + 1) * HD], U[:, :, U_KI:U_KI + HD])
            ins.then_inc(*rope_ready.up())
            dve.wait_ge(*conv_rstd(L, 1))
            step(v.tensor_tensor(cacc[:, :, :], cacc[:, :, :], ctmp[:, 0, :].unsqueeze(1).to_broadcast([P, 2, SEQ]),
                                 ALU.mult))
            for j in range(2):
                ins = v.tensor_scalar(cacc[:, j, :], cacc[:, j, :], col("ln_g", j), col("ln_b", j),
                                      ALU.mult, ALU.add)
            ins.then_inc(*conv_norm.up())
            dve.wait_ge(*ecum_ready(L, 1))
            v.tensor_tensor(xdd[:, :].rearrange("p (h d) -> p h d", h=SSD_H),
                            xd[:, 0, :].rearrange("p (h d) -> p h d", h=SSD_H), along(ecum[:, 0, :], SSD_P),
                            ALU.mult).then_inc(*xdd_ready.up())
            bank = group()
            dve.wait_ge(*a_free(L, A_SEG))
            for tt in range(NT):
                cb = bank[:, tt * 2 * P:(tt + 1) * 2 * P].rearrange("p (g l) -> p g l", g=2).unsqueeze(2) \
                    .to_broadcast([P, 2, 4, P])
                lm = LM[:, tt, :, :].rearrange("p (g h) l -> p g h l", g=2)
                v.tensor_tensor(lm, lm, cb, ALU.mult).then_inc(*m_ready.up())
            dve.wait_ge(*m_ready(L, NT))
            v.tensor_copy(m8[:, 0, 0:1], one[:, :]).then_inc(*v_free.up())
            dve.wait_ge(*conv_exp(L, 1))
            step(v.tensor_scalar(ctmp[:, :, :], ctmp[:, :, :], 1.0, None, ALU.add))
            step(v.reciprocal(ctmp[:, :, :], ctmp[:, :, :]))
            v.tensor_tensor(ctmp[:, :, :], ctmp[:, :, :], cacc[:, :, :], ALU.mult).then_inc(*conv_out.up())
            n = 0
            for tt in range(NT):
                keys = P * (tt + 1)
                for pair in range(IDX_H // 2):
                    n += 1
                    dve.wait_ge(*a_free(L, A_INDEX + n))
                    for j in range(2):
                        h = index_head(pair, j)
                        w = U[:, tt, U_W + h:U_W + h + 1]
                        x, s = rl[:, (n - 1) % 2, j, 0:keys], score[:, tt, 0:keys]
                        if h == 0:
                            step(v.tensor_scalar(s, x, w, None, ALU.mult))
                        elif j == 0:
                            step(v.scalar_tensor_tensor(out=s, in0=x, scalar=w, in1=s, op0=ALU.mult, op1=ALU.add))
                        else:
                            v.scalar_tensor_tensor(out=s, in0=x, scalar=w, in1=s, op0=ALU.mult, op1=ALU.add) \
                                .then_inc(*score_used.up())
                            dve.wait_ge(*score_used(L, n))
            dve.wait_ge(*mem_rstd(L, 1))
            for tt in range(NT):
                v.tensor_scalar(H[:, tt, :], H[:, tt, :], rs[:, 18 + tt:19 + tt], None, ALU.mult) \
                    .then_inc(*mem_ready.up())
            for tt in range(NT):
                d = slice(tt * P, (tt + 1) * P)
                note(v.tensor_tensor(score[:, tt, d], score[:, tt, d], neg_att[:, :], ALU.add))
            for i in range(TOPK // 8):
                dve.wait_ge(*dve_step(L, dve_step.count(L)))
                for tt in range(NT):
                    note(v.max(m8[:, tt, :], score[:, tt, 0:P * (tt + 1)]))
                dve.wait_ge(*dve_step(L, dve_step.count(L)))
                for tt in range(NT):
                    s = score[:, tt, 0:P * (tt + 1)]
                    note(v.match_replace(s, m8[:, tt, :], s, TAKEN))
            dve.wait_ge(*dve_step(L, dve_step.count(L)))
            for tt in range(NT):
                keys = P * (tt + 1)
                note(v.tensor_scalar(abias[:, tt, 0:keys], score[:, tt, 0:keys], TAKEN, MASKED,
                                     ALU.not_equal, ALU.mult))
            dve.wait_ge(*dve_step(L, dve_step.count(L)))
            for tt in range(NT):
                d = slice(tt * P, (tt + 1) * P)
                note(v.tensor_tensor(abias[:, tt, d], abias[:, tt, d], neg_att[:, :], ALU.add))
            for tt in range(NT):
                bank = group()
                v.tensor_tensor(ysk[:, tt, :], ysk[:, tt, :], bank[:, :], ALU.add).then_inc(*v_free.up())
            bank = group()
            v.tensor_tensor(xd[:, 1, :].rearrange("p (h d) -> p h d", h=SSD_H),
                            bank[:, :].rearrange("p (h d) -> p h d", h=SSD_H), along(ecum[:, 1, :], SSD_P),
                            ALU.mult).then_inc(*v_free.up())
            dve.wait_ge(*v_free(L, nv[0]))
            step(v.tensor_tensor(ysk[:, 1, :], ysk[:, 1, :], xd[:, 1, :], ALU.add))
            step(v.tensor_tensor(ysk[:, :, :], ysk[:, :, :], Z[:, :, :], ALU.mult))
            head_squares(ysk[:, :, :], D_SSD // 2, 28, y_ss)
            dve.wait_ge(*a_free(L, A_KV))
            dve.wait_ge(*y_ss(L, 1))
            head_squares(kvt[:, :, 0:D_ATT], HD, 20, hn_ss)
            dve.wait_ge(*hn_ss(L, 1))
            for tt in range(NT):
                keys = P * (tt + 1)
                softmax_in(tt, keys, abias[:, tt, :])
                softmax_out(tt, keys, tt + 1)
                if tt + 1 < NT:
                    dve.wait_ge(*v_full(L, nv[0] + 1))
            dve.wait_ge(*hn_rstd(L, 1))
            kh = kvt[:, :, 0:D_ATT].rearrange("p t (h d) -> p t h d", d=HD)
            v.tensor_tensor(kh, kh, along(rs[:, 20:28].rearrange("p (t h) -> p t h", t=NT), HD), ALU.mult) \
                .then_inc(*hn_ready.up())
            dve.wait_ge(*y_rstd(L, 1))
            yh = ysk[:, :, :].rearrange("p t (g d) -> p t g d", g=2)
            v.tensor_tensor(yh, yh, along(rs[:, 28:32].rearrange("p (t g) -> p t g", t=NT), SEQ), ALU.mult) \
                .then_inc(*y_ready.up())
            for item in range(12, 15):
                c0 = (item - 12) * WIDE
                width = min(WIDE, D_MODEL - c0)
                for tt in range(NT):
                    bank = group()
                    x = X[:, tt, c0:c0 + width]
                    v.tensor_tensor(x, x, bank[:, 0:width], ALU.add).then_inc(*v_free.up())
            dve.wait_ge(*v_free(L, nv[0]))
            v.tensor_copy(ffn_g[:, :], ffn_g2[:, L, :]).then_inc(*x_ready.up())
            normalise(2)
            dve.wait_ge(*a_free(L, A_MQ))
            head_squares(mq[:, :, :], HD, 20, hn_ss)
            dve.wait_ge(*hn_rstd(L, 2))
            qh = mq[:, :, :].rearrange("p t (h d) -> p t h d", d=HD)
            v.tensor_tensor(qh, qh, along(rs[:, 20:28].rearrange("p (t h) -> p t h", t=NT), HD), ALU.mult) \
                .then_inc(*hn_ready.up())
            for tt in range(NT):
                softmax_in(tt, SEQ, None)
                softmax_out(tt, SEQ, NT + tt + 1)
                if tt + 1 < NT:
                    dve.wait_ge(*v_full(L, nv[0] + 1))
            for half in range(2):
                for tt in range(NT):
                    bank = group()
                    x = X[:, tt, half * 512:(half + 1) * 512]
                    v.tensor_tensor(x, x, bank[:, :], ALU.add).then_inc(*v_free.up())
            dve.wait_ge(*v_free(L, nv[0]))
            v.tensor_copy(flag[:, :], flags[:, L:L + 1]).then_inc(*x_ready.up())
            normalise(3)
            v.tensor_copy(flag[:, :], flags[:, L:L + 1]).then_inc(*ffn_g_ready.up())
            bank = group()
            v.tensor_copy(rin[:, :, 0:N_EXP], bank[:, 0:NT * N_EXP].rearrange("p (t e) -> p t e", t=NT)) \
                .then_inc(*v_free.up())
            dve.wait_ge(*v_free(L, nv[0]))
            for tt in range(NT):
                note(v.max(m8[:, tt, :], rin[:, tt, 0:N_EXP]))
            dve.wait_ge(*dve_step(L, dve_step.count(L)))
            note(v.tensor_tensor(rsc[:, 0, :], m8[:, :, 1], m8[:, :, 0], ALU.subtract))
            step(v.tensor_copy(tr[:, :, 0:2], m8[:, :, 0:2]))
            for tt in range(NT):
                note(v.tensor_scalar(rel[:, tt, :], rin[:, tt, 0:N_EXP], m8[:, tt, 0:1], None, ALU.subtract))
                note(v.match_replace(mr[:, tt, :], tr[:, tt, :], rin[:, tt, :], PICKED))
            dve.wait_ge(*dve_step(L, dve_step.count(L)))
            v.tensor_scalar(rmask[:, :, :], mr[:, :, 0:N_EXP], PICKED, None, ALU.is_equal).then_inc(*mask_ready.up())
            v.tensor_copy(tabf[:, 7:8], one[:, :]).then_inc(*top2_ready.up())
            dve.wait_ge(*top2_exp(L, 1))
            dve.wait_ge(*mask_ready(L, 1))
            note(v.tensor_scalar(rsc[:, 2, :], rsc[:, 1, :], 1.0, None, ALU.add))
            step(v.tensor_tensor(gate[:, :, :], rel[:, :, :], rmask[:, :, :], ALU.mult))
            step(v.reciprocal(rsc[:, 3, :], rsc[:, 2, :]))
            note(v.tensor_tensor(gate[:, :, :], gate[:, :, :], along(rsc[:, 3, :], N_EXP), ALU.mult))
            bank = group()
            step(v.scalar_tensor_tensor(out=posm[:, :, :], in0=bank[:, 0:NT * N_EXP]
                                        .rearrange("p (t e) -> p t e", t=NT), scalar=1.0, in1=rmask[:, :, :],
                                        op0=ALU.add, op1=ALU.mult))
            note(v.tensor_scalar(posm[:, :, :], posm[:, :, :], -1.0, None, ALU.add))
            v.tensor_scalar(cnt[:, 0, :], bank[:, 16:24], BLOCK + 0.5, None, ALU.is_gt).then_inc(*v_free.up())
            dve.wait_ge(*v_free(L, nv[0]))
            step(v.tensor_tensor_scan(cnt[:, 1, :], ones[:, 0:N_EXP], cnt[:, 0, :], 0.0, ALU.mult, ALU.add))
            for k in range(MAX_OVER):
                note(v.scalar_tensor_tensor(out=oh[:, k, :], in0=cnt[:, 1, :], scalar=float(k + 1), in1=cnt[:, 0, :],
                                            op0=ALU.is_equal, op1=ALU.mult))
            note(v.tensor_copy(BT[:, :, 0:N_EXP], posm[:, :, :]))
            note(v.tensor_copy(GT[:, :, 0:N_EXP], gate[:, :, :]))
            note(v.tensor_scalar(tabf[:, 0:1], cnt[:, 1, N_EXP - 1:N_EXP], flag[:, :], 1.0, ALU.mult, ALU.add))
            step(v.tensor_scalar(tabf[:, 1:2], flag[:, :], float(N_EXP), None, ALU.mult))
            for k in range(MAX_OVER):
                for i, (x, at, dst) in enumerate(((erow[:, :], 0.0, tabf[:, 2 + k:3 + k]),
                                   (posm[:, 0, :], -float(BLOCK), BT[:, 0, N_EXP + k:N_EXP + k + 1]),
                                   (posm[:, 1, :], -float(BLOCK), BT[:, 1, N_EXP + k:N_EXP + k + 1]),
                                   (gate[:, 0, :], 0.0, GT[:, 0, N_EXP + k:N_EXP + k + 1]),
                                   (gate[:, 1, :], 0.0, GT[:, 1, N_EXP + k:N_EXP + k + 1]))):
                    note(v.tensor_tensor_reduce(rtmp[:, 5 * k + i, :], oh[:, k, :], x, 1.0, at, ALU.mult, ALU.add, dst))
            dve.wait_ge(*dve_step(L, dve_step.count(L)))
            note(v.tensor_tensor(BT[:, :, :], BT[:, :, :], BT0[:, :, :], ALU.subtract))
            step(v.tensor_scalar(rsc[:, 0, 0:1], flag[:, :], -1.0, 1.0, ALU.mult, ALU.add))
            note(v.scalar_tensor_tensor(out=BT[:, :, :], in0=BT[:, :, :], scalar=flag[:, :], in1=BT0[:, :, :],
                                        op0=ALU.mult, op1=ALU.add))
            note(v.tensor_scalar(GT[:, :, :], GT[:, :, :], flag[:, :], rsc[:, 0, 0:1], ALU.mult, ALU.add))
            v.tensor_copy(tabi[:, :], tabf[:, :]).then_inc(*table_ready.up())
            dve.wait_ge(*table_ready(L, 1))

            more = dve.value_load(tabi[0:1, 0:1], min_val=1, max_val=MAX_OVER + 1)

            def activate(g, done, i):
                dve.wait_ge(*silu_ready(g, done + 1))
                v.tensor_tensor(aT[:, i % 2, :], sg[:, i % 2, :], PA[i % 2][:, P:2 * P], ALU.mult) \
                    .then_inc(act_ready.sem, 1)

            with dve.Fori(0, blocks_fixed(L) - 1 + more) as b:
                g = first_block(L) + b
                for tt in range(NT):
                    ins = v.tensor_scalar(PM[:, tt, :], iota_j[:, :], BT[:, tt, bass.ds(b, 1)], None, ALU.is_equal)
                ins.then_inc(place_ready.sem, 1)
                for tt in range(NT):
                    ins = v.tensor_scalar(PG[:, tt, :], iota_j[:, :], BT[:, tt, bass.ds(b, 1)],
                                          GT[:, tt, bass.ds(b, 1)], ALU.is_equal, ALU.mult)
                ins.then_inc(place_ready.sem, 1)
                for half in range(2):
                    dve.wait_ge(*hc_full(g, half + 1))
                    v.tensor_tensor(hcT[:, half * 4:half * 4 + 4, :],
                                    PV[half][:, :].rearrange("p (c j) -> p c j", c=4),
                                    along(ffn_g[:, half * 4:half * 4 + 4], P), ALU.mult).then_inc(hc_ready.sem, 1)
                with dve.Fori(0, ROUNDS) as r:
                    for s in range(LOOP_SLOTS):
                        activate(g, r * LOOP_SLOTS + s, s)
                activate(g, FT - 1, 1)
                for i in range(4):
                    tt, half = i % 2, i // 2
                    dve.wait_ge(*sc_full(g, i + 1))
                    x = X[:, tt, half * 512:(half + 1) * 512]
                    v.tensor_tensor(x, x, PV[2 + i % 2][:, :], ALU.add).then_inc(x_added.sem, 1)

        @block.vector
        def _(dve):
            for j in range(8):
                nc.vector.memset(inv[:, j:j + 1], ROPE_THETA ** (-2.0 * j / ROT))
            nc.vector.memset(rin[:, :, :], PAD)
            nc.vector.memset(tr[:, :, :], PAD).then_inc(act_ready.sem, 1)
            nc.vector.memset(tabf[:, :], 0.0).then_inc(x_added.sem, 1)
            dve.wait_ge(x_added.sem, 1)
            dve.wait_ge(in_small, 48)
            n = [0]

            def link(ins):
                n[0] += 1
                ins.then_inc(trig_step, 1)
                dve.wait_ge(trig_step, n[0])
            link(nc.vector.tensor_copy(pos_f[:, :], pos_i[:, :]))
            for t in range(NT):
                link(nc.vector.tensor_scalar(ang[:, t, :], inv[:, :], pos_f[:, t:t + 1], None, ALU.mult))
            link(nc.vector.tensor_scalar(kay[:, :, :], ang[:, :, :], 1.0 / TWO_PI, ROUND_BIG, ALU.mult, ALU.add))
            link(nc.vector.tensor_scalar(kay[:, :, :], kay[:, :, :], -ROUND_BIG, None, ALU.add))
            for part in TURN_PARTS:
                link(nc.vector.scalar_tensor_tensor(out=ang[:, :, :], in0=kay[:, :, :], scalar=-part,
                                                    in1=ang[:, :, :], op0=ALU.mult, op1=ALU.add))
            dve.wait_ge(trig_act, 1)
            link(nc.vector.tensor_tensor(cs_[:, :, :], kay[:, :, :], kay[:, :, :], ALU.mult))
            link(nc.vector.tensor_scalar(cs_[:, :, :], cs_[:, :, :], -2.0, 1.0, ALU.mult, ALU.add))
            dve.wait_ge(const_ready, 2)
            for L in range(DEPTH):
                dve_layer(dve, L)

        if DEBUG:
            print({s.name: s.n / DEPTH for s in signals if s.n and s.n / DEPTH != 1})


def kernel(**inputs):
    import numpy as np
    import concourse.bacc as bacc
    from concourse.bass_utils import run_bass_kernel_spmd

    a = {k: np.asarray(v) for k, v in inputs.items()}

    def tiles(w):
        return w.reshape(-1, P, w.shape[-1]).transpose(1, 0, 2).reshape(P, -1)

    def column(v):
        return v.reshape(-1, P).T

    cols, rows, wmix = [], [], np.zeros((DEPTH * MIX_ITEMS, P, SLOT), np.float32)
    for l in range(DEPTH):
        w_in, w_out, w_kv = a["w_in"][l], a["w_out"][l], a["memx_w_kv"][l]
        dw = a["conv_dw_w"][l].T.reshape(2, P, CONV_W).transpose(1, 0, 2).reshape(P, -1)
        sw = a["ssd_conv_w"][l].T.reshape(KT, P, SSD_CONV).transpose(1, 0, 2).reshape(P, -1)
        twice = [np.concatenate([a[n][l]] * 2)[:, None] for n in ("memx_q_norm_g", "memx_k_norm_g")]
        cols.append(np.concatenate([column(a["mix_norm_g"][l]), column(a["memx_norm_g"][l]),
                                    column(a["mem_norm_g"][l]), dw, column(a["conv_ln_g"][l]),
                                    column(a["conv_ln_b"][l]), sw, column(a["ssd_conv_b"][l]),
                                    column(a["ssd_norm_g"][l])] + twice, axis=1))
        rows.append(np.concatenate([a["att_q_norm_g"][l], a["att_k_norm_g"][l], a["ssd_dt_bias"][l],
                                    a["ssd_a_log"][l], a["ssd_d"][l]]))
        xbc_conv = np.concatenate([w_in[:, 1024:2048], w_in[:, 0:512]], axis=1)
        u = np.concatenate([w_in[:, 2056:3408], w_in[:, 2048:2056]], axis=1)
        items = [tiles(xbc_conv[:, i * WIDE:(i + 1) * WIDE]) for i in range(4)]
        items += [tiles(u[:, i * WIDE:(i + 1) * WIDE]) for i in range(4)]
        items += [tiles(w_in[:, 512:512 + WIDE]),
                  np.concatenate([tiles(w_in[:, 512 + WIDE:1024]), tiles(a["conv_pw_w"][l])], axis=1)]
        items += [tiles(w_kv[:, 0:WIDE]), tiles(w_kv[:, WIDE:])]
        w_o = a["memx_w_o"][l]
        items += [tiles(w_out[:, 0:WIDE]), tiles(w_out[:, WIDE:2 * WIDE]),
                  np.concatenate([tiles(w_out[:, 2 * WIDE:]), w_o[0:P]], axis=1),
                  np.concatenate([tiles(a["memx_w_q"][l]), w_o[P:2 * P]], axis=1)]
        for i, item in enumerate(items):
            wmix[l * MIX_ITEMS + i, :, 0:item.shape[1]] = item
    wffn = np.empty(((1 + N_EXP) * FT, P, SLOT), np.float32)
    for kind, at in (("w_gate", 0), ("w_up", KT * P)):
        for e in range(1 + N_EXP):
            w = a["ffn_" + kind][0] if e == 0 else a["moe_" + kind][0][e - 1]
            wffn[e * FT:(e + 1) * FT, :, at:at + KT * P] = \
                w.reshape(KT, P, FT, P).transpose(2, 1, 0, 3).reshape(FT, P, KT * P)
    for e in range(1 + N_EXP):
        w = a["ffn_w_down"][0] if e == 0 else a["moe_w_down"][0][e - 1]
        wffn[e * FT:(e + 1) * FT, :, 2 * KT * P:] = w.reshape(FT, P, D_MODEL)

    arrays = {
        "x_dram": a["x"], "mem_dram": a["mem"],
        "positions_dram": np.ascontiguousarray(a["positions"].reshape(NT, P).T),
        "cols_dram": np.stack(cols), "rows_dram": np.stack(rows),
        "ffn_g_dram": np.ascontiguousarray(a["ffn_norm_g"].reshape(DEPTH, KT, P).transpose(2, 0, 1)),
        "router_dram": np.ascontiguousarray(tiles(a["moe_w_router"][0]).reshape(P, KT, N_EXP)),
        "wmix_dram": wmix, "wffn_dram": wffn,
    }
    nc = bacc.Bacc("TRN2", target_bir_lowering=False, num_devices=1)
    args = [nc.dram_tensor(n, v.shape, mybir.dt.from_np(v.dtype), kind="ExternalInput").ap()
            for n, v in arrays.items()]
    args.append(nc.dram_tensor("out_dram", (1, SEQ, D_MODEL), F32, kind="ExternalOutput").ap())
    trunk_kernel(nc, *args)
    r = run_bass_kernel_spmd(nc, [arrays], core_ids=[0])
    return r.results[0]["out_dram"]
```

```python
from contextlib import ExitStack

import concourse.bass as bass
from concourse import mybir

F32 = mybir.dt.float32
F32R = mybir.dt.float32r
I32 = mybir.dt.int32
ALU = mybir.AluOpType
ACT = mybir.ActivationFunctionType
AX_X = mybir.AxisListType.X

P = 128
SEQ, D_MODEL, DEPTH = 256, 1024, 2
NT = SEQ // P
KT = D_MODEL // P
D_CONV, CONV_W = 256, 31
D_SSD, SSD_H, SSD_P, SSD_CONV = 512, 8, 64, 4
D_ATT, ATT_H, HD = 256, 4, 64
IDX_H = 8
TOPK = 64
ROPE_THETA, ROT = 500000.0, 16
MEM_H = 4
D_FF, N_EXP = 2816, 8
FT = D_FF // P
N_MOE = DEPTH // 2
EPS = 1e-6

WSLOTS = 8
SLOT = 3 * KT * P
MIX_ITEMS = 16
WIDE = SLOT // KT
LOOP_SLOTS = WSLOTS - 1
ROUNDS = FT // LOOP_SLOTS
BLOCK = 96
MAX_OVER = (2 * SEQ) // (BLOCK + 1)
FURTHER = (SEQ - 1) // BLOCK
N_CAND = FURTHER * N_EXP
GU_COLS, D_COLS = 2 * KT * P, D_MODEL

U_V, U_QI, U_KI, U_W, U_DT, U_N = 512, 768, 1280, 1344, 1352, 1360
U_HEADS = 21

COLS = {}
_n = 0
for _name, _w in (("mix_g", KT), ("memx_g", KT), ("mem_g", KT), ("conv_w", 2 * CONV_W), ("ln_g", 2),
                  ("ln_b", 2), ("ssd_w", KT * SSD_CONV), ("ssd_b", KT), ("ssd_g", 4),
                  ("mq_g", 1), ("mk_g", 1)):
    COLS[_name] = _n
    _n += _w
N_COLS = _n
R_QK, R_DTB, R_ALOG, R_D, N_ROWS = 0, 128, 136, 144, 152

MASKED = -1e30
TAKEN = -3e38
PAD = -3e38
PICKED = -2e38


TWO_PI = 6.283185307179586
TURN_PARTS = (6.28125, 0.0019350051879882812, 3.0199159819567e-07)
ROUND_BIG = 12582912.0
DEBUG = False

RAISES = {
    "x_low": 4,
    "x_high": 4,
    "router_step": 52,
    "router_full": 2,
    "a_full": 71, "a_free": 71, "v_full": 26, "v_free": 26, "dve_step": 172, "act_step": 17,
    "x_ready": 2, "rstd_ready": 3, "h_ready": 6, "xbc_conv": 4, "xc_ready": 4, "a_ready": 2,
    "m_ready": 2, "score_used": 8, "att_ready": 4, "exp_ready": 4, "p_ready": 4, "mem_ready": 2,
    "hn_ss": 2, "hn_rstd": 2, "hn_ready": 2,
    "gu_full": FT, "silu_ready": FT, "act_ready": FT, "high_gu": FT, "low_gu": FT, "high_d": FT, "low_d": FT,
    "turned": FT, "act_high": FT, "act_low": FT, "dense_added": 4, "hc_full": 2, "hc_ready": 2,
    "sc_full": 4, "moe_added": 4,
}
A_SEG, A_INDEX, A_KV, A_MQ = 26, 31, 47, 60


class Signal:

    def __init__(self, sem, name, per, start=0, laps=1):
        self.sem, self.name, self.per, self.start, self.laps, self.n = sem, name, per, start, laps, 0

    def count(self, lap):
        return self.n - lap * self.per

    def up(self):
        self.n += 1
        return self.sem, 1

    def __call__(self, lap, k):
        return self.sem, lap * self.per + (self.start + k)


def index_head(pair, j):
    return 4 * (pair // 2) + pair % 2 + 2 * j


def trunk_kernel(nc, x_in, mem_in, pos_in, cols_in, rows_in, ffn_g_in, router_in, wmix, wffn, out):
    with ExitStack() as ctx:
        def sb(name, shape, dt=F32):
            return ctx.enter_context(nc.sbuf_tensor(name, shape, dt))

        signals = []

        def signal(name, start=0, laps=DEPTH):
            s = Signal(ctx.enter_context(nc.semaphore(name)), name, RAISES.get(name, 1), start, laps)
            signals.append(s)
            return s

        XR_COLS = KT * (SEQ + 3)
        shared = (("W", [P, WSLOTS, SLOT]), ("FB", [P, XR_COLS + KT * SEQ + 2 * NT * D_SSD]),
                  ("H", [P, NT, D_MODEL]), ("HT", [P, KT, SEQ]), ("U", [P, NT, U_N]))
        with ExitStack() as names:
            W, FB, H, HT, U = (names.enter_context(nc.sbuf_tensor(n, shape, F32)) for n, shape in shared)
        W_R, FB_R, H_R, HT_R, U_R = (sb(n + "_R", shape, F32R) for n, shape in shared)
        X = sb("X", [P, NT, D_MODEL])
        XR_LM = FB[:, 0:XR_COLS]
        XR = XR_LM.rearrange("p (k s) -> p k s", k=KT)
        XC = FB[:, XR_COLS:XR_COLS + KT * SEQ].rearrange("p (k s) -> p k s", k=KT)
        LM = XR_LM[:, 0:NT * SSD_H * P].rearrange("p (t h l) -> p t h l", t=NT, h=SSD_H)
        Z = sb("Z", [P, NT, D_SSD])
        hpad = sb("hpad", [P, 2, SEQ + CONV_W - 1])
        cacc = sb("cacc", [P, 2, SEQ])
        ctmp = sb("ctmp", [P, 2, SEQ])
        xd, ysk = (FB[:, XR_COLS + KT * SEQ + i * NT * D_SSD:XR_COLS + KT * SEQ + (i + 1) * NT * D_SSD]
                   .rearrange("p (t n) -> p t n", t=NT) for i in range(2))
        WHgu = [FB_R[:, i * GU_COLS:(i + 1) * GU_COLS] for i in range(2)]
        WHd = [FB_R[:, 2 * GU_COLS + i * D_COLS:2 * GU_COLS + (i + 1) * D_COLS] for i in range(2)]
        xdd = sb("xdd", [P, D_SSD])
        btok = sb("btok", [P, 2, P])
        st = sb("st", [P, 2, 256])
        qkT = sb("qkT", [P, 4, SEQ])
        qiT = sb("qiT", [P, 4, SEQ])
        kiT = sb("kiT", [P, SEQ])
        kk = sb("kk", [P, NT, P])
        score = sb("score", [P, NT, SEQ])
        rl = sb("rl", [P, 2, 2, SEQ])
        abias = sb("abias", [P, NT, SEQ])
        prob = sb("prob", [P, 4, SEQ])
        pT = sb("pT", [P, 2, 4, P])
        RN = NT * U_HEADS * 8
        TA = H[:, :, :].rearrange("p t (h l) -> p t h l", h=SSD_H)
        YT = HT
        MT = XC
        kvt = LM[:, 0, :, :].rearrange("p h l -> p (h l)").rearrange("p (t n) -> p t n", t=NT)
        KTm = LM[:, 1, 0:4, :].rearrange("p h l -> p (h l)").rearrange("p (t n) -> p t n", t=2)
        mq = LM[:, 1, 4:8, :].rearrange("p h l -> p (h l)").rearrange("p (t n) -> p t n", t=NT)
        mqT = st
        rt = [t[:, :, :].rearrange("p c s -> p (c s)")[:, i * RN:(i + 1) * RN]
              .rearrange("p (t h d) -> p t h d", t=NT, h=U_HEADS) for t in (qkT, qiT) for i in range(2)]
        oT = xdd[:, :].rearrange("p (t n) -> p t n", t=2)
        junk = rl[:, :, :, :].rearrange("p a b s -> p (a b s)")
        HTH, HTL = H_R[:, :, :].rearrange("p t n -> p (t n)").rearrange("p (k s) -> p k s", k=KT), HT_R
        sgd, atd, ahd, ald = (u[:, i // 2, (i % 2) * 2 * SEQ:(i % 2 + 1) * 2 * SEQ]
                              .rearrange("p (b j) -> p b j", b=2) for i, u in enumerate((U, U, U_R, U_R)))
        hcT = U[:, 0, 0:KT * BLOCK].rearrange("p (c j) -> p c j", c=KT)
        HTf = HT_R[:, :, :].rearrange("p k s -> p (k s)")
        hcH, hcL = (HTf[:, i * KT * BLOCK:(i + 1) * KT * BLOCK].rearrange("p (c j) -> p c j", c=KT)
                    for i in range(2))
        sg, at_ = (U[0:BLOCK, 1, i * 2 * P:(i + 1) * 2 * P].rearrange("p (b j) -> p b j", b=2) for i in range(2))
        aH, aL = (U_R[:, 1, 4 * P + i * 2 * BLOCK:4 * P + (i + 1) * 2 * BLOCK].rearrange("p (b j) -> p b j", b=2)
                  for i in range(2))
        yc = Z[0:BLOCK, :, :].rearrange("p t n -> p (t n)")
        PM = qiT[:, 0, 0:NT * BLOCK].rearrange("p (t j) -> p t j", t=NT)
        PG = qiT[:, 1, 0:NT * BLOCK].rearrange("p (t j) -> p t j", t=NT)
        PGT = qiT[0:BLOCK, 2, :].rearrange("p (t j) -> p t j", t=NT)

        ident = sb("ident", [P, P])
        tri = sb("tri", [P, P])
        tri_s = sb("tri_s", [P, P])
        ones = sb("ones", [P, P])
        neg_ssd = sb("neg_ssd", [P, P])
        neg_att = sb("neg_att", [P, P])
        iota_j = sb("iota_j", [P, P])
        cols = sb("cols", [P, N_COLS])
        rows = sb("rows", [P, N_ROWS])
        ffn_g2 = sb("ffn_g2", [P, DEPTH, KT])
        ffn_g = sb("ffn_g", [P, KT])
        wr = sb("wr", [P, KT, N_EXP])
        pos_i = sb("pos_i", [P, NT], I32)
        pos_f = sb("pos_f", [P, NT])
        ang = sb("ang", [P, NT, 8])
        kay = sb("kay", [P, NT, 8])
        cs_ = sb("cs_", [P, NT, 8])
        sn_ = sb("sn_", [P, NT, 8])
        inv = sb("inv", [P, 8])
        eps = sb("eps", [P, 1])
        one = sb("one", [P, 1])
        ss = sb("ss", [P, 32])
        rs = sb("rs", [P, 32])
        dts = sb("dts", [P, 6, NT, SSD_H])
        anum = sb("anum", [P, SSD_H])
        cum = sb("cum", [P, NT, 2, SSD_H])
        ecum = sb("ecum", [P, 2, SSD_H])
        m8 = sb("m8", [P, NT, 8])
        nmx = sb("nmx", [P, 4])
        psm = sb("psm", [P, 4])
        prs = sb("prs", [P, 4])
        rin = sb("rin", [P, NT, 16])
        tr = sb("tr", [P, NT, 8])
        mr = sb("mr", [P, NT, 16])
        rmask = sb("rmask", [P, NT, N_EXP])
        rel = sb("rel", [P, NT, N_EXP])
        rsc = sb("rsc", [P, 4, NT])
        gate = sb("gate", [P, NT, N_CAND])
        posm = sb("posm", [P, NT, N_CAND])
        cnt = sb("cnt", [P, 2, N_CAND])
        oh = sb("oh", [P, MAX_OVER, N_CAND])
        rtmp = sb("rtmp", [P, 5 * MAX_OVER, N_CAND])
        NB = N_EXP + MAX_OVER + 1
        BT = sb("BT", [P, NT, NB])
        GT = sb("GT", [P, NT, NB])
        tabf = sb("tabf", [P, 8])
        erow = sb("erow", [P, N_CAND])
        tabi = sb("tabi", [P, 8], I32)

        PA = [ctx.enter_context(nc.psum_tensor(f"PA{i}", [P, 512], F32)) for i in range(4)]
        PV = [ctx.enter_context(nc.psum_tensor(f"PV{i}", [P, 512], F32)) for i in range(4)]

        slot_full = [ctx.enter_context(nc.semaphore(f"slot_full{s}")) for s in range(WSLOTS)]
        slot_free = [ctx.enter_context(nc.semaphore(f"slot_free{s}")) for s in range(WSLOTS)]
        in_x = ctx.enter_context(nc.semaphore("in_x"))
        in_small = ctx.enter_context(nc.semaphore("in_small"))
        in_ffn = ctx.enter_context(nc.semaphore("in_ffn"))
        in_params = ctx.enter_context(nc.semaphore("in_params"))
        next_params = ctx.enter_context(nc.semaphore("next_params"))
        in_mem = ctx.enter_context(nc.semaphore("in_mem"))
        out_done = ctx.enter_context(nc.semaphore("out_done"))
        const_ready = ctx.enter_context(nc.semaphore("const_ready"))
        set_up = ctx.enter_context(nc.semaphore("set_up"))
        trig_step = ctx.enter_context(nc.semaphore("trig_step"))
        trig_act = ctx.enter_context(nc.semaphore("trig_act"))
        a_full, a_free = signal("a_full"), signal("a_free")
        v_full, v_free = signal("v_full"), signal("v_free")
        dve_step = signal("dve_step")
        act_step = signal("act_step")
        x_ready = signal("x_ready")
        rstd_ready = signal("rstd_ready")
        h_ready = signal("h_ready")
        xr_ready = signal("xr_ready")
        xbc_conv = signal("xbc_conv")
        xc_ready = signal("xc_ready")
        conv_acc = signal("conv_acc")
        conv_centred = signal("conv_centred")
        conv_rstd = signal("conv_rstd")
        conv_norm = signal("conv_norm")
        conv_aff = signal("conv_aff")
        conv_exp = signal("conv_exp")
        conv_out = signal("conv_out")
        qk_ss, qk_rstd = signal("qk_ss"), signal("qk_rstd")
        dt_in = signal("dt_in")
        dt_log = signal("dt_log")
        rope_ready = signal("rope_ready")
        a_ready = signal("a_ready")
        xdd_ready = signal("xdd_ready")
        cum_ready = signal("cum_ready")
        ecum_ready = signal("ecum_ready")
        m_ready = signal("m_ready")
        score_used = signal("score_used")
        att_ready = signal("att_ready")
        exp_ready = signal("exp_ready")
        p_ready = signal("p_ready")
        y_ss, y_rstd = signal("y_ss"), signal("y_rstd")
        y_ready = signal("y_ready")
        mem_rstd = signal("mem_rstd")
        mem_ready = signal("mem_ready")
        hn_ss, hn_rstd = signal("hn_ss"), signal("hn_rstd")
        hn_ready = signal("hn_ready")
        ffn_g_ready = signal("ffn_g_ready")
        router_full, router_step = signal("router_full", laps=N_MOE), signal("router_step", laps=N_MOE)
        router_read = signal("router_read", laps=N_MOE)
        mask_ready = signal("mask_ready", laps=N_MOE)
        top2_ready = signal("top2_ready", laps=N_MOE)
        top2_exp = signal("top2_exp", laps=N_MOE)
        table_ready = signal("table_ready", laps=N_MOE)
        gu_full = signal("gu_full")
        silu_ready = signal("silu_ready")
        act_ready = signal("act_ready", start=1)
        high_gu, low_gu = signal("high_gu"), signal("low_gu")
        high_d, low_d = signal("high_d"), signal("low_d")
        turned = signal("turned")
        act_high, act_low = signal("act_high"), signal("act_low")
        dense_added = signal("dense_added", laps=1)
        x_high, x_low = signal("x_high", laps=1), signal("x_low", laps=1)
        hc_high, hc_low = signal("hc_high"), signal("hc_low")
        pm_ready, pg_ready = signal("pm_ready"), signal("pg_ready")
        hc_full, hc_ready = signal("hc_full"), signal("hc_ready")
        pgt_full, pgt_ready = signal("pgt_full"), signal("pgt_ready", start=1)
        yc_ready = signal("yc_ready", start=1)
        sc_full, moe_added = signal("sc_full"), signal("moe_added")

        block = ctx.enter_context(nc.Block())

        released = {}

        def first_block(L):
            return L

        def params_ready(L):
            return (in_params, 32) if L == 0 else (next_params, 32 * L)

        def slot_loads(L, s, item=None, g=None, r=0):
            a_block = ROUNDS if s else 1
            if g is None:
                return L * (MIX_ITEMS // WSLOTS) + first_block(L) * a_block + item // WSLOTS
            return (L + 1) * (MIX_ITEMS // WSLOTS) + g * a_block + r

        def slot_of(t):
            return 0 if t == 0 else 1 + (t - 1) % LOOP_SLOTS

        def chunk_full(L, g, t):
            s = slot_of(t)
            return slot_full[s], (slot_loads(L, s, g=g, r=(t - 1) // LOOP_SLOTS if t else 0) + 1) * 16

        def chunk_done(g, t):
            if t < 0:
                g, t = g - 1, t + FT
            s = slot_of(t)
            return slot_free[s], chunk_reads(s, g, (t - 1) // LOOP_SLOTS if t else 0) + 1

        def chunk_reads(s, g, r=0):
            return 1 + g * (ROUNDS if s else 1) + r

        def pe_layer(pe, L):
            na, nv = [0], [0]

            def a_bank():
                na[0] += 1
                if na[0] > 4:
                    pe.wait_ge(*a_free(L, na[0] - 4))
                return PA[(na[0] - 1) % 4]

            def v_bank():
                nv[0] += 1
                if nv[0] > 4:
                    pe.wait_ge(*v_free(L, nv[0] - 4))
                return PV[(nv[0] - 1) % 4]

            def a_taken():
                pe.wait_ge(*a_free(L, na[0]))

            def arrived(item):
                s = item % WSLOTS
                pe.wait_ge(slot_full[s], (slot_loads(L, s, item=item) + 1) * 16)
                return W[:, s, :]

            def k_tiles(view, width, at=0):
                return view[:, at:at + KT * width].rearrange("p (k n) -> p k n", k=KT)

            def transposes(tiles, src):
                for at in range(0, len(tiles), 2):
                    bank = a_bank()
                    for j, tile in enumerate(tiles[at:at + 2]):
                        for tt in range(NT):
                            last = pe.transpose(bank[:, j * SEQ + tt * P:j * SEQ + (tt + 1) * P],
                                                src(tile, tt), ident[:, :])
                    last.then_inc(*a_full.up())

            def accumulate(dst, pairs):
                for i, (lhsT, rhs) in enumerate(pairs):
                    last = pe.matmul(dst, lhsT, rhs, start=(i == 0), stop=(i == len(pairs) - 1))
                return last

            def tokens_by(dst, act, view, tt):
                return accumulate(dst, [(act[:, k, tt * P:(tt + 1) * P], view[:, k, :]) for k in range(KT)])

            pe.wait_ge(*h_ready(L, NT))
            transposes(list(range(KT)), lambda c, tt: H[:, tt, c * P:(c + 1) * P])
            a_taken()
            for tile in range(12):
                item = tile // 3
                view = k_tiles(arrived(item), WIDE)
                if tile % 2 == 0:
                    bank = a_bank()
                f = (tile % 3) * P
                last = accumulate(bank[:, (tile % 2) * SEQ:(tile % 2 + 1) * SEQ],
                                  [(view[:, k, f:f + P], HT[:, k, :]) for k in range(KT)])
                if tile % 2:
                    last.then_inc(*a_full.up())
                released[item] = a_full, na[0]
            for item in range(4, 8):
                width = WIDE if item < 7 else U_N - 3 * WIDE
                view = k_tiles(arrived(item), width)
                for tt in range(NT):
                    tokens_by(a_bank()[:, 0:width], HT, view, tt).then_inc(*a_full.up())
                released[item] = a_full, na[0]
            pe.wait_ge(*conv_acc(L, 1))
            accumulate(v_bank()[:, 0:SEQ], [(ones[:, :], cacc[:, j, :]) for j in range(2)]).then_inc(*v_full.up())
            z0, z1 = k_tiles(arrived(8), WIDE), k_tiles(arrived(9), P)
            for tt in range(NT):
                bank = a_bank()
                tokens_by(bank[:, 0:WIDE], HT, z0, tt)
                tokens_by(bank[:, WIDE:512], HT, z1, tt).then_inc(*a_full.up())
            released[8] = a_full, na[0]
            pe.wait_ge(*conv_centred(L, 1))
            accumulate(a_bank()[:, 0:SEQ], [(ones[:, :], ctmp[:, j, :]) for j in range(2)]).then_inc(*a_full.up())
            pe.wait_ge(*xc_ready(L, 4))
            for tt in range(NT):
                bank = v_bank()
                for j in range(4):
                    last = pe.transpose(bank[:, j * P:(j + 1) * P], XC[:, j, tt * P:(tt + 1) * P], ident[:, :])
                last.then_inc(*v_full.up())
            bank = a_bank()
            for j in range(2):
                last = pe.transpose(bank[:, j * P:(j + 1) * P], XC[:, 4 + j, 0:P], ident[:, :])
            last.then_inc(*a_full.up())
            b_group = na[0]
            pe.wait_ge(*a_ready(L, 1))
            bank = v_bank()
            for tt in range(NT):
                pe.matmul(bank[:, tt * 16:tt * 16 + 8], tri[:, :], dts[:, 4, tt, :], start=True, stop=True)
                last = pe.matmul(bank[:, tt * 16 + 8:tt * 16 + 16], ones[:, :], dts[:, 4, tt, :],
                                 start=True, stop=True)
            last.then_inc(*v_full.up())
            pe.wait_ge(*a_ready(L, 2))
            for tt in range(NT):
                for half in range(2):
                    bank = a_bank()
                    hs = slice(half * 4, half * 4 + 4)
                    pe.matmul(bank[:, :], ones[:, :], TA[:, tt, hs, :], start=True, stop=False)
                    pe.matmul(bank[:, :], tri[:, :], dts[:, 5, tt, hs].unsqueeze(2).to_broadcast([P, 4, P]),
                              start=False, stop=False)
                    pe.matmul(bank[:, :], ident[:, :], neg_ssd[:, :].unsqueeze(1).to_broadcast([P, 4, P]),
                              start=False, stop=True).then_inc(*a_full.up())
            released["TA"] = a_full, na[0]
            bank = v_bank()
            for tt in range(NT):
                for g in range(2):
                    o = (tt * 2 + g) * P
                    last = pe.matmul(bank[:, o:o + P], XC[:, 4 + g, tt * P:(tt + 1) * P],
                                     XC[:, 6 + g, tt * P:(tt + 1) * P], start=True, stop=True)
            last.then_inc(*v_full.up())
            pe.wait_ge(*rope_ready(L, 1))
            transposes([0, 1, 2, 3], lambda c, tt: U[:, tt, U_QI + c * P:U_QI + (c + 1) * P])
            transposes([0], lambda c, tt: kk[:, tt, :])
            index_group = na[0]
            transposes([0, 1, 2, 3], lambda c, tt: U[:, tt, c * P:(c + 1) * P])
            pe.wait_ge(*a_free(L, index_group))
            for tt in range(NT):
                keys = P * (tt + 1)
                for pair in range(IDX_H // 2):
                    bank = a_bank()
                    r = slice(HD * (pair % 2), HD * (pair % 2) + HD)
                    for j in range(2):
                        last = pe.matmul(bank[:, j * SEQ:j * SEQ + keys],
                                         qiT[r, index_head(pair, j) // 2, tt * P:(tt + 1) * P],
                                         kiT[r, 0:keys], start=True, stop=True)
                    last.then_inc(*a_full.up())
            pe.wait_ge(*conv_out(L, 1))
            pw = W[:, 9 % WSLOTS, KT * P:KT * P + 2 * D_CONV].rearrange("p (k n) -> p k n", k=2)
            bank = a_bank()
            for j in range(2):
                last = accumulate(bank[:, j * SEQ:(j + 1) * SEQ],
                                  [(pw[:, k, j * P:(j + 1) * P], ctmp[:, k, :]) for k in range(2)])
            last.then_inc(*a_full.up())
            released[9] = a_full, na[0]
            pe.wait_ge(*xdd_ready(L, 1))
            pe.wait_ge(*a_free(L, b_group))
            bank = a_bank()
            for g in range(2):
                last = pe.matmul(bank[:, g * SEQ:(g + 1) * SEQ], btok[:, g, :], xdd[:, g * SEQ:(g + 1) * SEQ],
                                 start=True, stop=True)
            last.then_inc(*a_full.up())
            for tt in range(NT):
                pe.wait_ge(*m_ready(L, tt + 1))
                bank = v_bank()
                for h in range(SSD_H):
                    last = pe.matmul(bank[:, h * SSD_P:(h + 1) * SSD_P], LM[:, tt, h, :],
                                     xd[:, tt, h * SSD_P:(h + 1) * SSD_P], start=True, stop=True)
                last.then_inc(*v_full.up())
            a_taken()
            bank = v_bank()
            for g in range(2):
                last = pe.matmul(bank[:, g * SEQ:(g + 1) * SEQ], XC[:, 6 + g, P:2 * P], st[:, g, :],
                                 start=True, stop=True)
            last.then_inc(*v_full.up())
            pe.wait_ge(*mem_ready(L, NT))
            transposes(list(range(KT)), lambda c, tt: H[:, tt, c * P:(c + 1) * P])
            a_taken()
            kv0, kv1 = k_tiles(arrived(10), WIDE), k_tiles(arrived(11), P)
            for tt in range(NT):
                bank = a_bank()
                tokens_by(bank[:, 0:WIDE], MT, kv0, tt)
                tokens_by(bank[:, WIDE:512], MT, kv1, tt).then_inc(*a_full.up())
            released[10] = released[11] = a_full, na[0]

            def att_logits(tt, qT, kT, keys):
                for odd in range(2):
                    bank = v_bank()
                    r = slice(HD * odd, HD * odd + HD)
                    for j in range(2):
                        last = pe.matmul(bank[:, j * keys:(j + 1) * keys], qT[r, j, tt * P:(tt + 1) * P],
                                         kT[r, j, 0:keys], start=True, stop=True)
                    last.then_inc(*v_full.up())

            def p_transposes(tiles):
                for s in range(tiles):
                    bank = a_bank()
                    for h in range(4):
                        last = pe.transpose(bank[:, h * P:(h + 1) * P], prob[:, h, s * P:(s + 1) * P], ident[:, :])
                    last.then_inc(*a_full.up())

            def weighted_values(tiles, v):
                bank = a_bank()
                for h in range(4):
                    r = HD * (h % 2)
                    last = accumulate(bank[r:r + HD, (h // 2) * P:(h // 2 + 1) * P],
                                      [(v(s, h), pT[:, s, h, :]) for s in range(tiles)])
                last.then_inc(*a_full.up())

            for tt in range(NT):
                att_logits(tt, qkT[:, 0:2, :], qkT[:, 2:4, :], P * (tt + 1))
                pe.wait_ge(*p_ready(L, tt + 1))
                p_transposes(tt + 1)
                a_taken()
                weighted_values(tt + 1, lambda s, h: U[:, s, U_V + h * HD:U_V + (h + 1) * HD])
            pe.wait_ge(*hn_ready(L, 1))
            transposes([0, 1], lambda c, tt: kvt[:, tt, c * P:(c + 1) * P])
            pe.wait_ge(*y_ready(L, 1))
            transposes([0, 1, 2, 3], lambda c, tt: ysk[:, tt, c * P:(c + 1) * P])
            a_taken()
            for item in range(12, 15):
                width = WIDE if item < 14 else D_MODEL - 2 * WIDE
                view = k_tiles(arrived(item), width)
                for tt in range(NT):
                    tokens_by(v_bank()[:, 0:width], YT, view, tt).then_inc(*v_full.up())
                released[item] = v_full, nv[0]
            pe.wait_ge(*h_ready(L, 2 * NT))
            transposes(list(range(KT)), lambda c, tt: H[:, tt, c * P:(c + 1) * P])
            a_taken()
            wq = k_tiles(arrived(15), D_ATT)
            bank = a_bank()
            for tt in range(NT):
                last = tokens_by(bank[:, tt * D_ATT:(tt + 1) * D_ATT], HT, wq, tt)
            last.then_inc(*a_full.up())
            pe.wait_ge(*hn_ready(L, 2))
            transposes([0, 1], lambda c, tt: mq[:, tt, c * P:(c + 1) * P])
            a_taken()
            for tt in range(NT):
                att_logits(tt, mqT, KTm, SEQ)
                pe.wait_ge(*p_ready(L, NT + tt + 1))
                p_transposes(2)
                a_taken()
                weighted_values(2, lambda s, h: kvt[:, s, D_ATT + h * HD:D_ATT + (h + 1) * HD])
            a_taken()
            wo = [W[:, 14 % WSLOTS, KT * 256:KT * 256 + D_MODEL], W[:, 15 % WSLOTS, KT * 256:KT * 256 + D_MODEL]]
            for half in range(2):
                for tt in range(NT):
                    accumulate(v_bank()[:, :], [(oT[:, k, tt * P:(tt + 1) * P],
                                                 wo[k][:, half * 512:(half + 1) * 512])
                                                for k in range(2)]).then_inc(*v_full.up())
            released[14] = released[15] = v_full, nv[0]
            pe.wait_ge(*h_ready(L, 3 * NT))
            transposes(list(range(KT)), lambda c, tt: H[:, tt, c * P:(c + 1) * P])
            a_taken()
            pe.wait_ge(*v_free(L, nv[0]))
            if L % 2 == 0:
                pe_dense(pe, L)
            else:
                pe_moe(pe, L)

        GU = (PA[0], PA[1])

        def three_passes(pe, dst, a_high, a_low, b_high, b_low, start, stop):
            pe.matmul(dst, a_high, b_high, start=start, stop=False, skip_group_check=True)
            pe.matmul(dst, a_high, b_low, start=False, stop=False, skip_group_check=True)
            return pe.matmul(dst, a_low, b_high, start=False, stop=stop, skip_group_check=True)

        def gu_parts(t):
            return [w.rearrange("p (m k n) -> p m k n", m=2, k=KT)
                    for w in (WHgu[t % 2], W_R[:, slot_of(t), 0:GU_COLS])]

        def before_gate_up(pe, g, t):
            if t > 0 or not isinstance(g, int):
                pe.wait_ge(*act_ready(g, t - 1))
            pe.wait_ge(*low_gu(g, t + 1))

        def down(pe, g, t, sums, high, low):
            wh, wl = WHd[t % 2], W_R[:, slot_of(t), GU_COLS:SLOT]
            half = [slice((i % 2) * 512, (i % 2 + 1) * 512) for i in range(len(sums))]
            pe.wait_ge(*act_high(g, t + 1))
            pe.wait_ge(*low_d(g, t + 1))
            for i, bank in enumerate(sums):
                pe.matmul(bank, high(i), wh[:, half[i]], start=(t == 0), stop=False, skip_group_check=True)
                pe.matmul(bank, high(i), wl[:, half[i]], start=False, stop=False, skip_group_check=True)
            pe.wait_ge(*act_low(g, t + 1))
            for i, bank in enumerate(sums):
                last = pe.matmul(bank, low(i), wh[:, half[i]], start=False, stop=(t == FT - 1),
                                 skip_group_check=True)
            last.then_inc(slot_free[slot_of(t)], 1)

        def pe_dense(pe, L):
            g = first_block(L)
            sums = [b[:, :] for b in (PA[2], PA[3], PV[0], PV[1])]
            high, low = ([lambda i, t=t, a=a: a[:, t % 2, (i // 2) * P:(i // 2 + 1) * P] for t in range(FT)]
                         for a in (ahd, ald))
            pe.wait_ge(*x_low(0, 4))
            for t in range(FT):
                before_gate_up(pe, g, t)
                wh, wl = gu_parts(t)
                for m in range(2):
                    for k in range(KT):
                        last = three_passes(pe, GU[t % 2][:, m * SEQ:(m + 1) * SEQ], wh[:, m, k, :], wl[:, m, k, :],
                                            HTH[:, k, :], HTL[:, k, :], k == 0, k == KT - 1)
                last.then_inc(gu_full.sem, 1)
                if t:
                    down(pe, g, t - 1, sums, high[t - 1], low[t - 1])
            down(pe, g, FT - 1, sums, high[FT - 1], low[FT - 1])

        def pe_moe(pe, L):
            M = L // 2
            for tt in range(NT):
                for k in range(KT):
                    last = pe.matmul(PV[2][:, tt * N_EXP:(tt + 1) * N_EXP], HT[:, k, tt * P:(tt + 1) * P],
                                     wr[:, k, :], start=(k == 0), stop=(k == KT - 1))
            last.then_inc(*router_full.up())
            pe.wait_ge(*mask_ready(M, 1))
            for at, pairs in ((0, [(tri_s, 0)]), (8, [(tri_s, 1), (ones, 0)]), (16, [(ones, 0), (ones, 1)])):
                for i, (m, tt) in enumerate(pairs):
                    last = pe.matmul(PV[3][:, at:at + N_EXP], m[:, :], rmask[:, tt, :], start=(i == 0),
                                     stop=(i == len(pairs) - 1))
            last.then_inc(*router_full.up())
            pe.wait_ge(*table_ready(M, 1))
            more = pe.value_load(tabi[0:1, 0:1], min_val=1, max_val=MAX_OVER + 1)

            def gather(b):
                pe.wait_ge(*pm_ready(b, 1))
                for half in range(2):
                    for c in range(4):
                        k = half * 4 + c
                        for tt in range(NT):
                            last = pe.matmul(PV[half][:, c * BLOCK:(c + 1) * BLOCK], H[:, tt, k * P:(k + 1) * P],
                                             PM[:, tt, :], start=(tt == 0), stop=(tt == NT - 1))
                    last.then_inc(hc_full.sem, 1)

            def scatter(q, first):
                for tt in range(NT):
                    if first:
                        pe.wait_ge(*moe_added(q, tt + 1))
                    pe.matmul(PV[tt][:, :], PGT[:, tt, :], yc[:, first * 512:(first + 1) * 512],
                              start=True, stop=True).then_inc(sc_full.sem, 1)

            gather(0)
            with pe.Fori(0, N_EXP - 1 + more) as b:
                g = first_block(L) + b
                sums = [PA[2][0:BLOCK, :], PA[3][0:BLOCK, :]]

                def gate_up(t, half):
                    wh, wl = gu_parts(t)
                    for k in range(half * KT // 2, (half + 1) * KT // 2):
                        last = three_passes(pe, GU[t % 2][0:BLOCK, 0:2 * P], hcH[:, k, :],
                                            hcL[:, k, :], wh[:, :, k, :], wl[:, :, k, :],
                                            k == 0, k == KT - 1)
                    return last

                def turn(t):
                    pe.wait_ge(*act_ready(g, t + 1))
                    pe.transpose(PV[3][:, 0:BLOCK], at_[:, t % 2, :], ident[0:BLOCK, 0:BLOCK]) \
                        .then_inc(turned.sem, 1)

                pe.wait_ge(*hc_low(b, 1))
                for t in range(FT):
                    before_gate_up(pe, g, t)
                    gate_up(t, 0)
                    if t:
                        turn(t - 1)
                    gate_up(t, 1).then_inc(gu_full.sem, 1)
                    if t == 1:
                        pe.wait_ge(*yc_ready(b, 0))
                    if t:
                        down(pe, g, t - 1, sums, lambda i: aH[:, (t - 1) % 2, :],
                             lambda i: aL[:, (t - 1) % 2, :])
                    if t == 1:
                        pe.wait_ge(*pgt_ready(b, 0))
                        scatter(b, 0)
                    if t == 3:
                        scatter(b, 1)
                    if t == 5:
                        pe.wait_ge(*pg_ready(b, 1))
                        for tt in range(NT):
                            last = pe.transpose(PV[2][0:BLOCK, tt * P:(tt + 1) * P], PG[:, tt, :], ident[:, :])
                        last.then_inc(pgt_full.sem, 1)
                    if t == 6:
                        pe.wait_ge(*moe_added(b, 4))
                        gather(b + 1)
                turn(FT - 1)
                down(pe, g, FT - 1, sums, lambda i: aH[:, (FT - 1) % 2, :],
                     lambda i: aL[:, (FT - 1) % 2, :])
            pe.wait_ge(*yc_ready(N_EXP - 1 + more, 0))
            pe.wait_ge(*pgt_ready(N_EXP - 1 + more, 0))
            pe.wait_ge(*hc_ready(N_EXP - 1 + more, 2))
            for half in range(2):
                scatter(N_EXP - 1 + more, half)

        @block.tensor
        def _(pe):
            pe.wait_ge(const_ready, 2)
            pe.wait_ge(in_ffn, 32)
            for L in range(DEPTH):
                pe_layer(pe, L)

        @block.sync
        def _(sp):
            sp.dma_start(X[:, :, :], x_in.rearrange("a (t p) d -> p (a t) d", p=P)).then_inc(in_x, 16)

            def chunk(g, r, s, expert, after=None):
                if after is not None:
                    sp.wait_ge(*after)
                sp.wait_ge(slot_free[s], chunk_reads(s, g, r))
                sp.dma_start(W[:, s, :], wffn[bass.ds(expert * FT + r * LOOP_SLOTS + s, 1), :, :]
                             .rearrange("a p n -> p (a n)")).then_inc(slot_full[s], 16)

            def expert_chunks(g, expert, first_round=0):
                if not first_round:
                    chunk(g, 0, 0, expert)
                with sp.Fori(first_round, ROUNDS) as r:
                    for s in range(1, WSLOTS):
                        chunk(g, r, s, expert)

            for L in range(DEPTH):
                for item in range(MIX_ITEMS):
                    s = item % WSLOTS
                    if item >= WSLOTS:
                        done, k = released[item - WSLOTS]
                        sp.wait_ge(*done(L, k))
                    elif L:
                        sp.wait_ge(slot_free[s], chunk_reads(s, first_block(L)))
                    sp.dma_start(W[:, s, :], wmix[L * MIX_ITEMS + item]).then_inc(slot_full[s], 16)
                g0, moe = first_block(L), L % 2
                for s in range(WSLOTS):
                    done, k = released[WSLOTS + s]
                    chunk(g0, 0, s, moe, done(L, k))
                expert_chunks(g0, moe, 1)
                if moe:
                    with sp.Fori(1, N_EXP - 1) as b:
                        expert_chunks(g0 + b, b + 1)
                    sp.wait_ge(*table_ready(L // 2, 1))
                    more = sp.value_load(tabi[0:1, 0:1], min_val=1, max_val=MAX_OVER + 1)
                    with sp.Fori(0, more) as j:
                        expert = sp.value_load(tabi[0:1, bass.ds(j + 1, 1)], min_val=0, max_val=N_EXP)
                        expert_chunks(g0 + (N_EXP - 1) + j, expert)
            chunk(first_block(DEPTH - 1) + (N_EXP - 1) + more, 0, 0, 0)
            sp.wait_ge(*moe_added(N_EXP + more, 0))
            sp.dma_start(out.rearrange("a (t p) d -> p (a t) d", p=P), X[:, :, :]).then_inc(out_done, 16)
            sp.wait_ge(out_done, 16)

        @block.gpsimd
        def _(pool):
            for s in range(WSLOTS):
                nc.gpsimd.memset(ss[:, s:s + 1], 0.0).then_inc(slot_free[s], 1)
            nc.gpsimd.memset(ident[:, :], 0.0)
            nc.gpsimd.memset(tri[:, :], 1.0)
            nc.gpsimd.memset(tri_s[:, :], 1.0)
            nc.gpsimd.memset(ones[:, :], 1.0)
            nc.gpsimd.memset(neg_ssd[:, :], 0.0)
            nc.gpsimd.memset(neg_att[:, :], 0.0)
            nc.gpsimd.memset(hpad[:, :, :], 0.0)
            nc.gpsimd.memset(eps[:, :], EPS)
            nc.gpsimd.memset(one[:, :], 1.0).then_inc(const_ready, 1)
            pool.wait_ge(const_ready, 1)

            def cut(t, pattern, base, channel, op, fill):
                return nc.gpsimd.affine_select(out=t[:, :], in_=t[:, :], compare_op=op, fill=fill, base=base,
                                               pattern=pattern, channel_multiplier=channel)
            cut(ident, [[-1, P]], 0, 1, ALU.not_equal, 1.0)
            cut(tri, [[1, P]], 0, -1, ALU.is_ge, 0.0)
            cut(tri_s, [[1, P]], 0, -1, ALU.is_gt, 0.0)
            cut(neg_ssd, [[1, P]], 0, -1, ALU.is_ge, MASKED)
            cut(neg_att, [[-1, P]], 0, 1, ALU.is_ge, MASKED)
            nc.gpsimd.iota(iota_j[:, :], [[1, P]], base=0, channel_multiplier=0,
                           allow_small_or_imprecise_dtypes=True)
            nc.gpsimd.iota(erow[:, :], [[0, FURTHER], [1, N_EXP]], base=1, channel_multiplier=0,
                           allow_small_or_imprecise_dtypes=True).then_inc(const_ready, 1)
            for L in range(DEPTH):
                done, k = released["TA"]
                pool.wait_ge(*done(L, k))
                pool.dma_start(H[:, :, :], mem_in.rearrange("a (t p) d -> p (a t) d", p=P)).then_inc(in_mem, 16)
                if L + 1 < DEPTH:
                    pool.wait_ge(*x_ready(L, 2))
                    pool.dma_start(cols[:, :], cols_in[L + 1]).then_inc(next_params, 16)
                    pool.dma_start(rows[:, :], rows_in[L + 1:L + 2, :].to_broadcast([P, N_ROWS])) \
                        .then_inc(next_params, 16)

        def act_layer(act, L):
            act.wait_ge(*params_ready(L))
            na = [0]

            def step(ins):
                ins.then_inc(*act_step.up())
                act.wait_ge(*act_step(L, act_step.count(L)))

            def group():
                na[0] += 1
                act.wait_ge(*a_full(L, na[0]))
                return PA[(na[0] - 1) % 4]

            def col(name, at=0):
                return cols[:, COLS[name] + at:COLS[name] + at + 1]

            def copy(dst, src, scale=1.0):
                return act.activation(dst, src, ACT.Copy, scale=scale)

            def pair_of(bank):
                return bank[:, :].rearrange("p (j s) -> p j s", j=2)

            def copy_group(dst, src):
                copy(dst, src).then_inc(*a_free.up())

            def take_tiles(dst, tiles, gain):
                for at in range(0, tiles, 2):
                    bank = group()
                    for j in range(2):
                        last = copy(dst[:, at + j, :], bank[:, j * SEQ:(j + 1) * SEQ], gain(at + j))
                    last.then_inc(*a_free.up())

            def rstd(at, n, width, done):
                step(act.activation(rs[:, at:at + n], ss[:, at:at + n], ACT.Ln, bias=eps[:, :], scale=1.0 / width))
                act.activation(rs[:, at:at + n], rs[:, at:at + n], ACT.Exp, scale=-0.5).then_inc(*done.up())

            def squares(src, at):
                for tt in range(NT):
                    step(act.activation(junk, src[:, tt, :], ACT.Square, accum_out=ss[:, at + tt:at + tt + 1]))

            def softmax_exp(tt, keys, ready):
                act.wait_ge(*att_ready(L, ready))
                for h in range(4):
                    last = act.activation(prob[:, h, 0:keys], prob[:, h, 0:keys], ACT.Exp,
                                          bias=nmx[:, h:h + 1], accum_out=psm[:, h:h + 1])
                last.then_inc(*exp_ready.up())

            def take_p(tiles):
                for s in range(tiles):
                    copy_group(pT[:, s, :, :], group()[:, :].rearrange("p (h t) -> p h t", h=4))

            def take_o(dst, tt):
                copy_group(dst[:, :, tt * P:(tt + 1) * P], group()[:, 0:2 * P].rearrange("p (j t) -> p j t", j=2))

            if L == 0:
                act.wait_ge(in_x, 16)
            else:
                act.wait_ge(*dense_added(0, 4))
            squares(X, 0)
            rstd(0, NT, D_MODEL, rstd_ready)
            take_tiles(HT, KT, lambda k: col("mix_g", k))
            for at in range(0, KT, 2):
                copy_group(XR[:, at:at + 2, 3:3 + SEQ], pair_of(group()))
            copy_group(hpad[:, :, CONV_W - 1:], pair_of(group()))
            act.activation(ctmp[:, :, :], pair_of(group()), ACT.Exp, scale=-1.0).then_inc(*a_free.up())
            for item in range(4, 8):
                width = WIDE if item < 7 else U_N - 3 * WIDE
                c0 = (item - 4) * WIDE
                for tt in range(NT):
                    copy_group(U[:, tt, c0:c0 + width], group()[:, 0:width])
            for at in range(0, KT, 2):
                act.wait_ge(*xbc_conv(L, at // 2 + 1))
                act.activation(XC[:, at:at + 2, :], XC[:, at:at + 2, :], ACT.Silu).then_inc(*xc_ready.up())
            for tt in range(NT):
                act.activation(Z[:, tt, :], group()[:, :], ACT.Silu).then_inc(*a_free.up())
            act.wait_ge(*dt_in(L, 1))
            step(act.activation(dts[:, 2, :, :], dts[:, 1, :, :], ACT.Exp, scale=-1.0))
            act.activation(anum[:, :], rows[:, R_ALOG:R_ALOG + SSD_H], ACT.Exp)
            act.activation(dts[:, 2, :, :], dts[:, 2, :, :], ACT.Ln, bias=one[:, :]).then_inc(*dt_log.up())
            act.wait_ge(*qk_ss(L, 1))
            rstd(2, 16, HD, qk_rstd)
            bank = group()
            act.activation(ctmp[:, 0, :], bank[:, 0:SEQ], ACT.Ln, bias=eps[:, :], scale=1.0 / D_CONV) \
                .then_inc(*a_free.up())
            act.wait_ge(*a_free(L, na[0]))
            act.activation(ctmp[:, 0, :], ctmp[:, 0, :], ACT.Exp, scale=-0.5).then_inc(*conv_rstd.up())
            copy_group(btok[:, :, :], group()[:, 0:2 * P].rearrange("p (g n) -> p g n", g=2))
            act.wait_ge(*cum_ready(L, 1))
            act.activation(ecum[:, :, :], ecum[:, :, :], ACT.Exp).then_inc(*ecum_ready.up())
            for tt in range(NT):
                for half in range(2):
                    act.activation(LM[:, tt, half * 4:half * 4 + 4, :],
                                   group()[:, :].rearrange("p (h l) -> p h l", h=4), ACT.Exp) \
                        .then_inc(*a_free.up())
            for at in (0, 2):
                copy_group(qiT[:, at:at + 2, :], pair_of(group()))
            copy_group(kiT[:, :], group()[:, 0:SEQ])
            for at in (0, 2):
                copy_group(qkT[:, at:at + 2, :], pair_of(group()))
            act.wait_ge(*conv_norm(L, 1))
            act.activation(ctmp[:, :, :], cacc[:, :, :], ACT.Exp, scale=-1.0).then_inc(*conv_exp.up())
            for n in range(NT * IDX_H // 2):
                keys = P * (n // (IDX_H // 2) + 1)
                bank = group()
                if n >= 2:
                    act.wait_ge(*score_used(L, n - 1))
                act.activation(rl[:, n % 2, :, 0:keys], pair_of(bank)[:, :, 0:keys], ACT.Relu) \
                    .then_inc(*a_free.up())
            copy_group(YT[:, 0:2, :], pair_of(group()))
            copy_group(st[:, :, :], pair_of(group()))
            act.wait_ge(in_mem, 16 * (L + 1))
            act.wait_ge(*score_used(L, NT * IDX_H // 2))
            squares(H, 18)
            rstd(18, NT, D_MODEL, mem_rstd)
            take_tiles(MT, KT, lambda k: col("mem_g", k))
            for tt in range(NT):
                copy_group(kvt[:, tt, :], group()[:, :])
            for tt in range(NT):
                softmax_exp(tt, P * (tt + 1), tt + 1)
                take_p(tt + 1)
                take_o(YT[:, 6:8, :], tt)
            act.wait_ge(*hn_ss(L, 1))
            rstd(20, NT * MEM_H, HD, hn_rstd)
            bank = group()
            copy(KTm[:, :, :], pair_of(bank), col("mk_g")).then_inc(*a_free.up())
            act.wait_ge(*y_ss(L, 1))
            rstd(28, 4, D_SSD // 2, y_rstd)
            take_tiles(YT[:, 2:6, :], 4, lambda c: col("ssd_g", c))
            act.wait_ge(*x_ready(L, 1))
            squares(X, 0)
            rstd(0, NT, D_MODEL, rstd_ready)
            take_tiles(HT, KT, lambda k: col("memx_g", k))
            copy_group(mq[:, :, :], pair_of(group()))
            act.wait_ge(*hn_ss(L, 2))
            rstd(20, NT * MEM_H, HD, hn_rstd)
            bank = group()
            copy(mqT[:, :, :], pair_of(bank), col("mq_g")).then_inc(*a_free.up())
            for tt in range(NT):
                softmax_exp(tt, SEQ, NT + tt + 1)
                take_p(2)
                take_o(oT, tt)
            act.wait_ge(*x_ready(L, 2))
            squares(X, 0)
            rstd(0, NT, D_MODEL, rstd_ready)
            act.wait_ge(*ffn_g_ready(L, 1))
            take_tiles(HT, KT, lambda k: ffn_g[:, k:k + 1])

            def silu(g, t, n, dst):
                act.wait_ge(*gu_full(g, t + 1))
                act.activation(dst[:, t % 2, :], GU[t % 2][0:dst.shape[0], 0:n], ACT.Silu) \
                    .then_inc(silu_ready.sem, 1)

            def round_gu(g, t):
                if t == FT:
                    g, t = g + 1, 0
                if t >= 2 or not isinstance(g, int):
                    act.wait_ge(*gu_full(g, t - 1))
                act.wait_ge(*chunk_full(L, g, t))
                copy(WHgu[t % 2], W[:, slot_of(t), 0:GU_COLS]).then_inc(high_gu.sem, 1)

            def round_d(g, t):
                if t >= 2 or not isinstance(g, int):
                    act.wait_ge(*chunk_done(g, t - 2))
                copy(WHd[t % 2], W[:, slot_of(t), GU_COLS:SLOT]).then_inc(high_d.sem, 1)

            if L % 2 == 0:
                g = first_block(L)
                for i in range(4):
                    ks = slice(i * 2, i * 2 + 2)
                    if i == 0:
                        act.wait_ge(*a_free(L, na[0]))
                    copy(HTH[:, ks, :], HT[:, ks, :]).then_inc(*x_high.up())

                def act_parts(t):
                    act.wait_ge(*act_ready(g, t + 1))
                    copy(ahd[:, t % 2, :], atd[:, t % 2, :]).then_inc(act_high.sem, 1)

                round_gu(g, 0)
                for t in range(FT):
                    if t:
                        silu(g, t - 1, SEQ, sgd)
                    if t < FT - 1:
                        round_gu(g, t + 1)
                    if t:
                        act_parts(t - 1)
                    round_d(g, t)
                silu(g, FT - 1, SEQ, sgd)
                act_parts(FT - 1)
                return
            M = L // 2
            act.wait_ge(*top2_ready(M, 1))
            act.activation(rsc[:, 1, :], rsc[:, 0, :], ACT.Exp)
            act.activation(rel[:, :, :], rel[:, :, :], ACT.Exp).then_inc(*top2_exp.up())
            round_gu(first_block(L), 0)
            act.wait_ge(*table_ready(M, 1))
            more = act.value_load(tabi[0:1, 0:1], min_val=1, max_val=MAX_OVER + 1)

            def tokens_high(b):
                act.wait_ge(*hc_ready(b, 2))
                copy(hcH[:, :, :], hcT[:, :, :]).then_inc(hc_high.sem, 1)

            tokens_high(0)
            with act.Fori(0, N_EXP - 1 + more) as b:
                g = first_block(L) + b

                def act_parts(t):
                    act.wait_ge(*turned(b, t + 1))
                    copy(aH[:, t % 2, :], PV[3][:, 0:BLOCK]).then_inc(act_high.sem, 1)

                for t in range(FT):
                    if t:
                        silu(g, t - 1, P, sg)
                    round_gu(g, t + 1)
                    if t:
                        act_parts(t - 1)
                    round_d(g, t)
                    if t == 6:
                        act.wait_ge(*pgt_full(b, 1))
                        copy(PGT[:, :, :], PV[2][0:BLOCK, 0:NT * P].rearrange("p (t j) -> p t j", t=NT)) \
                            .then_inc(pgt_ready.sem, 1)
                silu(g, FT - 1, P, sg)
                tokens_high(b + 1)
                act_parts(FT - 1)
                act.wait_ge(*chunk_done(g, FT - 1))
                copy(yc[:, 0:512], PA[2][0:BLOCK, :])
                copy(yc[:, 512:1024], PA[3][0:BLOCK, :]).then_inc(yc_ready.sem, 1)

        @block.scalar
        def _(act):
            act.dma_start(pos_i[:, :], pos_in).then_inc(in_small, 16)
            act.dma_start(cols[:, :], cols_in[0]).then_inc(in_params, 16)
            act.dma_start(rows[:, :], rows_in[0:1, :].to_broadcast([P, N_ROWS])).then_inc(in_params, 16)
            act.dma_start(ffn_g2[:, :, :], ffn_g_in).then_inc(in_ffn, 16)
            act.dma_start(wr[:, :, :], router_in).then_inc(in_ffn, 16)
            act.wait_ge(const_ready, 2)
            act.wait_ge(in_small, 16)
            act.wait_ge(trig_step, 1 + NT + 2 + len(TURN_PARTS))
            nc.scalar.activation(sn_[:, :, :], ang[:, :, :], ACT.Sin)
            nc.scalar.activation(kay[:, :, :], ang[:, :, :], ACT.Sin, scale=0.5).then_inc(trig_act, 1)
            for L in range(DEPTH):
                act_layer(act, L)

        def dve_layer(dve, L):
            dve.wait_ge(*params_ready(L))
            nv = [0]
            v = nc.vector

            def step(ins):
                ins.then_inc(*dve_step.up())
                dve.wait_ge(*dve_step(L, dve_step.count(L)))

            def note(ins):
                ins.then_inc(*dve_step.up())

            def group():
                nv[0] += 1
                dve.wait_ge(*v_full(L, nv[0]))
                return PV[(nv[0] - 1) % 4]

            def col(name, at=0, n=1):
                return cols[:, COLS[name] + at:COLS[name] + at + n]

            def along(ap, n):
                return ap.unsqueeze(len(ap.shape)).to_broadcast(list(ap.shape) + [n])

            def normalise(ready):
                dve.wait_ge(*rstd_ready(L, ready))
                for tt in range(NT):
                    v.tensor_scalar(H[:, tt, :], X[:, tt, :], rs[:, tt:tt + 1], None, ALU.mult) \
                        .then_inc(*h_ready.up())

            def head_squares(src, width, at, done):
                n = src.shape[2]
                tmp = prob[:, :, :].rearrange("p h s -> p (h s)")[:, 0:NT * n].rearrange("p (t n) -> p t n", t=NT)
                step(v.tensor_tensor(tmp, src, src, ALU.mult))
                v.tensor_reduce(ss[:, at:at + NT * n // width], tmp.rearrange("p t (h d) -> p (t h) d", d=width),
                                AX_X, ALU.add).then_inc(*done.up())

            def softmax_in(tt, keys, bias):
                for odd in range(2):
                    bank = group()
                    src = bank[:, 0:2 * keys].rearrange("p (h s) -> p h s", h=2)
                    dst = prob[:, :, :].rearrange("p (h o) s -> p o h s", o=2)[:, odd, :, 0:keys]
                    if bias is None:
                        v.tensor_scalar(dst, src, HD ** -0.5, None, ALU.mult).then_inc(*v_free.up())
                    else:
                        v.scalar_tensor_tensor(out=dst, in0=src, scalar=HD ** -0.5,
                                               in1=bias[:, 0:keys].unsqueeze(1).to_broadcast([P, 2, keys]),
                                               op0=ALU.mult, op1=ALU.add).then_inc(*v_free.up())
                dve.wait_ge(*v_free(L, nv[0]))
                v.tensor_reduce(nmx[:, :], prob[:, :, 0:keys], AX_X, ALU.max, negate=True).then_inc(*att_ready.up())

            def softmax_out(tt, keys, ready):
                dve.wait_ge(*exp_ready(L, ready))
                step(v.reciprocal(prs[:, :], psm[:, :]))
                v.tensor_tensor(prob[:, :, 0:keys], prob[:, :, 0:keys], along(prs[:, :], keys), ALU.mult) \
                    .then_inc(*p_ready.up())

            normalise(1)
            note(v.memset(XR[:, :, 0:3], 0.0))
            dve.wait_ge(*dve_step(L, dve_step.count(L)))
            for tile in range(KT):
                if tile % 2 == 0:
                    dve.wait_ge(*a_free(L, 4 + tile // 2 + 1))
            for at in range(0, KT, 2):
                for tap in range(SSD_CONV):
                    for tile in (at, at + 1):
                        w = col("ssd_w", tile * SSD_CONV + tap)
                        x = XR[:, tile, tap:tap + SEQ]
                        if tap == 0:
                            ins = v.tensor_scalar(XC[:, tile, :], x, w, col("ssd_b", tile), ALU.mult, ALU.add)
                        else:
                            ins = v.scalar_tensor_tensor(out=XC[:, tile, :], in0=x, scalar=w, in1=XC[:, tile, :],
                                                         op0=ALU.mult, op1=ALU.add)
                        if tap == SSD_CONV - 1 and tile % 2:
                            ins.then_inc(*xbc_conv.up())
                        else:
                            note(ins)
                    if tap < SSD_CONV - 1:
                        dve.wait_ge(*dve_step(L, dve_step.count(L)))
            dve.wait_ge(*a_free(L, 10))
            step(v.tensor_scalar(ctmp[:, :, :], ctmp[:, :, :], 1.0, None, ALU.add))
            step(v.reciprocal(ctmp[:, :, :], ctmp[:, :, :]))
            step(v.tensor_tensor(hpad[:, :, CONV_W - 1:], hpad[:, :, CONV_W - 1:], ctmp[:, :, :], ALU.mult))
            for tap in range(CONV_W):
                for j in range(2):
                    w = col("conv_w", j * CONV_W + tap)
                    x = hpad[:, j, tap:tap + SEQ]
                    if tap == 0:
                        ins = v.tensor_scalar(cacc[:, j, :], x, w, None, ALU.mult)
                    else:
                        dve.wait_ge(*dve_step(L, dve_step.count(L) - 1))
                        ins = v.scalar_tensor_tensor(out=cacc[:, j, :], in0=x, scalar=w, in1=cacc[:, j, :],
                                                     op0=ALU.mult, op1=ALU.add)
                    if tap == CONV_W - 1 and j == 1:
                        ins.then_inc(*conv_acc.up())
                    else:
                        note(ins)
            dve.wait_ge(*conv_acc(L, 1))
            bank = group()
            v.scalar_tensor_tensor(out=cacc[:, :, :], in0=bank[:, 0:SEQ].unsqueeze(1).to_broadcast([P, 2, SEQ]),
                                   scalar=-1.0 / D_CONV, in1=cacc[:, :, :], op0=ALU.mult, op1=ALU.add) \
                .then_inc(*v_free.up())
            dve.wait_ge(*v_free(L, nv[0]))
            v.tensor_tensor(ctmp[:, :, :], cacc[:, :, :], cacc[:, :, :], ALU.mult).then_inc(*conv_centred.up())
            dve.wait_ge(*a_free(L, 18))
            for tt in range(NT):
                step(v.tensor_tensor(dts[:, 0, tt, :], U[:, tt, U_DT:U_DT + SSD_H], rows[:, R_DTB:R_DTB + SSD_H],
                                     ALU.add))
            v.scalar_tensor_tensor(out=dts[:, 1, :, :], in0=dts[:, 0, :, :], scalar=-1.0, in1=dts[:, 0, :, :],
                                   op0=ALU.mult, op1=ALU.max).then_inc(*dt_in.up())
            head_squares(U[:, :, 0:2 * D_ATT], HD, 2, qk_ss)
            dve.wait_ge(*dt_log(L, 1))
            step(v.scalar_tensor_tensor(out=dts[:, 3, :, :], in0=dts[:, 0, :, :], scalar=0.0, in1=dts[:, 2, :, :],
                                        op0=ALU.max, op1=ALU.add))
            an = anum[:, :].unsqueeze(1).to_broadcast([P, NT, SSD_H])
            step(v.tensor_tensor(dts[:, 5, :, :], dts[:, 3, :, :], an, ALU.mult))
            v.tensor_scalar(dts[:, 4, :, :], dts[:, 5, :, :], -1.0, None, ALU.mult).then_inc(*a_ready.up())
            dve.wait_ge(*a_ready(L, 1))
            for tt in range(NT):
                ins = v.tensor_tensor(TA[:, tt, :, :], tri[:, :].unsqueeze(1).to_broadcast([P, SSD_H, P]),
                                      along(dts[:, 4, tt, :], P), ALU.mult)
            ins.then_inc(*a_ready.up())
            for tt in range(NT):
                bank = group()
                src = bank[:, :].rearrange("p (h d) -> p h d", h=SSD_H)
                note(v.tensor_tensor(xd[:, tt, :].rearrange("p (h d) -> p h d", h=SSD_H), src,
                                     along(dts[:, 3, tt, :], SSD_P), ALU.mult))
                v.tensor_tensor(ysk[:, tt, :].rearrange("p (h d) -> p h d", h=SSD_H), src,
                                along(rows[:, R_D:R_D + SSD_H], SSD_P), ALU.mult).then_inc(*v_free.up())
            bank = group()
            v.tensor_copy(cum[:, :, :, :], bank[:, 0:32].rearrange("p (t k h) -> p t k h", t=NT, k=2)) \
                .then_inc(*v_free.up())
            dve.wait_ge(*v_free(L, nv[0]))
            note(v.tensor_tensor(ecum[:, 0, :], cum[:, 0, 1, :], cum[:, 0, 0, :], ALU.subtract))
            v.tensor_copy(ecum[:, 1, :], cum[:, 1, 0, :]).then_inc(*cum_ready.up())
            dve.wait_ge(*qk_rstd(L, 1))
            qk = U[:, :, 0:2 * D_ATT]
            for tt in range(NT):
                step(v.tensor_tensor(qk[:, tt, :].rearrange("p (h d) -> p h d", d=HD),
                                     qk[:, tt, :].rearrange("p (h d) -> p h d", d=HD),
                                     along(rs[:, 2 + tt * 8:10 + tt * 8], HD), ALU.mult))
                gains = rows[:, R_QK:R_QK + 2 * HD].rearrange("p (m d) -> p m d", m=2).unsqueeze(2) \
                    .to_broadcast([P, 2, ATT_H, HD])
                step(v.tensor_tensor(qk[:, tt, :].rearrange("p (m h d) -> p m h d", m=2, d=HD),
                                     qk[:, tt, :].rearrange("p (m h d) -> p m h d", m=2, d=HD), gains, ALU.mult))
            heads = U[:, :, 0:U_HEADS * HD].rearrange("p t (h d) -> p t h d", d=HD)
            x1, x2 = heads[:, :, :, 0:8], heads[:, :, :, 8:16]
            c_, s_ = (t[:, :, :].unsqueeze(2).to_broadcast([P, NT, U_HEADS, 8]) for t in (cs_, sn_))
            for i, (x, y) in enumerate(((x1, c_), (x2, s_), (x2, c_), (x1, s_))):
                note(v.tensor_tensor(rt[i][:, :, :, :], x, y, ALU.mult))
            dve.wait_ge(*dve_step(L, dve_step.count(L)))
            for lo, hi in ((0, 2 * ATT_H), (3 * ATT_H, U_HEADS)):
                note(v.tensor_tensor(x1[:, :, lo:hi, :], rt[0][:, :, lo:hi, :], rt[1][:, :, lo:hi, :], ALU.subtract))
                note(v.tensor_tensor(x2[:, :, lo:hi, :], rt[2][:, :, lo:hi, :], rt[3][:, :, lo:hi, :], ALU.add))
            dve.wait_ge(*dve_step(L, dve_step.count(L)))
            note(v.tensor_scalar(U[:, :, U_W:U_W + IDX_H], U[:, :, U_W:U_W + IDX_H],
                                 IDX_H ** -0.5 * HD ** -0.5, None, ALU.mult))
            for j in range(2):
                ins = v.tensor_copy(kk[:, :, j * HD:(j + 1) * HD], U[:, :, U_KI:U_KI + HD])
            ins.then_inc(*rope_ready.up())
            dve.wait_ge(*conv_rstd(L, 1))
            step(v.tensor_tensor(cacc[:, :, :], cacc[:, :, :], ctmp[:, 0, :].unsqueeze(1).to_broadcast([P, 2, SEQ]),
                                 ALU.mult))
            for j in range(2):
                ins = v.tensor_scalar(cacc[:, j, :], cacc[:, j, :], col("ln_g", j), col("ln_b", j),
                                      ALU.mult, ALU.add)
            ins.then_inc(*conv_norm.up())
            dve.wait_ge(*ecum_ready(L, 1))
            v.tensor_tensor(xdd[:, :].rearrange("p (h d) -> p h d", h=SSD_H),
                            xd[:, 0, :].rearrange("p (h d) -> p h d", h=SSD_H), along(ecum[:, 0, :], SSD_P),
                            ALU.mult).then_inc(*xdd_ready.up())
            bank = group()
            dve.wait_ge(*a_free(L, A_SEG))
            for tt in range(NT):
                cb = bank[:, tt * 2 * P:(tt + 1) * 2 * P].rearrange("p (g l) -> p g l", g=2).unsqueeze(2) \
                    .to_broadcast([P, 2, 4, P])
                lm = LM[:, tt, :, :].rearrange("p (g h) l -> p g h l", g=2)
                v.tensor_tensor(lm, lm, cb, ALU.mult).then_inc(*m_ready.up())
            dve.wait_ge(*m_ready(L, NT))
            v.tensor_copy(m8[:, 0, 0:1], one[:, :]).then_inc(*v_free.up())
            dve.wait_ge(*conv_exp(L, 1))
            step(v.tensor_scalar(ctmp[:, :, :], ctmp[:, :, :], 1.0, None, ALU.add))
            step(v.reciprocal(ctmp[:, :, :], ctmp[:, :, :]))
            v.tensor_tensor(ctmp[:, :, :], ctmp[:, :, :], cacc[:, :, :], ALU.mult).then_inc(*conv_out.up())
            n = 0
            for tt in range(NT):
                keys = P * (tt + 1)
                for pair in range(IDX_H // 2):
                    n += 1
                    dve.wait_ge(*a_free(L, A_INDEX + n))
                    for j in range(2):
                        h = index_head(pair, j)
                        w = U[:, tt, U_W + h:U_W + h + 1]
                        x, s = rl[:, (n - 1) % 2, j, 0:keys], score[:, tt, 0:keys]
                        if h == 0:
                            step(v.tensor_scalar(s, x, w, None, ALU.mult))
                        elif j == 0:
                            step(v.scalar_tensor_tensor(out=s, in0=x, scalar=w, in1=s, op0=ALU.mult, op1=ALU.add))
                        else:
                            v.scalar_tensor_tensor(out=s, in0=x, scalar=w, in1=s, op0=ALU.mult, op1=ALU.add) \
                                .then_inc(*score_used.up())
                            dve.wait_ge(*score_used(L, n))
            dve.wait_ge(*mem_rstd(L, 1))
            for tt in range(NT):
                v.tensor_scalar(H[:, tt, :], H[:, tt, :], rs[:, 18 + tt:19 + tt], None, ALU.mult) \
                    .then_inc(*mem_ready.up())
            for tt in range(NT):
                d = slice(tt * P, (tt + 1) * P)
                note(v.tensor_tensor(score[:, tt, d], score[:, tt, d], neg_att[:, :], ALU.add))
            for i in range(TOPK // 8):
                dve.wait_ge(*dve_step(L, dve_step.count(L)))
                for tt in range(NT):
                    note(v.max(m8[:, tt, :], score[:, tt, 0:P * (tt + 1)]))
                dve.wait_ge(*dve_step(L, dve_step.count(L)))
                for tt in range(NT):
                    s = score[:, tt, 0:P * (tt + 1)]
                    note(v.match_replace(s, m8[:, tt, :], s, TAKEN))
            dve.wait_ge(*dve_step(L, dve_step.count(L)))
            for tt in range(NT):
                keys = P * (tt + 1)
                note(v.tensor_scalar(abias[:, tt, 0:keys], score[:, tt, 0:keys], TAKEN, MASKED,
                                     ALU.not_equal, ALU.mult))
            dve.wait_ge(*dve_step(L, dve_step.count(L)))
            for tt in range(NT):
                d = slice(tt * P, (tt + 1) * P)
                note(v.tensor_tensor(abias[:, tt, d], abias[:, tt, d], neg_att[:, :], ALU.add))
            for tt in range(NT):
                bank = group()
                v.tensor_tensor(ysk[:, tt, :], ysk[:, tt, :], bank[:, :], ALU.add).then_inc(*v_free.up())
            bank = group()
            v.tensor_tensor(xd[:, 1, :].rearrange("p (h d) -> p h d", h=SSD_H),
                            bank[:, :].rearrange("p (h d) -> p h d", h=SSD_H), along(ecum[:, 1, :], SSD_P),
                            ALU.mult).then_inc(*v_free.up())
            dve.wait_ge(*v_free(L, nv[0]))
            step(v.tensor_tensor(ysk[:, 1, :], ysk[:, 1, :], xd[:, 1, :], ALU.add))
            step(v.tensor_tensor(ysk[:, :, :], ysk[:, :, :], Z[:, :, :], ALU.mult))
            head_squares(ysk[:, :, :], D_SSD // 2, 28, y_ss)
            dve.wait_ge(*a_free(L, A_KV))
            dve.wait_ge(*y_ss(L, 1))
            head_squares(kvt[:, :, 0:D_ATT], HD, 20, hn_ss)
            dve.wait_ge(*hn_ss(L, 1))
            for tt in range(NT):
                keys = P * (tt + 1)
                softmax_in(tt, keys, abias[:, tt, :])
                softmax_out(tt, keys, tt + 1)
                if tt + 1 < NT:
                    dve.wait_ge(*v_full(L, nv[0] + 1))
            dve.wait_ge(*hn_rstd(L, 1))
            kh = kvt[:, :, 0:D_ATT].rearrange("p t (h d) -> p t h d", d=HD)
            v.tensor_tensor(kh, kh, along(rs[:, 20:28].rearrange("p (t h) -> p t h", t=NT), HD), ALU.mult) \
                .then_inc(*hn_ready.up())
            dve.wait_ge(*y_rstd(L, 1))
            yh = ysk[:, :, :].rearrange("p t (g d) -> p t g d", g=2)
            v.tensor_tensor(yh, yh, along(rs[:, 28:32].rearrange("p (t g) -> p t g", t=NT), SEQ), ALU.mult) \
                .then_inc(*y_ready.up())
            for item in range(12, 15):
                c0 = (item - 12) * WIDE
                width = min(WIDE, D_MODEL - c0)
                for tt in range(NT):
                    bank = group()
                    x = X[:, tt, c0:c0 + width]
                    v.tensor_tensor(x, x, bank[:, 0:width], ALU.add).then_inc(*v_free.up())
            dve.wait_ge(*v_free(L, nv[0]))
            v.tensor_copy(ffn_g[:, :], ffn_g2[:, L, :]).then_inc(*x_ready.up())
            normalise(2)
            dve.wait_ge(*a_free(L, A_MQ))
            head_squares(mq[:, :, :], HD, 20, hn_ss)
            dve.wait_ge(*hn_rstd(L, 2))
            qh = mq[:, :, :].rearrange("p t (h d) -> p t h d", d=HD)
            v.tensor_tensor(qh, qh, along(rs[:, 20:28].rearrange("p (t h) -> p t h", t=NT), HD), ALU.mult) \
                .then_inc(*hn_ready.up())
            for tt in range(NT):
                softmax_in(tt, SEQ, None)
                softmax_out(tt, SEQ, NT + tt + 1)
                if tt + 1 < NT:
                    dve.wait_ge(*v_full(L, nv[0] + 1))
            for half in range(2):
                for tt in range(NT):
                    bank = group()
                    x = X[:, tt, half * 512:(half + 1) * 512]
                    v.tensor_tensor(x, x, bank[:, :], ALU.add).then_inc(*v_free.up())
            dve.wait_ge(*v_free(L, nv[0]))
            v.tensor_copy(m8[:, 0, 0:1], one[:, :]).then_inc(*x_ready.up())
            normalise(3)
            v.tensor_copy(m8[:, 0, 1:2], one[:, :]).then_inc(*ffn_g_ready.up())

            def activate(g, t, n, src, dst):
                i = t % 2
                dve.wait_ge(*silu_ready(g, t + 1))
                v.tensor_tensor(dst[:, i, :], src[:, i, :], GU[i][0:dst.shape[0], n:2 * n], ALU.mult) \
                    .then_inc(act_ready.sem, 1)

            def less(dst, whole, high):
                return v.tensor_tensor(dst, whole, high, ALU.subtract)

            def rest_gu(g, t):
                if t == FT:
                    g, t = g + 1, 0
                w, low = (x[:, slot_of(t), 0:GU_COLS] for x in (W, W_R))
                dve.wait_ge(*high_gu(g, t + 1))
                less(low, w, WHgu[t % 2]).then_inc(low_gu.sem, 1)

            def rest_d(g, t):
                w, low = (x[:, slot_of(t), GU_COLS:SLOT] for x in (W, W_R))
                dve.wait_ge(*high_d(g, t + 1))
                less(low, w, WHd[t % 2]).then_inc(low_d.sem, 1)

            if L % 2 == 0:
                g = first_block(L)
                for i in range(4):
                    ks = slice(i * 2, i * 2 + 2)
                    dve.wait_ge(*x_high(0, i + 1))
                    less(HTL[:, ks, :], HT[:, ks, :], HTH[:, ks, :]).then_inc(*x_low.up())

                def act_rest(t):
                    dve.wait_ge(*act_high(g, t + 1))
                    less(ald[:, t % 2, :], atd[:, t % 2, :], ahd[:, t % 2, :]) \
                        .then_inc(act_low.sem, 1)

                rest_gu(g, 0)
                for t in range(FT):
                    if t:
                        activate(g, t - 1, SEQ, sgd, atd)
                    if t < FT - 1:
                        rest_gu(g, t + 1)
                    if t:
                        act_rest(t - 1)
                    rest_d(g, t)
                activate(g, FT - 1, SEQ, sgd, atd)
                act_rest(FT - 1)
                dve.wait_ge(*chunk_done(g, FT - 1))
                for i, bank in enumerate((PA[2], PA[3], PV[0], PV[1])):
                    x = X[:, i // 2, (i % 2) * 512:(i % 2 + 1) * 512]
                    v.tensor_tensor(x, x, bank[:, :], ALU.add).then_inc(*dense_added.up())
                dve.wait_ge(*dense_added(0, 4))
                return
            M = L // 2

            def step(ins):
                ins.then_inc(*router_step.up())
                dve.wait_ge(*router_step(M, router_step.count(M)))

            def note(ins):
                ins.then_inc(*router_step.up())

            def noted():
                dve.wait_ge(*router_step(M, router_step.count(M)))

            dve.wait_ge(*router_full(M, 1))
            step(v.tensor_copy(rin[:, :, 0:N_EXP], PV[2][:, 0:NT * N_EXP].rearrange("p (t e) -> p t e", t=NT)))
            for tt in range(NT):
                note(v.max(m8[:, tt, :], rin[:, tt, 0:N_EXP]))
            noted()
            note(v.tensor_tensor(rsc[:, 0, :], m8[:, :, 1], m8[:, :, 0], ALU.subtract))
            step(v.tensor_copy(tr[:, :, 0:2], m8[:, :, 0:2]))
            for tt in range(NT):
                note(v.tensor_scalar(rel[:, tt, :], rin[:, tt, 0:N_EXP], m8[:, tt, 0:1], None, ALU.subtract))
                note(v.match_replace(mr[:, tt, :], tr[:, tt, :], rin[:, tt, :], PICKED))
            noted()
            v.tensor_scalar(rmask[:, :, :], mr[:, :, 0:N_EXP], PICKED, None, ALU.is_equal).then_inc(*mask_ready.up())
            v.tensor_copy(tabf[:, 7:8], one[:, :]).then_inc(*top2_ready.up())
            dve.wait_ge(*top2_exp(M, 1))
            dve.wait_ge(*mask_ready(M, 1))
            note(v.tensor_scalar(rsc[:, 2, :], rsc[:, 1, :], 1.0, None, ALU.add))
            step(v.tensor_tensor(gate[:, :, 0:N_EXP], rel[:, :, :], rmask[:, :, :], ALU.mult))
            step(v.reciprocal(rsc[:, 3, :], rsc[:, 2, :]))
            step(v.tensor_tensor(gate[:, :, 0:N_EXP], gate[:, :, 0:N_EXP], along(rsc[:, 3, :], N_EXP), ALU.mult))
            dve.wait_ge(*router_full(M, 2))
            bank = PV[3]
            step(v.scalar_tensor_tensor(out=posm[:, :, 0:N_EXP], in0=bank[:, 0:NT * N_EXP]
                                        .rearrange("p (t e) -> p t e", t=NT), scalar=1.0, in1=rmask[:, :, :],
                                        op0=ALU.add, op1=ALU.mult))
            step(v.tensor_scalar(posm[:, :, 0:N_EXP], posm[:, :, 0:N_EXP], -1.0, None, ALU.add))
            for i in range(FURTHER):
                c = slice(i * N_EXP, (i + 1) * N_EXP)
                if i:
                    note(v.tensor_scalar(posm[:, :, c], posm[:, :, 0:N_EXP], -float(i * BLOCK), None, ALU.add))
                    note(v.tensor_copy(gate[:, :, c], gate[:, :, 0:N_EXP]))
                ins = v.tensor_scalar(cnt[:, 0, c], bank[:, 16:24], (i + 1) * BLOCK + 0.5, None, ALU.is_gt)
                if i < FURTHER - 1:
                    note(ins)
                else:
                    ins.then_inc(*router_read.up())
            noted()
            dve.wait_ge(*router_read(M, 1))
            step(v.tensor_tensor_scan(cnt[:, 1, :], ones[:, 0:N_CAND], cnt[:, 0, :], 0.0, ALU.mult, ALU.add))
            for k in range(MAX_OVER):
                note(v.scalar_tensor_tensor(out=oh[:, k, :], in0=cnt[:, 1, :], scalar=float(k + 1), in1=cnt[:, 0, :],
                                            op0=ALU.is_equal, op1=ALU.mult))
            note(v.tensor_copy(BT[:, :, 0:N_EXP], posm[:, :, 0:N_EXP]))
            note(v.tensor_copy(GT[:, :, 0:N_EXP], gate[:, :, 0:N_EXP]))
            note(v.tensor_scalar(tabf[:, 0:1], cnt[:, 1, N_CAND - 1:N_CAND], 1.0, None, ALU.add))
            noted()
            for k in range(MAX_OVER):
                for i, (x, at, dst) in enumerate(((erow[:, :], 0.0, tabf[:, 2 + k:3 + k]),
                                   (posm[:, 0, :], -float(BLOCK), BT[:, 0, N_EXP + k:N_EXP + k + 1]),
                                   (posm[:, 1, :], -float(BLOCK), BT[:, 1, N_EXP + k:N_EXP + k + 1]),
                                   (gate[:, 0, :], 0.0, GT[:, 0, N_EXP + k:N_EXP + k + 1]),
                                   (gate[:, 1, :], 0.0, GT[:, 1, N_EXP + k:N_EXP + k + 1]))):
                    note(v.tensor_tensor_reduce(rtmp[:, 5 * k + i, :], oh[:, k, :], x, 1.0, at, ALU.mult, ALU.add, dst))
            noted()
            v.tensor_copy(tabi[:, :], tabf[:, :]).then_inc(*table_ready.up())
            dve.wait_ge(*table_ready(M, 1))

            more = dve.value_load(tabi[0:1, 0:1], min_val=1, max_val=MAX_OVER + 1)

            def place(dst, b, gates, done):
                for tt in range(NT):
                    col_b = BT[:, tt, bass.ds(b, 1)]
                    if gates:
                        ins = v.tensor_scalar(dst[:, tt, :], iota_j[:, 0:BLOCK], col_b, GT[:, tt, bass.ds(b, 1)],
                                              ALU.is_equal, ALU.mult)
                    else:
                        ins = v.tensor_scalar(dst[:, tt, :], iota_j[:, 0:BLOCK], col_b, None, ALU.is_equal)
                ins.then_inc(done.sem, 1)

            def take_tokens(b):
                for half in range(2):
                    dve.wait_ge(*hc_full(b, half + 1))
                    v.tensor_tensor(hcT[:, half * 4:half * 4 + 4, :],
                                    PV[half][:, 0:4 * BLOCK].rearrange("p (c j) -> p c j", c=4),
                                    along(ffn_g[:, half * 4:half * 4 + 4], BLOCK), ALU.mult) \
                        .then_inc(hc_ready.sem, 1)

            def add(q, half):
                for tt in range(NT):
                    dve.wait_ge(*sc_full(q, 2 * half + tt + 1))
                    x = X[:, tt, half * 512:(half + 1) * 512]
                    v.tensor_tensor(x, x, PV[tt][:, :], ALU.add).then_inc(moe_added.sem, 1)

            v.memset(yc, 0.0).then_inc(yc_ready.sem, 1)
            v.memset(PGT[:, :, :], 0.0).then_inc(pgt_ready.sem, 1)
            place(PM, 0, False, pm_ready)
            take_tokens(0)

            def tokens_low(b):
                dve.wait_ge(*hc_high(b, 1))
                less(hcL[:, :, :], hcT[:, :, :], hcH[:, :, :]).then_inc(hc_low.sem, 1)

            rest_gu(first_block(L), 0)
            tokens_low(0)
            with dve.Fori(0, N_EXP - 1 + more) as b:
                g = first_block(L) + b

                def act_rest(t):
                    dve.wait_ge(*act_high(g, t + 1))
                    less(aL[:, t % 2, :], PV[3][:, 0:BLOCK], aH[:, t % 2, :]) \
                        .then_inc(act_low.sem, 1)

                for t in range(FT):
                    if t:
                        activate(g, t - 1, P, sg, at_)
                    rest_gu(g, t + 1)
                    if t:
                        act_rest(t - 1)
                    rest_d(g, t)
                    if t == 2:
                        add(b, 0)
                    if t == 4:
                        add(b, 1)
                        place(PG, b, True, pg_ready)
                        place(PM, b + 1, False, pm_ready)
                    if t == 8:
                        take_tokens(b + 1)
                activate(g, FT - 1, P, sg, at_)
                tokens_low(b + 1)
                act_rest(FT - 1)
            for half in range(2):
                add(N_EXP - 1 + more, half)

        @block.vector
        def _(dve):
            for j in range(8):
                nc.vector.memset(inv[:, j:j + 1], ROPE_THETA ** (-2.0 * j / ROT))
            nc.vector.memset(rin[:, :, :], PAD)
            nc.vector.memset(tr[:, :, :], PAD).then_inc(act_ready.sem, 1)
            nc.vector.memset(BT[:, :, :], -1.0)
            nc.vector.memset(tabf[:, :], float(N_EXP)).then_inc(set_up, 1)
            dve.wait_ge(set_up, 1)
            dve.wait_ge(in_small, 16)
            n = [0]

            def link(ins):
                n[0] += 1
                ins.then_inc(trig_step, 1)
                dve.wait_ge(trig_step, n[0])
            link(nc.vector.tensor_copy(pos_f[:, :], pos_i[:, :]))
            for t in range(NT):
                link(nc.vector.tensor_scalar(ang[:, t, :], inv[:, :], pos_f[:, t:t + 1], None, ALU.mult))
            link(nc.vector.tensor_scalar(kay[:, :, :], ang[:, :, :], 1.0 / TWO_PI, ROUND_BIG, ALU.mult, ALU.add))
            link(nc.vector.tensor_scalar(kay[:, :, :], kay[:, :, :], -ROUND_BIG, None, ALU.add))
            for part in TURN_PARTS:
                link(nc.vector.scalar_tensor_tensor(out=ang[:, :, :], in0=kay[:, :, :], scalar=-part,
                                                    in1=ang[:, :, :], op0=ALU.mult, op1=ALU.add))
            dve.wait_ge(trig_act, 1)
            link(nc.vector.tensor_tensor(cs_[:, :, :], kay[:, :, :], kay[:, :, :], ALU.mult))
            link(nc.vector.tensor_scalar(cs_[:, :, :], cs_[:, :, :], -2.0, 1.0, ALU.mult, ALU.add))
            dve.wait_ge(const_ready, 2)
            for L in range(DEPTH):
                dve_layer(dve, L)

        if DEBUG:
            print({s.name: s.n / s.laps for s in signals if s.n and s.n / s.laps != 1})


def kernel(**inputs):
    import numpy as np
    import concourse.bacc as bacc
    from concourse.bass_utils import run_bass_kernel_spmd

    a = {k: np.asarray(v) for k, v in inputs.items()}

    def tiles(w):
        return w.reshape(-1, P, w.shape[-1]).transpose(1, 0, 2).reshape(P, -1)

    def column(v):
        return v.reshape(-1, P).T

    cols, rows, wmix = [], [], np.zeros((DEPTH * MIX_ITEMS, P, SLOT), np.float32)
    for l in range(DEPTH):
        w_in, w_out, w_kv = a["w_in"][l], a["w_out"][l], a["memx_w_kv"][l]
        dw = a["conv_dw_w"][l].T.reshape(2, P, CONV_W).transpose(1, 0, 2).reshape(P, -1)
        sw = a["ssd_conv_w"][l].T.reshape(KT, P, SSD_CONV).transpose(1, 0, 2).reshape(P, -1)
        twice = [np.concatenate([a[n][l]] * 2)[:, None] for n in ("memx_q_norm_g", "memx_k_norm_g")]
        cols.append(np.concatenate([column(a["mix_norm_g"][l]), column(a["memx_norm_g"][l]),
                                    column(a["mem_norm_g"][l]), dw, column(a["conv_ln_g"][l]),
                                    column(a["conv_ln_b"][l]), sw, column(a["ssd_conv_b"][l]),
                                    column(a["ssd_norm_g"][l])] + twice, axis=1))
        rows.append(np.concatenate([a["att_q_norm_g"][l], a["att_k_norm_g"][l], a["ssd_dt_bias"][l],
                                    a["ssd_a_log"][l], a["ssd_d"][l]]))
        xbc_conv = np.concatenate([w_in[:, 1024:2048], w_in[:, 0:512]], axis=1)
        u = np.concatenate([w_in[:, 2056:3408], w_in[:, 2048:2056]], axis=1)
        items = [tiles(xbc_conv[:, i * WIDE:(i + 1) * WIDE]) for i in range(4)]
        items += [tiles(u[:, i * WIDE:(i + 1) * WIDE]) for i in range(4)]
        items += [tiles(w_in[:, 512:512 + WIDE]),
                  np.concatenate([tiles(w_in[:, 512 + WIDE:1024]), tiles(a["conv_pw_w"][l])], axis=1)]
        items += [tiles(w_kv[:, 0:WIDE]), tiles(w_kv[:, WIDE:])]
        w_o = a["memx_w_o"][l]
        items += [tiles(w_out[:, 0:WIDE]), tiles(w_out[:, WIDE:2 * WIDE]),
                  np.concatenate([tiles(w_out[:, 2 * WIDE:]), w_o[0:P]], axis=1),
                  np.concatenate([tiles(a["memx_w_q"][l]), w_o[P:2 * P]], axis=1)]
        for i, item in enumerate(items):
            wmix[l * MIX_ITEMS + i, :, 0:item.shape[1]] = item
    wffn = np.empty(((1 + N_EXP) * FT, P, SLOT), np.float32)
    for kind, at in (("w_gate", 0), ("w_up", KT * P)):
        for e in range(1 + N_EXP):
            w = a["ffn_" + kind][0] if e == 0 else a["moe_" + kind][0][e - 1]
            wffn[e * FT:(e + 1) * FT, :, at:at + KT * P] = \
                w.reshape(KT, P, FT, P).transpose(2, 1, 0, 3).reshape(FT, P, KT * P)
    for e in range(1 + N_EXP):
        w = a["ffn_w_down"][0] if e == 0 else a["moe_w_down"][0][e - 1]
        wffn[e * FT:(e + 1) * FT, :, 2 * KT * P:] = w.reshape(FT, P, D_MODEL)

    arrays = {
        "x_dram": a["x"], "mem_dram": a["mem"],
        "positions_dram": np.ascontiguousarray(a["positions"].reshape(NT, P).T),
        "cols_dram": np.stack(cols), "rows_dram": np.stack(rows),
        "ffn_g_dram": np.ascontiguousarray(a["ffn_norm_g"].reshape(DEPTH, KT, P).transpose(2, 0, 1)),
        "router_dram": np.ascontiguousarray(tiles(a["moe_w_router"][0]).reshape(P, KT, N_EXP)),
        "wmix_dram": wmix, "wffn_dram": wffn,
    }
    nc = bacc.Bacc("TRN2", target_bir_lowering=False, num_devices=1)
    args = [nc.dram_tensor(n, v.shape, mybir.dt.from_np(v.dtype), kind="ExternalInput").ap()
            for n, v in arrays.items()]
    args.append(nc.dram_tensor("out_dram", (1, SEQ, D_MODEL), F32, kind="ExternalOutput").ap())
    trunk_kernel(nc, *args)
    r = run_bass_kernel_spmd(nc, [arrays], core_ids=[0])
    return r.results[0]["out_dram"]
```

```python
from contextlib import ExitStack

import concourse.bass as bass
from concourse import mybir

F32 = mybir.dt.float32
F32R = mybir.dt.float32r
BF16 = mybir.dt.bfloat16
I32 = mybir.dt.int32
ALU = mybir.AluOpType
ACT = mybir.ActivationFunctionType
AX_X = mybir.AxisListType.X

P = 128
SEQ, D_MODEL, DEPTH = 256, 1024, 2
NT = SEQ // P
KT = D_MODEL // P
D_CONV, CONV_W = 256, 31
D_SSD, SSD_H, SSD_P, SSD_CONV = 512, 8, 64, 4
D_ATT, ATT_H, HD = 256, 4, 64
IDX_H = 8
TOPK = 64
ROPE_THETA, ROT = 500000.0, 16
MEM_H = 4
D_FF, N_EXP = 2816, 8
FT = D_FF // P
N_MOE = DEPTH // 2
EPS = 1e-6

WSLOTS = 8
SLOT = 3 * KT * P
MIX_ITEMS = 16
WIDE = SLOT // KT
LOOP_SLOTS = WSLOTS - 1
ROUNDS = FT // LOOP_SLOTS
BLOCK = 96
MAX_OVER = (2 * SEQ) // (BLOCK + 1)
FURTHER = (SEQ - 1) // BLOCK
N_CAND = FURTHER * N_EXP
GU_COLS, D_COLS = 2 * KT * P, D_MODEL

U_V, U_QI, U_KI, U_W, U_DT, U_N = 512, 768, 1280, 1344, 1352, 1360
U_HEADS = 21

COLS = {}
_n = 0
for _name, _w in (("mix_g", KT), ("memx_g", KT), ("mem_g", KT), ("conv_w", 2 * CONV_W), ("ln_g", 2),
                  ("ln_b", 2), ("ssd_w", KT * SSD_CONV), ("ssd_b", KT), ("ssd_g", 4),
                  ("mq_g", 1), ("mk_g", 1)):
    COLS[_name] = _n
    _n += _w
N_COLS = _n
R_QK, R_DTB, R_ALOG, R_D, N_ROWS = 0, 128, 136, 144, 152

LOG_EXP = "natural_log_exp_and_others"
MASKED = -1e30
TAKEN = -3e38
PAD = -3e38
PICKED = -2e38

TWO_PI = 6.283185307179586
TURN_PARTS = (6.28125, 0.0019350051879882812, 3.0199159819567e-07)
ROUND_BIG = 12582912.0

RAISES = {
    "x_low": 4,
    "x_high": 4,
    "router_step": 52,
    "router_full": 2,
    "a_full": 65, "a_free": 65, "v_full": 32, "v_free": 32, "dve_step": 170, "act_step": 20,
    "x_ready": 4, "rstd_ready": 6, "h_ready": 6, "xbc_conv": 4, "xc_ready": 4, "a_ready": 2,
    "m_ready": 2, "score_used": 8, "att_ready": 4, "exp_ready": 4, "p_ready": 4, "mem_ready": 2,
    "hn_ss": 2, "hn_rstd": 2,
    "gu_full": FT, "silu_ready": FT, "act_ready": FT,
    "high_gu": FT, "low_gu": FT, "high_d": FT, "low_d": FT,
    "turned": FT, "act_high": FT, "act_low": FT, "dense_added": 4, "hc_full": 2, "hc_ready": 2,
    "sc_full": 4, "moe_added": 4,
}
A_SEG, A_INDEX, A_KV, A_MQ = 24, 29, 45, 56


class Signal:

    def __init__(self, sem, name, per, start=0, laps=1):
        self.sem, self.name, self.per, self.start, self.laps, self.n = sem, name, per, start, laps, 0

    def count(self, lap):
        return self.n - lap * self.per

    def up(self):
        self.n += 1
        return self.sem, 1

    def __call__(self, lap, k):
        return self.sem, lap * self.per + (self.start + k)


def index_head(pair, j):
    return 4 * (pair // 2) + pair % 2 + 2 * j


def trunk_kernel(nc, x_in, mem_in, pos_in, cols_in, rows_in, ffn_g_in, router_in, wmix, wffn, out):
    with ExitStack() as ctx:
        def sb(name, shape, dt=F32):
            return ctx.enter_context(nc.sbuf_tensor(name, shape, dt))

        signals = []

        def signal(name, start=0, laps=DEPTH):
            s = Signal(ctx.enter_context(nc.semaphore(name)), name, RAISES.get(name, 1), start, laps)
            signals.append(s)
            return s

        XR_COLS = KT * (SEQ + 3)
        shared = (("W", [P, WSLOTS, SLOT]), ("FB", [P, XR_COLS + KT * SEQ + 2 * NT * D_SSD]),
                  ("H", [P, NT, D_MODEL]), ("HT", [P, KT, SEQ]), ("U", [P, NT, U_N]))
        with ExitStack() as names:
            W, FB, H, HT, U = (names.enter_context(nc.sbuf_tensor(n, shape, F32)) for n, shape in shared)
        W_R, FB_R, H_R, HT_R, U_R = (sb(n + "_R", shape, F32R) for n, shape in shared)
        X = sb("X", [P, NT, D_MODEL])
        XR_LM = FB[:, 0:XR_COLS]
        XR = XR_LM.rearrange("p (k s) -> p k s", k=KT)
        XC = FB[:, XR_COLS:XR_COLS + KT * SEQ].rearrange("p (k s) -> p k s", k=KT)
        LM = XR_LM[:, 0:NT * SSD_H * P].rearrange("p (t h l) -> p t h l", t=NT, h=SSD_H)
        Z = sb("Z", [P, NT, D_SSD])
        hpad = sb("hpad", [P, 2, SEQ + CONV_W - 1])
        cacc = sb("cacc", [P, 2, SEQ])
        ctmp = sb("ctmp", [P, 2, SEQ])
        xd, ysk = (FB[:, XR_COLS + KT * SEQ + i * NT * D_SSD:XR_COLS + KT * SEQ + (i + 1) * NT * D_SSD]
                   .rearrange("p (t n) -> p t n", t=NT) for i in range(2))
        WHgu = [FB_R[:, i * GU_COLS:(i + 1) * GU_COLS] for i in (1, 0)]
        WHd = [FB_R[:, 2 * GU_COLS + i * D_COLS:2 * GU_COLS + (i + 1) * D_COLS] for i in range(2)]
        xdd = sb("xdd", [P, D_SSD])
        btok = sb("btok", [P, 2, P])
        st = sb("st", [P, 2, 256])
        qkT = sb("qkT", [P, 4, SEQ])
        qiT = sb("qiT", [P, 4, SEQ])
        kiT = sb("kiT", [P, SEQ])
        kk = sb("kk", [P, NT, P])
        score = sb("score", [P, NT, SEQ])
        rl = sb("rl", [P, 2, 2, SEQ])
        abias = sb("abias", [P, NT, SEQ])
        prob = sb("prob", [P, NT, 4, SEQ])
        pT = sb("pT", [P, 2, 4, P])
        RN = NT * U_HEADS * 8
        TA = H[:, :, :].rearrange("p t (h l) -> p t h l", h=SSD_H)
        YT = HT
        MT = XC
        kvt = LM[:, 0, :, :].rearrange("p h l -> p (h l)").rearrange("p (t n) -> p t n", t=NT)
        KTm = LM[:, 1, 0:4, :].rearrange("p h l -> p (h l)").rearrange("p (t n) -> p t n", t=2)
        mq = LM[:, 1, 4:8, :].rearrange("p h l -> p (h l)").rearrange("p (t n) -> p t n", t=NT)
        mqT = st
        rt = [t[:, :, :].rearrange("p c s -> p (c s)")[:, i * RN:(i + 1) * RN]
              .rearrange("p (t h d) -> p t h d", t=NT, h=U_HEADS) for t in (qkT, qiT) for i in range(2)]
        oT = xdd[:, :].rearrange("p (t n) -> p t n", t=2)
        junk = rl[:, :, :, :].rearrange("p a b s -> p (a b s)")
        HTH, HTL = H_R[:, :, :].rearrange("p t n -> p (t n)").rearrange("p (k s) -> p k s", k=KT), HT_R
        sgd, atd, ahd, ald = (u[:, i // 2, (i % 2) * 2 * SEQ:(i % 2 + 1) * 2 * SEQ]
                              .rearrange("p (b j) -> p b j", b=2) for i, u in enumerate((U, U, U_R, U_R)))
        hcT = U[:, 0, 0:KT * BLOCK].rearrange("p (c j) -> p c j", c=KT)
        HTf = HT_R[:, :, :].rearrange("p k s -> p (k s)")
        hcH, hcL = (HTf[:, i * KT * BLOCK:(i + 1) * KT * BLOCK].rearrange("p (c j) -> p c j", c=KT)
                    for i in range(2))
        sg, at_ = (U[0:BLOCK, 1, i * 2 * P:(i + 1) * 2 * P].rearrange("p (b j) -> p b j", b=2) for i in range(2))
        aH, aL = (U_R[:, 1, 4 * P + i * 2 * BLOCK:4 * P + (i + 1) * 2 * BLOCK].rearrange("p (b j) -> p b j", b=2)
                  for i in range(2))
        yc = Z[0:BLOCK, :, :].rearrange("p t n -> p (t n)")
        PM = qiT[:, 0, 0:NT * BLOCK].rearrange("p (t j) -> p t j", t=NT)
        PG = qiT[:, 1, 0:NT * BLOCK].rearrange("p (t j) -> p t j", t=NT)
        PGT = qiT[0:BLOCK, 2, :].rearrange("p (t j) -> p t j", t=NT)

        ident = sb("ident", [P, P])
        tri = sb("tri", [P, P])
        tri_s = sb("tri_s", [P, P])
        ones = sb("ones", [P, P])
        ident_b = sb("ident_b", [P, P], BF16)
        neg_ssd = sb("neg_ssd", [P, P], BF16)
        neg_att = sb("neg_att", [P, P])
        iota_j = sb("iota_j", [P, P])
        cols = sb("cols", [P, N_COLS])
        rows = sb("rows", [P, N_ROWS])
        ffn_g2 = sb("ffn_g2", [P, DEPTH, KT])
        ffn_g = sb("ffn_g", [P, KT])
        wr = sb("wr", [P, KT, N_EXP])
        pos_i = sb("pos_i", [P, NT], I32)
        pos_f = sb("pos_f", [P, NT])
        ang = sb("ang", [P, NT, 8])
        kay = sb("kay", [P, NT, 8])
        cs_ = sb("cs_", [P, NT, 8])
        sn_ = sb("sn_", [P, NT, 8])
        inv = sb("inv", [P, 8])
        eps = sb("eps", [P, 1])
        one = sb("one", [P, 1])
        ss = sb("ss", [P, 32])
        rs = sb("rs", [P, 32])
        dts = sb("dts", [P, 6, NT, SSD_H])
        anum = sb("anum", [P, SSD_H])
        cum = sb("cum", [P, NT, 2, SSD_H])
        ncum = sb("ncum", [P, NT, SSD_H])
        ecum = sb("ecum", [P, 2, SSD_H])
        m8 = sb("m8", [P, NT, 8])
        nmx = sb("nmx", [P, NT, 4])
        psm = sb("psm", [P, NT, 4])
        prs = sb("prs", [P, NT, 4])
        rin = sb("rin", [P, NT, 16])
        tr = sb("tr", [P, NT, 8])
        mr = sb("mr", [P, NT, 16])
        rmask = sb("rmask", [P, NT, N_EXP])
        rel = sb("rel", [P, NT, N_EXP])
        rsc = sb("rsc", [P, 4, NT])
        gate = sb("gate", [P, NT, N_CAND])
        posm = sb("posm", [P, NT, N_CAND])
        cnt = sb("cnt", [P, 2, N_CAND])
        oh = score[:, :, :].rearrange("p t s -> p (t s)")[:, 5 * MAX_OVER * N_CAND:6 * MAX_OVER * N_CAND] \
            .rearrange("p (i e) -> p i e", e=N_CAND)
        rtmp = score[:, :, :].rearrange("p t s -> p (t s)")[:, 0:5 * MAX_OVER * N_CAND] \
            .rearrange("p (i e) -> p i e", e=N_CAND)
        NB = N_EXP + MAX_OVER + 1
        BT = sb("BT", [P, NT, NB])
        GT = sb("GT", [P, NT, NB])
        tabf = sb("tabf", [P, 8])
        erow = sb("erow", [P, N_CAND])
        tabi = sb("tabi", [P, 8], I32)

        PA = [ctx.enter_context(nc.psum_tensor(f"PA{i}", [P, 512], F32)) for i in range(4)]
        PV = [ctx.enter_context(nc.psum_tensor(f"PV{i}", [P, 512], F32)) for i in range(4)]

        slot_full = [ctx.enter_context(nc.semaphore(f"slot_full{s}")) for s in range(WSLOTS)]
        slot_free = [ctx.enter_context(nc.semaphore(f"slot_free{s}")) for s in range(WSLOTS)]
        in_x = [ctx.enter_context(nc.semaphore(f"in_x{tt}")) for tt in range(NT)]
        in_small = ctx.enter_context(nc.semaphore("in_small"))
        in_ffn = ctx.enter_context(nc.semaphore("in_ffn"))
        in_params = ctx.enter_context(nc.semaphore("in_params"))
        next_params = ctx.enter_context(nc.semaphore("next_params"))
        in_mem = ctx.enter_context(nc.semaphore("in_mem"))
        out_done = ctx.enter_context(nc.semaphore("out_done"))
        const_ready = ctx.enter_context(nc.semaphore("const_ready"))
        zeros_ready = ctx.enter_context(nc.semaphore("zeros_ready"))
        set_up = ctx.enter_context(nc.semaphore("set_up"))
        trig_step = ctx.enter_context(nc.semaphore("trig_step"))
        trig_act = ctx.enter_context(nc.semaphore("trig_act"))
        a_full, a_free = signal("a_full"), signal("a_free")
        v_full, v_free = signal("v_full"), signal("v_free")
        dve_step = signal("dve_step")
        act_step = signal("act_step")
        x_ready = signal("x_ready")
        rstd_ready = signal("rstd_ready")
        h_ready = signal("h_ready")
        xr_ready = signal("xr_ready")
        xbc_conv = signal("xbc_conv")
        xc_ready = signal("xc_ready")
        conv_acc = signal("conv_acc")
        conv_centred = signal("conv_centred")
        conv_rstd = signal("conv_rstd")
        conv_norm = signal("conv_norm")
        conv_aff = signal("conv_aff")
        conv_out = signal("conv_out")
        qk_ss, qk_rstd = signal("qk_ss"), signal("qk_rstd")
        dt_in = signal("dt_in")
        dt_log = signal("dt_log")
        rope_ready = signal("rope_ready")
        a_ready = signal("a_ready")
        xdd_ready = signal("xdd_ready")
        cum_ready = signal("cum_ready")
        ecum_ready = signal("ecum_ready")
        m_ready = signal("m_ready")
        score_used = signal("score_used")
        att_ready = signal("att_ready")
        exp_ready = signal("exp_ready")
        p_ready = signal("p_ready")
        y_ss, y_rstd = signal("y_ss"), signal("y_rstd")
        y_ready = signal("y_ready")
        mem_rstd = signal("mem_rstd")
        mem_ready = signal("mem_ready")
        hn_ss, hn_rstd = signal("hn_ss"), signal("hn_rstd")
        hn_ready = signal("hn_ready")
        ffn_g_ready = signal("ffn_g_ready")
        router_full, router_step = signal("router_full", laps=N_MOE), signal("router_step", laps=N_MOE)
        router_read = signal("router_read", laps=N_MOE)
        mask_ready = signal("mask_ready", laps=N_MOE)
        top2_ready = signal("top2_ready", laps=N_MOE)
        top2_exp = signal("top2_exp", laps=N_MOE)
        table_ready = signal("table_ready", laps=N_MOE)
        gu_full = signal("gu_full")
        silu_ready = signal("silu_ready")
        act_ready = signal("act_ready", start=1)
        high_gu, low_gu = signal("high_gu"), signal("low_gu")
        high_d, low_d = signal("high_d"), signal("low_d")
        turned = signal("turned")
        act_high, act_low = signal("act_high"), signal("act_low")
        dense_added = signal("dense_added", laps=1)
        x_high, x_low = signal("x_high", laps=1), signal("x_low", laps=1)
        hc_high, hc_low = signal("hc_high"), signal("hc_low")
        pm_ready, pg_ready = signal("pm_ready"), signal("pg_ready")
        hc_full, hc_ready = signal("hc_full"), signal("hc_ready")
        pgt_full, pgt_ready = signal("pgt_full"), signal("pgt_ready", start=1)
        yc_ready = signal("yc_ready", start=1)
        sc_full, moe_added = signal("sc_full"), signal("moe_added")

        block = ctx.enter_context(nc.Block())

        released = {}

        def first_block(L):
            return L

        def params_ready(L):
            return (in_params, 32) if L == 0 else (next_params, 32 * L)

        def slot_loads(L, s, item=None, g=None, r=0):
            a_block = ROUNDS if s else 1
            if g is None:
                return L * (MIX_ITEMS // WSLOTS) + first_block(L) * a_block + item // WSLOTS
            return (L + 1) * (MIX_ITEMS // WSLOTS) + g * a_block + r

        def slot_of(t):
            return 0 if t == 0 else 1 + (t - 1) % LOOP_SLOTS

        def chunk_full(L, g, t):
            s = slot_of(t)
            return slot_full[s], (slot_loads(L, s, g=g, r=(t - 1) // LOOP_SLOTS if t else 0) + 1) * 16

        def chunk_done(g, t):
            if t < 0:
                g, t = g - 1, t + FT
            s = slot_of(t)
            return slot_free[s], chunk_reads(s, g, (t - 1) // LOOP_SLOTS if t else 0) + 1

        def chunk_reads(s, g, r=0):
            return 1 + g * (ROUNDS if s else 1) + r

        def pe_layer(pe, L):
            na, nv = [0], [0]

            def a_bank():
                na[0] += 1
                if na[0] > 4:
                    pe.wait_ge(*a_free(L, na[0] - 4))
                return PA[(na[0] - 1) % 4]

            def v_bank():
                nv[0] += 1
                if nv[0] > 4:
                    pe.wait_ge(*v_free(L, nv[0] - 4))
                return PV[(nv[0] - 1) % 4]

            def a_taken():
                pe.wait_ge(*a_free(L, na[0]))

            def arrived(item):
                s = item % WSLOTS
                pe.wait_ge(slot_full[s], (slot_loads(L, s, item=item) + 1) * 16)
                return W[:, s, :]

            def k_tiles(view, width, at=0):
                return view[:, at:at + KT * width].rearrange("p (k n) -> p k n", k=KT)

            def transposes(tiles, src):
                for at in range(0, len(tiles), 2):
                    bank = a_bank()
                    for j, tile in enumerate(tiles[at:at + 2]):
                        for tt in range(NT):
                            last = pe.transpose(bank[:, j * SEQ + tt * P:j * SEQ + (tt + 1) * P],
                                                src(tile, tt), ident[:, :])
                    last.then_inc(*a_full.up())

            def normed_transposes(norm):
                for tt in range(NT):
                    pe.wait_ge(*h_ready(L, norm * NT + tt + 1))
                    for c0 in range(0, KT, 4):
                        bank = v_bank() if tt else a_bank()
                        for j in range(4):
                            last = pe.transpose(bank[:, j * P:(j + 1) * P], H[:, tt, (c0 + j) * P:(c0 + j + 1) * P],
                                                ident[:, :])
                        last.then_inc(*(v_full if tt else a_full).up())
                a_taken()
                pe.wait_ge(*v_free(L, nv[0]))

            def accumulate(dst, pairs):
                for i, (lhsT, rhs) in enumerate(pairs):
                    last = pe.matmul(dst, lhsT, rhs, start=(i == 0), stop=(i == len(pairs) - 1))
                return last

            def tokens_by(dst, act, view, tt):
                return accumulate(dst, [(act[:, k, tt * P:(tt + 1) * P], view[:, k, :]) for k in range(KT)])

            normed_transposes(0)
            for tile in range(12):
                item = tile // 3
                view = k_tiles(arrived(item), WIDE)
                if tile % 2 == 0:
                    bank = a_bank()
                f = (tile % 3) * P
                last = accumulate(bank[:, (tile % 2) * SEQ:(tile % 2 + 1) * SEQ],
                                  [(view[:, k, f:f + P], HT[:, k, :]) for k in range(KT)])
                if tile % 2:
                    last.then_inc(*a_full.up())
                released[item] = a_full, na[0]
            for item in range(4, 8):
                width = WIDE if item < 7 else U_N - 3 * WIDE
                view = k_tiles(arrived(item), width)
                for tt in range(NT):
                    tokens_by(a_bank()[:, 0:width], HT, view, tt).then_inc(*a_full.up())
                released[item] = a_full, na[0]
            pe.wait_ge(*conv_acc(L, 1))
            pe.wait_ge(const_ready, 3)
            accumulate(v_bank()[:, 0:SEQ], [(ones[:, :], cacc[:, j, :]) for j in range(2)]).then_inc(*v_full.up())
            z0, z1 = k_tiles(arrived(8), WIDE), k_tiles(arrived(9), P)
            for tt in range(NT):
                bank = a_bank()
                tokens_by(bank[:, 0:WIDE], HT, z0, tt)
                tokens_by(bank[:, WIDE:512], HT, z1, tt).then_inc(*a_full.up())
            released[8] = a_full, na[0]
            pe.wait_ge(*conv_centred(L, 1))
            accumulate(a_bank()[:, 0:SEQ], [(ones[:, :], ctmp[:, j, :]) for j in range(2)]).then_inc(*a_full.up())
            pe.wait_ge(*xc_ready(L, 4))
            for tt in range(NT):
                bank = v_bank()
                for j in range(4):
                    last = pe.transpose(bank[:, j * P:(j + 1) * P], XC[:, j, tt * P:(tt + 1) * P], ident[:, :])
                last.then_inc(*v_full.up())
            bank = a_bank()
            for j in range(2):
                last = pe.transpose(bank[:, j * P:(j + 1) * P], XC[:, 4 + j, 0:P], ident[:, :])
            last.then_inc(*a_full.up())
            b_group = na[0]
            pe.wait_ge(const_ready, 3)
            pe.wait_ge(*a_ready(L, 1))
            bank = v_bank()
            for tt in range(NT):
                pe.matmul(bank[:, tt * 16:tt * 16 + 8], tri[:, :], dts[:, 4, tt, :], start=True, stop=True)
                last = pe.matmul(bank[:, tt * 16 + 8:tt * 16 + 16], ones[:, :], dts[:, 4, tt, :],
                                 start=True, stop=True)
            last.then_inc(*v_full.up())
            pe.wait_ge(*a_ready(L, 2))
            for tt in range(NT):
                for half in range(2):
                    bank = a_bank()
                    hs = slice(half * 4, half * 4 + 4)
                    pe.matmul(bank[:, :], ones[:, :], TA[:, tt, hs, :], start=True, stop=False)
                    pe.matmul(bank[:, :], ident_b[:, :], neg_ssd[:, :].unsqueeze(1).to_broadcast([P, 4, P]),
                              start=False, stop=True).then_inc(*a_full.up())
            released["TA"] = a_full, na[0]
            bank = v_bank()
            for tt in range(NT):
                for g in range(2):
                    o = (tt * 2 + g) * P
                    last = pe.matmul(bank[:, o:o + P], XC[:, 4 + g, tt * P:(tt + 1) * P],
                                     XC[:, 6 + g, tt * P:(tt + 1) * P], start=True, stop=True)
            last.then_inc(*v_full.up())
            pe.wait_ge(*rope_ready(L, 1))
            transposes([0, 1, 2, 3], lambda c, tt: U[:, tt, U_QI + c * P:U_QI + (c + 1) * P])
            transposes([0], lambda c, tt: kk[:, tt, :])
            index_group = na[0]
            transposes([0, 1, 2, 3], lambda c, tt: U[:, tt, c * P:(c + 1) * P])
            pe.wait_ge(*a_free(L, index_group))
            for tt in range(NT):
                keys = P * (tt + 1)
                for pair in range(IDX_H // 2):
                    bank = a_bank()
                    r = slice(HD * (pair % 2), HD * (pair % 2) + HD)
                    for j in range(2):
                        last = pe.matmul(bank[:, j * SEQ:j * SEQ + keys],
                                         qiT[r, index_head(pair, j) // 2, tt * P:(tt + 1) * P],
                                         kiT[r, 0:keys], start=True, stop=True)
                    last.then_inc(*a_full.up())
            pe.wait_ge(*conv_out(L, 1))
            pw = W[:, 9 % WSLOTS, KT * P:KT * P + 2 * D_CONV].rearrange("p (k n) -> p k n", k=2)
            bank = a_bank()
            for j in range(2):
                last = accumulate(bank[:, j * SEQ:(j + 1) * SEQ],
                                  [(pw[:, k, j * P:(j + 1) * P], ctmp[:, k, :]) for k in range(2)])
            last.then_inc(*a_full.up())
            released[9] = a_full, na[0]
            pe.wait_ge(*xdd_ready(L, 1))
            pe.wait_ge(*a_free(L, b_group))
            bank = a_bank()
            for g in range(2):
                last = pe.matmul(bank[:, g * SEQ:(g + 1) * SEQ], btok[:, g, :], xdd[:, g * SEQ:(g + 1) * SEQ],
                                 start=True, stop=True)
            last.then_inc(*a_full.up())
            for tt in range(NT):
                pe.wait_ge(*m_ready(L, tt + 1))
                bank = v_bank()
                for h in range(SSD_H):
                    last = pe.matmul(bank[:, h * SSD_P:(h + 1) * SSD_P], LM[:, tt, h, :],
                                     xd[:, tt, h * SSD_P:(h + 1) * SSD_P], start=True, stop=True)
                last.then_inc(*v_full.up())
            a_taken()
            bank = v_bank()
            for g in range(2):
                last = pe.matmul(bank[:, g * SEQ:(g + 1) * SEQ], XC[:, 6 + g, P:2 * P], st[:, g, :],
                                 start=True, stop=True)
            last.then_inc(*v_full.up())

            def att_logits(tt, qT, kT, keys):
                for odd in range(2):
                    bank = v_bank()
                    r = slice(HD * odd, HD * odd + HD)
                    for j in range(2):
                        last = pe.matmul(bank[:, j * keys:(j + 1) * keys], qT[r, j, tt * P:(tt + 1) * P],
                                         kT[r, j, 0:keys], start=True, stop=True)
                    last.then_inc(*v_full.up())

            def p_transposes(tt, tiles):
                for s in range(tiles):
                    bank = a_bank()
                    for h in range(4):
                        last = pe.transpose(bank[:, h * P:(h + 1) * P], prob[:, tt, h, s * P:(s + 1) * P], ident[:, :])
                    last.then_inc(*a_full.up())

            def weighted_values(tiles, v):
                bank = a_bank()
                for h in range(4):
                    r = HD * (h % 2)
                    last = accumulate(bank[r:r + HD, (h // 2) * P:(h // 2 + 1) * P],
                                      [(v(s, h), pT[:, s, h, :]) for s in range(tiles)])
                last.then_inc(*a_full.up())

            pe.wait_ge(*a_free(L, index_group + 2))
            for tt in range(NT):
                att_logits(tt, qkT[:, 0:2, :], qkT[:, 2:4, :], P * (tt + 1))
            pe.wait_ge(*mem_ready(L, NT))
            transposes(list(range(KT)), lambda c, tt: H[:, tt, c * P:(c + 1) * P])
            a_taken()
            kv0, kv1 = k_tiles(arrived(10), WIDE), k_tiles(arrived(11), P)
            for tt in range(NT):
                bank = a_bank()
                tokens_by(bank[:, 0:WIDE], MT, kv0, tt)
                tokens_by(bank[:, WIDE:512], MT, kv1, tt).then_inc(*a_full.up())
            released[10] = released[11] = a_full, na[0]

            pe.wait_ge(*y_ready(L, 1))
            transposes([0, 1, 2, 3], lambda c, tt: ysk[:, tt, c * P:(c + 1) * P])
            for tt in range(NT):
                pe.wait_ge(*p_ready(L, tt + 1))
                p_transposes(tt, tt + 1)
                a_taken()
                weighted_values(tt + 1, lambda s, h: U[:, s, U_V + h * HD:U_V + (h + 1) * HD])
            pe.wait_ge(*hn_ready(L, 1))
            transposes([0, 1], lambda c, tt: kvt[:, tt, c * P:(c + 1) * P])
            a_taken()
            for tt in range(NT):
                for item in range(12, 15):
                    width = WIDE if item < 14 else D_MODEL - 2 * WIDE
                    if tt == 0:
                        arrived(item)
                    view = k_tiles(W[:, item % WSLOTS, :], width)
                    tokens_by(v_bank()[:, 0:width], YT, view, tt).then_inc(*v_full.up())
                    released[item] = v_full, nv[0]
            normed_transposes(1)
            wq = k_tiles(arrived(15), D_ATT)
            bank = a_bank()
            for tt in range(NT):
                last = tokens_by(bank[:, tt * D_ATT:(tt + 1) * D_ATT], HT, wq, tt)
            last.then_inc(*a_full.up())
            a_taken()
            transposes([0, 1], lambda c, tt: mq[:, tt, c * P:(c + 1) * P])
            a_taken()
            for tt in range(NT):
                att_logits(tt, mqT, KTm, SEQ)
            for tt in range(NT):
                pe.wait_ge(*p_ready(L, NT + tt + 1))
                p_transposes(tt, 2)
                a_taken()
                weighted_values(2, lambda s, h: kvt[:, s, D_ATT + h * HD:D_ATT + (h + 1) * HD])
            a_taken()
            wo = [W[:, 14 % WSLOTS, KT * 256:KT * 256 + D_MODEL], W[:, 15 % WSLOTS, KT * 256:KT * 256 + D_MODEL]]
            for tt in range(NT):
                for half in range(2):
                    accumulate(v_bank()[:, :], [(oT[:, k, tt * P:(tt + 1) * P],
                                                 wo[k][:, half * 512:(half + 1) * 512])
                                                for k in range(2)]).then_inc(*v_full.up())
            released[14] = released[15] = v_full, nv[0]
            normed_transposes(2)
            pe.wait_ge(*v_free(L, nv[0]))
            if L % 2 == 0:
                pe_dense(pe, L)
            else:
                pe_moe(pe, L)

        GU = (PA[0], PA[1])

        def three_passes(pe, dst, a_high, a_low, b_high, b_low, start, stop):
            pe.matmul(dst, a_high, b_high, start=start, stop=False, skip_group_check=True)
            pe.matmul(dst, a_high, b_low, start=False, stop=False, skip_group_check=True)
            return pe.matmul(dst, a_low, b_high, start=False, stop=stop, skip_group_check=True)

        def gu_parts(t):
            return [w.rearrange("p (m k n) -> p m k n", m=2, k=KT)
                    for w in (WHgu[t % 2], W_R[:, slot_of(t), 0:GU_COLS])]

        def before_gate_up(pe, g, t):
            if t > 0 or not isinstance(g, int):
                pe.wait_ge(*act_ready(g, t - 1))
            pe.wait_ge(*low_gu(g, t + 1))

        def down(pe, g, t, sums, high, low):
            wh, wl = WHd[t % 2], W_R[:, slot_of(t), GU_COLS:SLOT]
            half = [slice((i % 2) * 512, (i % 2 + 1) * 512) for i in range(len(sums))]
            pe.wait_ge(*act_high(g, t + 1))
            pe.wait_ge(*low_d(g, t + 1))
            for i, bank in enumerate(sums):
                pe.matmul(bank, high(i), wh[:, half[i]], start=(t == 0), stop=False, skip_group_check=True)
                pe.matmul(bank, high(i), wl[:, half[i]], start=False, stop=False, skip_group_check=True)
            pe.wait_ge(*act_low(g, t + 1))
            for i, bank in enumerate(sums):
                last = pe.matmul(bank, low(i), wh[:, half[i]], start=False, stop=(t == FT - 1),
                                 skip_group_check=True)
            last.then_inc(slot_free[slot_of(t)], 1)

        def pe_dense(pe, L):
            g = first_block(L)
            sums = [b[:, :] for b in (PA[2], PA[3], PV[0], PV[1])]
            high, low = ([lambda i, t=t, a=a: a[:, t % 2, (i // 2) * P:(i // 2 + 1) * P] for t in range(FT)]
                         for a in (ahd, ald))
            for t in range(FT):
                before_gate_up(pe, g, t)
                wh, wl = gu_parts(t)
                for m in range(2):
                    for k in range(KT):
                        if t == 0 and m == 0 and k % 2 == 0:
                            pe.wait_ge(*x_low(0, k // 2 + 1))
                        last = three_passes(pe, GU[t % 2][:, m * SEQ:(m + 1) * SEQ], wh[:, m, k, :], wl[:, m, k, :],
                                            HTH[:, k, :], HTL[:, k, :], k == 0, k == KT - 1)
                last.then_inc(gu_full.sem, 1)
                if t:
                    down(pe, g, t - 1, sums, high[t - 1], low[t - 1])
            down(pe, g, FT - 1, sums, high[FT - 1], low[FT - 1])

        def pe_moe(pe, L):
            M = L // 2
            pe.wait_ge(in_ffn, 32)
            for tt in range(NT):
                for k in range(KT):
                    last = pe.matmul(PV[2][:, tt * N_EXP:(tt + 1) * N_EXP], HT[:, k, tt * P:(tt + 1) * P],
                                     wr[:, k, :], start=(k == 0), stop=(k == KT - 1))
            last.then_inc(*router_full.up())
            pe.wait_ge(*mask_ready(M, 1))
            for at, pairs in ((0, [(tri_s, 0)]), (8, [(tri_s, 1), (ones, 0)]), (16, [(ones, 0), (ones, 1)])):
                for i, (m, tt) in enumerate(pairs):
                    last = pe.matmul(PV[3][:, at:at + N_EXP], m[:, :], rmask[:, tt, :], start=(i == 0),
                                     stop=(i == len(pairs) - 1))
            last.then_inc(*router_full.up())

            def gather(b):
                pe.wait_ge(*pm_ready(b, 1))
                for half in range(2):
                    for c in range(4):
                        k = half * 4 + c
                        for tt in range(NT):
                            last = pe.matmul(PV[half][:, c * BLOCK:(c + 1) * BLOCK], H[:, tt, k * P:(k + 1) * P],
                                             PM[:, tt, :], start=(tt == 0), stop=(tt == NT - 1))
                    last.then_inc(hc_full.sem, 1)

            def scatter(q, i):
                if i >= 2:
                    pe.wait_ge(*moe_added(q, i - 1))
                pe.matmul(PV[i % 2][:, :], PGT[:, i % 2, :], yc[:, (i // 2) * 512:(i // 2 + 1) * 512],
                          start=True, stop=True).then_inc(sc_full.sem, 1)

            gather(0)
            pe.wait_ge(*table_ready(M, 1))
            more = pe.value_load(tabi[0:1, 0:1], min_val=1, max_val=MAX_OVER + 1)
            with pe.Fori(0, N_EXP - 1 + more) as b:
                g = first_block(L) + b
                sums = [PA[2][0:BLOCK, :], PA[3][0:BLOCK, :]]

                def gate_up(t, half):
                    wh, wl = gu_parts(t)
                    for k in range(half * KT // 2, (half + 1) * KT // 2):
                        last = three_passes(pe, GU[t % 2][0:BLOCK, 0:2 * P], hcH[:, k, :],
                                            hcL[:, k, :], wh[:, :, k, :], wl[:, :, k, :],
                                            k == 0, k == KT - 1)
                    return last

                def turn(t):
                    pe.wait_ge(*act_ready(g, t + 1))
                    pe.transpose(PV[3][:, 0:BLOCK], at_[:, t % 2, :], ident[0:BLOCK, 0:BLOCK]) \
                        .then_inc(turned.sem, 1)

                pe.wait_ge(*hc_low(b, 1))
                for t in range(FT):
                    before_gate_up(pe, g, t)
                    gate_up(t, 0)
                    if t:
                        turn(t - 1)
                    gate_up(t, 1).then_inc(gu_full.sem, 1)
                    if t == 1:
                        pe.wait_ge(*yc_ready(b, 0))
                    if t:
                        down(pe, g, t - 1, sums, lambda i: aH[:, (t - 1) % 2, :],
                             lambda i: aL[:, (t - 1) % 2, :])
                    if t == 1:
                        pe.wait_ge(*pgt_ready(b, 0))
                    if t in (1, 3, 5, 7):
                        scatter(b, t // 2)
                    if t == 10:
                        pe.wait_ge(*moe_added(b, 4))
                        gather(b + 1)
                pe.wait_ge(*pg_ready(b, 1))
                for tt in range(NT):
                    last = pe.transpose(PV[2][0:BLOCK, tt * P:(tt + 1) * P], PG[:, tt, :], ident[:, :])
                last.then_inc(pgt_full.sem, 1)
                turn(FT - 1)
                down(pe, g, FT - 1, sums, lambda i: aH[:, (FT - 1) % 2, :],
                     lambda i: aL[:, (FT - 1) % 2, :])
            pe.wait_ge(*yc_ready(N_EXP - 1 + more, 0))
            pe.wait_ge(*pgt_ready(N_EXP - 1 + more, 0))
            pe.wait_ge(*hc_ready(N_EXP - 1 + more, 2))
            for i in range(4):
                scatter(N_EXP - 1 + more, i)

        @block.tensor
        def _(pe):
            pe.wait_ge(const_ready, 2)
            for L in range(DEPTH):
                pe_layer(pe, L)

        @block.sync
        def _(sp):
            for tt in range(NT):
                sp.dma_start(X[:, tt, :], x_in[0, tt * P:(tt + 1) * P, :]).then_inc(in_x[tt], 16)

            def chunk(g, r, s, expert, after=None):
                if after is not None:
                    sp.wait_ge(*after)
                sp.wait_ge(slot_free[s], chunk_reads(s, g, r))
                sp.dma_start(W[:, s, :], wffn[bass.ds(expert * FT + r * LOOP_SLOTS + s, 1), :, :]
                             .rearrange("a p n -> p (a n)")).then_inc(slot_full[s], 16)

            def expert_chunks(g, expert, first_round=0):
                if not first_round:
                    chunk(g, 0, 0, expert)
                with sp.Fori(first_round, ROUNDS) as r:
                    for s in range(1, WSLOTS):
                        chunk(g, r, s, expert)

            for L in range(DEPTH):
                for item in range(MIX_ITEMS):
                    s = item % WSLOTS
                    if item >= WSLOTS:
                        done, k = released[item - WSLOTS]
                        sp.wait_ge(*done(L, k))
                    elif L:
                        sp.wait_ge(slot_free[s], chunk_reads(s, first_block(L)))
                    sp.dma_start(W[:, s, :], wmix[L * MIX_ITEMS + item]).then_inc(slot_full[s], 16)
                g0, moe = first_block(L), L % 2
                for s in range(WSLOTS):
                    done, k = released[WSLOTS + s]
                    chunk(g0, 0, s, moe, done(L, k))
                expert_chunks(g0, moe, 1)
                if moe:
                    with sp.Fori(1, N_EXP - 1) as b:
                        expert_chunks(g0 + b, b + 1)
                    sp.wait_ge(*table_ready(L // 2, 1))
                    more = sp.value_load(tabi[0:1, 0:1], min_val=1, max_val=MAX_OVER + 1)
                    with sp.Fori(0, more) as j:
                        expert = sp.value_load(tabi[0:1, bass.ds(j + 1, 1)], min_val=0, max_val=N_EXP)
                        expert_chunks(g0 + (N_EXP - 1) + j, expert)
            for s in range(2):
                chunk(first_block(DEPTH - 1) + (N_EXP - 1) + more, 0, s, 0)
            for i in range(4):
                sp.wait_ge(*moe_added((N_EXP - 1) + more, i + 1))
                half = slice((i // 2) * 512, (i // 2 + 1) * 512)
                sp.dma_start(out[0, (i % 2) * P:(i % 2 + 1) * P, half], X[:, i % 2, half]).then_inc(out_done, 16)
            sp.wait_ge(out_done, 64)

        @block.gpsimd
        def _(pool):
            nc.gpsimd.memset(eps[:, :], EPS)
            nc.gpsimd.memset(ident[:, :], 0.0)
            nc.gpsimd.memset(one[:, :], 1.0).then_inc(const_ready, 1)
            pool.wait_ge(const_ready, 1)

            def cut(t, pattern, base, channel, op, fill):
                return nc.gpsimd.affine_select(out=t[:, :], in_=t[:, :], compare_op=op, fill=fill, base=base,
                                               pattern=pattern, channel_multiplier=channel)
            cut(ident, [[-1, P]], 0, 1, ALU.not_equal, 1.0).then_inc(const_ready, 1)
            for s in range(WSLOTS):
                nc.gpsimd.memset(iota_j[:, s:s + 1], 0.0).then_inc(slot_free[s], 1)
            nc.gpsimd.memset(tri[:, :], 1.0)
            nc.gpsimd.memset(tri_s[:, :], 1.0)
            nc.gpsimd.memset(ones[:, :], 1.0)
            nc.gpsimd.memset(neg_ssd[:, :], 0.0)
            nc.gpsimd.memset(neg_att[:, :], 0.0)
            nc.gpsimd.memset(hpad[:, :, :], 0.0).then_inc(zeros_ready, 1)
            pool.wait_ge(zeros_ready, 1)
            cut(tri, [[1, P]], 0, -1, ALU.is_ge, 0.0)
            cut(tri_s, [[1, P]], 0, -1, ALU.is_gt, 0.0)
            cut(neg_ssd, [[1, P]], 0, -1, ALU.is_ge, MASKED)
            nc.gpsimd.tensor_copy(ident_b[:, :], ident[:, :])
            cut(neg_att, [[-1, P]], 0, 1, ALU.is_ge, MASKED)
            nc.gpsimd.iota(iota_j[:, :], [[1, P]], base=0, channel_multiplier=0,
                           allow_small_or_imprecise_dtypes=True)
            nc.gpsimd.iota(erow[:, :], [[0, FURTHER], [1, N_EXP]], base=1, channel_multiplier=0,
                           allow_small_or_imprecise_dtypes=True).then_inc(const_ready, 1)
            for L in range(DEPTH):
                done, k = released["TA"]
                pool.wait_ge(*done(L, k))
                pool.dma_start(H[:, :, :], mem_in.rearrange("a (t p) d -> p (a t) d", p=P)).then_inc(in_mem, 16)
                if L + 1 < DEPTH:
                    pool.wait_ge(*x_ready(L, 2 * NT))
                    pool.dma_start(cols[:, :], cols_in[L + 1]).then_inc(next_params, 16)
                    pool.dma_start(rows[:, :], rows_in[L + 1:L + 2, :].to_broadcast([P, N_ROWS])) \
                        .then_inc(next_params, 16)

        def act_layer(act, L):
            na = [0]

            def step(ins):
                ins.then_inc(*act_step.up())
                act.wait_ge(*act_step(L, act_step.count(L)))

            def group():
                na[0] += 1
                act.wait_ge(*a_full(L, na[0]))
                return PA[(na[0] - 1) % 4]

            def col(name, at=0):
                return cols[:, COLS[name] + at:COLS[name] + at + 1]

            def copy(dst, src, scale=1.0):
                return act.activation(dst, src, ACT.Copy, scale=scale)

            def pair_of(bank):
                return bank[:, :].rearrange("p (j s) -> p j s", j=2)

            def copy_group(dst, src):
                copy(dst, src).then_inc(*a_free.up())

            def take_tiles(dst, tiles, gain):
                for at in range(0, tiles, 2):
                    bank = group()
                    for j in range(2):
                        last = copy(dst[:, at + j, :], bank[:, j * SEQ:(j + 1) * SEQ], gain(at + j))
                    last.then_inc(*a_free.up())

            def rstd(at, n, width, done):
                step(act.activation(rs[:, at:at + n], ss[:, at:at + n], ACT.Ln, bias=eps[:, :], scale=1.0 / width))
                act.activation(rs[:, at:at + n], rs[:, at:at + n], ACT.Exp, scale=-0.5).then_inc(*done.up())

            def squares(src, at):
                for tt in range(NT):
                    step(act.activation(junk, src[:, tt, :], ACT.Square, accum_out=ss[:, at + tt:at + tt + 1]))

            def x_rstd(tt, done):
                act.wait_ge(*done)
                step(act.activation(junk, X[:, tt, :], ACT.Square, accum_out=ss[:, tt:tt + 1]))
                rstd(tt, 1, D_MODEL, rstd_ready)

            def take_normed(gain):
                for c0 in range(0, KT, 4):
                    bank = group()
                    for j in range(4):
                        last = copy(HT[:, c0 + j, 0:P], bank[:, j * P:(j + 1) * P], gain(c0 + j))
                    last.then_inc(*a_free.up())

            def softmax_exp(tt, keys, ready):
                act.wait_ge(*att_ready(L, ready))
                for h in range(4):
                    last = act.activation(prob[:, tt, h, 0:keys], prob[:, tt, h, 0:keys], ACT.Exp,
                                          bias=nmx[:, tt, h:h + 1], accum_out=psm[:, tt, h:h + 1])
                last.then_inc(*exp_ready.up())

            def take_p(tiles):
                for s in range(tiles):
                    copy_group(pT[:, s, :, :], group()[:, :].rearrange("p (h t) -> p h t", h=4))

            def take_o(dst, tt):
                copy_group(dst[:, :, tt * P:(tt + 1) * P], group()[:, 0:2 * P].rearrange("p (j t) -> p j t", j=2))

            nc.scalar.preload_act_table_set(LOG_EXP)
            for tt in range(NT):
                x_rstd(tt, (in_x[tt], 16) if L == 0 else dense_added(0, 2 * (tt + 1)))
            act.wait_ge(*params_ready(L))
            take_normed(lambda k: col("mix_g", k))
            if L == 0:
                act.wait_ge(trig_step, 1 + NT + 2 + len(TURN_PARTS))
                act.activation(sn_[:, :, :], ang[:, :, :], ACT.Sin)
                act.activation(kay[:, :, :], ang[:, :, :], ACT.Sin, scale=0.5).then_inc(trig_act, 1)
                nc.scalar.preload_act_table_set(LOG_EXP)
            act.wait_ge(const_ready, 3)
            for at in range(0, KT, 2):
                copy_group(XR[:, at:at + 2, 3:3 + SEQ], pair_of(group()))
            copy_group(hpad[:, :, CONV_W - 1:], pair_of(group()))
            act.activation(ctmp[:, :, :], pair_of(group()), ACT.Sigmoid).then_inc(*a_free.up())
            for item in range(4, 8):
                width = WIDE if item < 7 else U_N - 3 * WIDE
                c0 = (item - 4) * WIDE
                for tt in range(NT):
                    copy_group(U[:, tt, c0:c0 + width], group()[:, 0:width])
                if item == 5:
                    for at in range(0, KT, 2):
                        act.wait_ge(*xbc_conv(L, at // 2 + 1))
                        act.activation(XC[:, at:at + 2, :], XC[:, at:at + 2, :], ACT.Silu).then_inc(*xc_ready.up())
                    nc.scalar.preload_act_table_set(LOG_EXP)
            act.wait_ge(*dt_in(L, 1))
            step(act.activation(dts[:, 2, :, :], dts[:, 1, :, :], ACT.Exp, scale=-1.0))
            act.activation(anum[:, :], rows[:, R_ALOG:R_ALOG + SSD_H], ACT.Exp)
            act.activation(dts[:, 2, :, :], dts[:, 2, :, :], ACT.Ln, bias=one[:, :]).then_inc(*dt_log.up())
            act.wait_ge(*qk_ss(L, 1))
            rstd(2, 16, HD, qk_rstd)
            for tt in range(NT):
                act.activation(Z[:, tt, :], group()[:, :], ACT.Silu).then_inc(*a_free.up())
            nc.scalar.preload_act_table_set(LOG_EXP)
            bank = group()
            act.activation(ctmp[:, 0, :], bank[:, 0:SEQ], ACT.Ln, bias=eps[:, :], scale=1.0 / D_CONV) \
                .then_inc(*a_free.up())
            act.wait_ge(*a_free(L, na[0]))
            act.activation(ctmp[:, 0, :], ctmp[:, 0, :], ACT.Exp, scale=-0.5).then_inc(*conv_rstd.up())
            copy_group(btok[:, :, :], group()[:, 0:2 * P].rearrange("p (g n) -> p g n", g=2))
            act.wait_ge(*cum_ready(L, 1))
            act.activation(ecum[:, :, :], ecum[:, :, :], ACT.Exp).then_inc(*ecum_ready.up())
            for tt in range(NT):
                for half in range(2):
                    bank = group()
                    for j in range(4):
                        h = half * 4 + j
                        last = act.activation(LM[:, tt, h, :], bank[:, j * P:(j + 1) * P], ACT.Exp,
                                              bias=ncum[:, tt, h:h + 1])
                    last.then_inc(*a_free.up())
            for at in (0, 2):
                copy_group(qiT[:, at:at + 2, :], pair_of(group()))
            copy_group(kiT[:, :], group()[:, 0:SEQ])
            for at in (0, 2):
                copy_group(qkT[:, at:at + 2, :], pair_of(group()))
            act.wait_ge(*conv_norm(L, 1))
            act.activation(ctmp[:, :, :], cacc[:, :, :], ACT.Silu).then_inc(*conv_out.up())
            nc.scalar.preload_act_table_set(LOG_EXP)
            for n in range(NT * IDX_H // 2):
                keys = P * (n // (IDX_H // 2) + 1)
                bank = group()
                if n >= 2:
                    act.wait_ge(*score_used(L, n - 1))
                act.activation(rl[:, n % 2, :, 0:keys], pair_of(bank)[:, :, 0:keys], ACT.Relu) \
                    .then_inc(*a_free.up())
            copy_group(YT[:, 0:2, :], pair_of(group()))
            copy_group(st[:, :, :], pair_of(group()))
            act.wait_ge(in_mem, 16 * (L + 1))
            act.wait_ge(*score_used(L, NT * IDX_H // 2))
            squares(H, 18)
            rstd(18, NT, D_MODEL, mem_rstd)
            take_tiles(MT, KT, lambda k: col("mem_g", k))
            for tt in range(NT):
                copy_group(kvt[:, tt, :], group()[:, :])
            act.wait_ge(*y_ss(L, 1))
            rstd(28, 4, D_SSD // 2, y_rstd)
            for tt in range(NT):
                softmax_exp(tt, P * (tt + 1), tt + 1)
            act.wait_ge(*hn_ss(L, 1))
            rstd(20, NT * MEM_H, HD, hn_rstd)
            take_tiles(YT[:, 2:6, :], 4, lambda c: col("ssd_g", c))
            for tt in range(NT):
                take_p(tt + 1)
                take_o(YT[:, 6:8, :], tt)
            bank = group()
            copy(KTm[:, :, :], pair_of(bank), col("mk_g")).then_inc(*a_free.up())

            def round_gu(g, t):
                if t >= FT:
                    g, t = g + 1, t - FT
                if t >= 2 or not isinstance(g, int):
                    act.wait_ge(*gu_full(g, t - 1))
                act.wait_ge(*chunk_full(L, g, t))
                copy(WHgu[t % 2], W[:, slot_of(t), 0:GU_COLS]).then_inc(high_gu.sem, 1)

            def round_d(g, t):
                if t >= FT:
                    g, t = g + 1, t - FT
                if t >= 2 or not isinstance(g, int):
                    act.wait_ge(*chunk_done(g, t - 2))
                copy(WHd[t % 2], W[:, slot_of(t), GU_COLS:SLOT]).then_inc(high_d.sem, 1)

            for tt in range(NT):
                x_rstd(tt, x_ready(L, tt + 1))
            take_normed(lambda k: col("memx_g", k))
            copy_group(mq[:, :, :], pair_of(group()))
            bank = group()
            copy(mqT[:, :, :], pair_of(bank), col("mq_g")).then_inc(*a_free.up())
            act.wait_ge(*hn_ss(L, 2))
            rstd(20, NT * MEM_H, HD, hn_rstd)
            for tt in range(NT):
                softmax_exp(tt, SEQ, NT + tt + 1)
            round_gu(first_block(L), 0)
            for tt in range(NT):
                take_p(2)
                take_o(oT, tt)
            round_gu(first_block(L), 1)
            for tt in range(NT):
                x_rstd(tt, x_ready(L, NT + tt + 1))
            act.wait_ge(*ffn_g_ready(L, 1))
            take_normed(lambda k: ffn_g[:, k:k + 1])

            def silu(g, t, n, dst):
                act.wait_ge(*gu_full(g, t + 1))
                act.activation(dst[:, t % 2, :], GU[t % 2][0:dst.shape[0], 0:n], ACT.Silu) \
                    .then_inc(silu_ready.sem, 1)

            if L % 2 == 0:
                g = first_block(L)
                for i in range(4):
                    ks = slice(i * 2, i * 2 + 2)
                    if i == 0:
                        act.wait_ge(*a_free(L, na[0]))
                        act.wait_ge(*v_free(L, RAISES["v_free"]))
                    copy(HTH[:, ks, :], HT[:, ks, :]).then_inc(*x_high.up())

                def act_parts(t):
                    act.wait_ge(*act_ready(g, t + 1))
                    copy(ahd[:, t % 2, :], atd[:, t % 2, :]).then_inc(act_high.sem, 1)

                for t in range(FT):
                    if t:
                        silu(g, t - 1, SEQ, sgd)
                    if 0 < t < FT - 1:
                        round_gu(g, t + 1)
                    if t:
                        act_parts(t - 1)
                    round_d(g, t)
                silu(g, FT - 1, SEQ, sgd)
                act_parts(FT - 1)
                return
            M = L // 2
            act.wait_ge(*top2_ready(M, 1))
            act.activation(rsc[:, 1, :], rsc[:, 0, :], ACT.Exp)
            act.activation(rel[:, :, :], rel[:, :, :], ACT.Exp).then_inc(*top2_exp.up())

            def tokens_high(b):
                act.wait_ge(*hc_ready(b, 2))
                copy(hcH[:, :, :], hcT[:, :, :]).then_inc(hc_high.sem, 1)

            def take_tokens(b, halves=(0, 1)):
                for half in halves:
                    act.wait_ge(*hc_full(b, half + 1))
                    for c in range(4):
                        k = 4 * half + c
                        last = copy(hcT[:, k, :], PV[half][:, c * BLOCK:(c + 1) * BLOCK], ffn_g[:, k:k + 1])
                    last.then_inc(hc_ready.sem, 1)

            take_tokens(0)
            tokens_high(0)
            round_d(first_block(L), 0)
            act.wait_ge(*table_ready(M, 1))
            more = act.value_load(tabi[0:1, 0:1], min_val=1, max_val=MAX_OVER + 1)
            with act.Fori(0, N_EXP - 1 + more) as b:
                g = first_block(L) + b

                def act_parts(t):
                    act.wait_ge(*turned(b, t + 1))
                    copy(aH[:, t % 2, :], PV[3][:, 0:BLOCK]).then_inc(act_high.sem, 1)

                for t in range(FT):
                    if t:
                        silu(g, t - 1, P, sg)
                        round_gu(g, t + 1)
                        act_parts(t - 1)
                        round_d(g, t)
                    if t in (12, 15):
                        take_tokens(b + 1, [t // 15])
                silu(g, FT - 1, P, sg)
                tokens_high(b + 1)
                round_gu(g, FT + 1)
                act_parts(FT - 1)
                round_d(g, FT)
                act.wait_ge(*pgt_full(b, 1))
                copy(PGT[:, :, :], PV[2][0:BLOCK, 0:NT * P].rearrange("p (t j) -> p t j", t=NT)) \
                    .then_inc(pgt_ready.sem, 1)
                act.wait_ge(*chunk_done(g, FT - 1))
                copy(yc[:, 0:512], PA[2][0:BLOCK, :])
                copy(yc[:, 512:1024], PA[3][0:BLOCK, :]).then_inc(yc_ready.sem, 1)

        @block.scalar
        def _(act):
            act.dma_start(pos_i[:, :], pos_in).then_inc(in_small, 16)
            act.dma_start(cols[:, :], cols_in[0]).then_inc(in_params, 16)
            act.dma_start(rows[:, :], rows_in[0:1, :].to_broadcast([P, N_ROWS])).then_inc(in_params, 16)
            act.dma_start(ffn_g2[:, :, :], ffn_g_in).then_inc(in_ffn, 16)
            act.dma_start(wr[:, :, :], router_in).then_inc(in_ffn, 16)
            act.wait_ge(const_ready, 1)
            for L in range(DEPTH):
                act_layer(act, L)

        def dve_layer(dve, L):
            nv = [0]
            v = nc.vector

            def step(ins):
                ins.then_inc(*dve_step.up())
                dve.wait_ge(*dve_step(L, dve_step.count(L)))

            def note(ins):
                ins.then_inc(*dve_step.up())

            def group():
                nv[0] += 1
                dve.wait_ge(*v_full(L, nv[0]))
                return PV[(nv[0] - 1) % 4]

            def col(name, at=0, n=1):
                return cols[:, COLS[name] + at:COLS[name] + at + n]

            def along(ap, n):
                return ap.unsqueeze(len(ap.shape)).to_broadcast(list(ap.shape) + [n])

            def normalise(norm, tt):
                dve.wait_ge(*rstd_ready(L, norm * NT + tt + 1))
                v.tensor_scalar(H[:, tt, :], X[:, tt, :], rs[:, tt:tt + 1], None, ALU.mult).then_inc(*h_ready.up())

            def take_normed(gain):
                for c0 in range(0, KT, 4):
                    bank = group()
                    v.tensor_tensor(HT[:, c0:c0 + 4, P:2 * P], bank[:, :].rearrange("p (c t) -> p c t", c=4),
                                    along(gain[:, c0:c0 + 4], P), ALU.mult).then_inc(*v_free.up())

            def x_done(norm, tt):
                dve.wait_ge(*v_free(L, nv[0]))
                v.tensor_copy(m8[:, tt, norm:norm + 1], one[:, :]).then_inc(*x_ready.up())

            def head_squares(src, width, at, done, tmp_at=prob[:, 0, :, :]):
                n = src.shape[2]
                tmp = tmp_at[:, :, :].rearrange("p h s -> p (h s)")[:, 0:NT * n].rearrange("p (t n) -> p t n", t=NT)
                step(v.tensor_tensor(tmp, src, src, ALU.mult))
                v.tensor_reduce(ss[:, at:at + NT * n // width], tmp.rearrange("p t (h d) -> p (t h) d", d=width),
                                AX_X, ALU.add).then_inc(*done.up())

            def softmax_in(tt, keys, bias):
                for odd in range(2):
                    bank = group()
                    src = bank[:, 0:2 * keys].rearrange("p (h s) -> p h s", h=2)
                    dst = prob[:, tt, :, :].rearrange("p (h o) s -> p o h s", o=2)[:, odd, :, 0:keys]
                    if bias is None:
                        for j in range(2):
                            at = 20 + tt * MEM_H + 2 * j + odd
                            ins = v.tensor_scalar(dst[:, j, :], src[:, j, :], rs[:, at:at + 1], HD ** -0.5,
                                                  ALU.mult, ALU.mult)
                        ins.then_inc(*v_free.up())
                    else:
                        v.scalar_tensor_tensor(out=dst, in0=src, scalar=HD ** -0.5,
                                               in1=bias[:, 0:keys].unsqueeze(1).to_broadcast([P, 2, keys]),
                                               op0=ALU.mult, op1=ALU.add).then_inc(*v_free.up())
                dve.wait_ge(*v_free(L, nv[0]))
                v.tensor_reduce(nmx[:, tt, :], prob[:, tt, :, 0:keys], AX_X, ALU.max, negate=True).then_inc(*att_ready.up())

            def softmax_out(tt, keys, ready):
                dve.wait_ge(*exp_ready(L, ready))
                step(v.reciprocal(prs[:, tt, :], psm[:, tt, :]))
                p = prob[:, tt, :, 0:keys]
                v.tensor_tensor(p, p, along(prs[:, tt, :], keys), ALU.mult) \
                    .then_inc(*p_ready.up())

            def less(dst, whole, high):
                return v.tensor_tensor(dst, whole, high, ALU.subtract)

            def rest_gu(g, t):
                if t >= FT:
                    g, t = g + 1, t - FT
                w, low = (x[:, slot_of(t), 0:GU_COLS] for x in (W, W_R))
                dve.wait_ge(*high_gu(g, t + 1))
                less(low, w, WHgu[t % 2]).then_inc(low_gu.sem, 1)

            for tt in range(NT):
                normalise(0, tt)
            dve.wait_ge(*params_ready(L))
            take_normed(col("mix_g", 0, KT))
            note(v.memset(XR[:, :, 0:3], 0.0))
            dve.wait_ge(*dve_step(L, dve_step.count(L)))
            for tile in range(KT):
                if tile % 2 == 0:
                    dve.wait_ge(*a_free(L, 2 + tile // 2 + 1))
            for at in range(0, KT, 2):
                for tap in range(SSD_CONV):
                    for tile in (at, at + 1):
                        w = col("ssd_w", tile * SSD_CONV + tap)
                        x = XR[:, tile, tap:tap + SEQ]
                        if tap == 0:
                            ins = v.tensor_scalar(XC[:, tile, :], x, w, col("ssd_b", tile), ALU.mult, ALU.add)
                        else:
                            ins = v.scalar_tensor_tensor(out=XC[:, tile, :], in0=x, scalar=w, in1=XC[:, tile, :],
                                                         op0=ALU.mult, op1=ALU.add)
                        if tap == SSD_CONV - 1 and tile % 2:
                            ins.then_inc(*xbc_conv.up())
                        else:
                            note(ins)
                    if tap < SSD_CONV - 1:
                        dve.wait_ge(*dve_step(L, dve_step.count(L)))
            dve.wait_ge(const_ready, 3)
            dve.wait_ge(*a_free(L, 8))
            step(v.tensor_tensor(hpad[:, :, CONV_W - 1:], hpad[:, :, CONV_W - 1:], ctmp[:, :, :], ALU.mult))
            for tap in range(CONV_W):
                for j in range(2):
                    w = col("conv_w", j * CONV_W + tap)
                    x = hpad[:, j, tap:tap + SEQ]
                    if tap == 0:
                        ins = v.tensor_scalar(cacc[:, j, :], x, w, None, ALU.mult)
                    else:
                        dve.wait_ge(*dve_step(L, dve_step.count(L) - 1))
                        ins = v.scalar_tensor_tensor(out=cacc[:, j, :], in0=x, scalar=w, in1=cacc[:, j, :],
                                                     op0=ALU.mult, op1=ALU.add)
                    if tap == CONV_W - 1 and j == 1:
                        ins.then_inc(*conv_acc.up())
                    else:
                        note(ins)
            dve.wait_ge(*a_free(L, 16))
            for tt in range(NT):
                step(v.tensor_tensor(dts[:, 0, tt, :], U[:, tt, U_DT:U_DT + SSD_H], rows[:, R_DTB:R_DTB + SSD_H],
                                     ALU.add))
            v.scalar_tensor_tensor(out=dts[:, 1, :, :], in0=dts[:, 0, :, :], scalar=-1.0, in1=dts[:, 0, :, :],
                                   op0=ALU.mult, op1=ALU.max).then_inc(*dt_in.up())
            dve.wait_ge(*conv_acc(L, 1))
            bank = group()
            v.scalar_tensor_tensor(out=cacc[:, :, :], in0=bank[:, 0:SEQ].unsqueeze(1).to_broadcast([P, 2, SEQ]),
                                   scalar=-1.0 / D_CONV, in1=cacc[:, :, :], op0=ALU.mult, op1=ALU.add) \
                .then_inc(*v_free.up())
            dve.wait_ge(*v_free(L, nv[0]))
            v.tensor_tensor(ctmp[:, :, :], cacc[:, :, :], cacc[:, :, :], ALU.mult).then_inc(*conv_centred.up())
            head_squares(U[:, :, 0:2 * D_ATT], HD, 2, qk_ss)
            dve.wait_ge(*dt_log(L, 1))
            step(v.scalar_tensor_tensor(out=dts[:, 3, :, :], in0=dts[:, 0, :, :], scalar=0.0, in1=dts[:, 2, :, :],
                                        op0=ALU.max, op1=ALU.add))
            an = anum[:, :].unsqueeze(1).to_broadcast([P, NT, SSD_H])
            step(v.tensor_tensor(dts[:, 5, :, :], dts[:, 3, :, :], an, ALU.mult))
            v.tensor_scalar(dts[:, 4, :, :], dts[:, 5, :, :], -1.0, None, ALU.mult).then_inc(*a_ready.up())
            dve.wait_ge(*a_ready(L, 1))
            for tt in range(NT):
                ins = v.tensor_tensor(TA[:, tt, :, :], tri[:, :].unsqueeze(1).to_broadcast([P, SSD_H, P]),
                                      along(dts[:, 4, tt, :], P), ALU.mult)
            ins.then_inc(*a_ready.up())
            if L == 0:
                dve.wait_ge(trig_act, 1)
                step(v.tensor_tensor(cs_[:, :, :], kay[:, :, :], kay[:, :, :], ALU.mult))
                step(v.tensor_scalar(cs_[:, :, :], cs_[:, :, :], -2.0, 1.0, ALU.mult, ALU.add))
            dve.wait_ge(*qk_rstd(L, 1))
            qk = U[:, :, 0:2 * D_ATT]
            for tt in range(NT):
                step(v.tensor_tensor(qk[:, tt, :].rearrange("p (h d) -> p h d", d=HD),
                                     qk[:, tt, :].rearrange("p (h d) -> p h d", d=HD),
                                     along(rs[:, 2 + tt * 8:10 + tt * 8], HD), ALU.mult))
                gains = rows[:, R_QK:R_QK + 2 * HD].rearrange("p (m d) -> p m d", m=2).unsqueeze(2) \
                    .to_broadcast([P, 2, ATT_H, HD])
                step(v.tensor_tensor(qk[:, tt, :].rearrange("p (m h d) -> p m h d", m=2, d=HD),
                                     qk[:, tt, :].rearrange("p (m h d) -> p m h d", m=2, d=HD), gains, ALU.mult))
            heads = U[:, :, 0:U_HEADS * HD].rearrange("p t (h d) -> p t h d", d=HD)
            x1, x2 = heads[:, :, :, 0:8], heads[:, :, :, 8:16]
            c_, s_ = (t[:, :, :].unsqueeze(2).to_broadcast([P, NT, U_HEADS, 8]) for t in (cs_, sn_))
            for i, (x, y) in enumerate(((x1, c_), (x2, s_), (x2, c_), (x1, s_))):
                note(v.tensor_tensor(rt[i][:, :, :, :], x, y, ALU.mult))
            dve.wait_ge(*dve_step(L, dve_step.count(L)))
            for lo, hi in ((0, 2 * ATT_H), (3 * ATT_H, U_HEADS)):
                note(v.tensor_tensor(x1[:, :, lo:hi, :], rt[0][:, :, lo:hi, :], rt[1][:, :, lo:hi, :], ALU.subtract))
                note(v.tensor_tensor(x2[:, :, lo:hi, :], rt[2][:, :, lo:hi, :], rt[3][:, :, lo:hi, :], ALU.add))
            dve.wait_ge(*dve_step(L, dve_step.count(L)))
            note(v.tensor_scalar(U[:, :, U_W:U_W + IDX_H], U[:, :, U_W:U_W + IDX_H],
                                 IDX_H ** -0.5 * HD ** -0.5, None, ALU.mult))
            for j in range(2):
                ins = v.tensor_copy(kk[:, :, j * HD:(j + 1) * HD], U[:, :, U_KI:U_KI + HD])
            ins.then_inc(*rope_ready.up())
            for tt in range(NT):
                bank = group()
                src = bank[:, :].rearrange("p (h d) -> p h d", h=SSD_H)
                note(v.tensor_tensor(xd[:, tt, :].rearrange("p (h d) -> p h d", h=SSD_H), src,
                                     along(dts[:, 3, tt, :], SSD_P), ALU.mult))
                v.tensor_tensor(ysk[:, tt, :].rearrange("p (h d) -> p h d", h=SSD_H), src,
                                along(rows[:, R_D:R_D + SSD_H], SSD_P), ALU.mult).then_inc(*v_free.up())
            bank = group()
            v.tensor_copy(cum[:, :, :, :], bank[:, 0:32].rearrange("p (t k h) -> p t k h", t=NT, k=2)) \
                .then_inc(*v_free.up())
            dve.wait_ge(*v_free(L, nv[0]))
            note(v.tensor_scalar(ncum[:, :, :], cum[:, :, 0, :], -1.0, None, ALU.mult))
            note(v.tensor_tensor(ecum[:, 0, :], cum[:, 0, 1, :], cum[:, 0, 0, :], ALU.subtract))
            v.tensor_copy(ecum[:, 1, :], cum[:, 1, 0, :]).then_inc(*cum_ready.up())
            dve.wait_ge(*conv_rstd(L, 1))
            step(v.tensor_tensor(cacc[:, :, :], cacc[:, :, :], ctmp[:, 0, :].unsqueeze(1).to_broadcast([P, 2, SEQ]),
                                 ALU.mult))
            for j in range(2):
                ins = v.tensor_scalar(cacc[:, j, :], cacc[:, j, :], col("ln_g", j), col("ln_b", j),
                                      ALU.mult, ALU.add)
            ins.then_inc(*conv_norm.up())
            dve.wait_ge(*ecum_ready(L, 1))
            v.tensor_tensor(xdd[:, :].rearrange("p (h d) -> p h d", h=SSD_H),
                            xd[:, 0, :].rearrange("p (h d) -> p h d", h=SSD_H), along(ecum[:, 0, :], SSD_P),
                            ALU.mult).then_inc(*xdd_ready.up())
            bank = group()
            dve.wait_ge(*a_free(L, A_SEG))
            for tt in range(NT):
                cb = bank[:, tt * 2 * P:(tt + 1) * 2 * P].rearrange("p (g l) -> p g l", g=2).unsqueeze(2) \
                    .to_broadcast([P, 2, 4, P])
                lm = LM[:, tt, :, :].rearrange("p (g h) l -> p g h l", g=2)
                v.tensor_tensor(lm, lm, cb, ALU.mult).then_inc(*m_ready.up())
            dve.wait_ge(*m_ready(L, NT))
            v.tensor_copy(m8[:, 0, 0:1], one[:, :]).then_inc(*v_free.up())
            n = 0
            for tt in range(NT):
                keys = P * (tt + 1)
                for pair in range(IDX_H // 2):
                    n += 1
                    dve.wait_ge(*a_free(L, A_INDEX + n))
                    for j in range(2):
                        h = index_head(pair, j)
                        w = U[:, tt, U_W + h:U_W + h + 1]
                        x, s = rl[:, (n - 1) % 2, j, 0:keys], score[:, tt, 0:keys]
                        if h == 0:
                            step(v.tensor_scalar(s, x, w, None, ALU.mult))
                        elif j == 0:
                            step(v.scalar_tensor_tensor(out=s, in0=x, scalar=w, in1=s, op0=ALU.mult, op1=ALU.add))
                        else:
                            v.scalar_tensor_tensor(out=s, in0=x, scalar=w, in1=s, op0=ALU.mult, op1=ALU.add) \
                                .then_inc(*score_used.up())
                            dve.wait_ge(*score_used(L, n))
            dve.wait_ge(*mem_rstd(L, 1))
            for tt in range(NT):
                v.tensor_scalar(H[:, tt, :], H[:, tt, :], rs[:, 18 + tt:19 + tt], None, ALU.mult) \
                    .then_inc(*mem_ready.up())
            for tt in range(NT):
                bank = group()
                v.tensor_tensor(ysk[:, tt, :], ysk[:, tt, :], bank[:, :], ALU.add).then_inc(*v_free.up())
            bank = group()
            v.tensor_tensor(xd[:, 1, :].rearrange("p (h d) -> p h d", h=SSD_H),
                            bank[:, :].rearrange("p (h d) -> p h d", h=SSD_H), along(ecum[:, 1, :], SSD_P),
                            ALU.mult).then_inc(*v_free.up())
            dve.wait_ge(*v_free(L, nv[0]))
            step(v.tensor_tensor(ysk[:, 1, :], ysk[:, 1, :], xd[:, 1, :], ALU.add))
            step(v.tensor_tensor(ysk[:, :, :], ysk[:, :, :], Z[:, :, :], ALU.mult))
            head_squares(ysk[:, :, :], D_SSD // 2, 28, y_ss)
            for tt in range(NT):
                d = slice(tt * P, (tt + 1) * P)
                note(v.tensor_tensor(score[:, tt, d], score[:, tt, d], neg_att[:, :], ALU.add))
            for i in range(TOPK // 8):
                dve.wait_ge(*dve_step(L, dve_step.count(L)))
                for tt in range(NT):
                    note(v.max(m8[:, tt, :], score[:, tt, 0:P * (tt + 1)]))
                dve.wait_ge(*dve_step(L, dve_step.count(L)))
                for tt in range(NT):
                    s = score[:, tt, 0:P * (tt + 1)]
                    note(v.match_replace(s, m8[:, tt, :], s, TAKEN))
            dve.wait_ge(*dve_step(L, dve_step.count(L)))
            for tt in range(NT):
                keys = P * (tt + 1)
                note(v.tensor_scalar(abias[:, tt, 0:keys], score[:, tt, 0:keys], TAKEN, MASKED,
                                     ALU.not_equal, ALU.mult))
            dve.wait_ge(*dve_step(L, dve_step.count(L)))
            for tt in range(NT):
                d = slice(tt * P, (tt + 1) * P)
                note(v.tensor_tensor(abias[:, tt, d], abias[:, tt, d], neg_att[:, :], ALU.add))
            dve.wait_ge(*y_ss(L, 1))
            dve.wait_ge(*dve_step(L, dve_step.count(L)))
            for tt in range(NT):
                softmax_in(tt, P * (tt + 1), abias[:, tt, :])
            dve.wait_ge(*y_rstd(L, 1))
            yh = ysk[:, :, :].rearrange("p t (g d) -> p t g d", g=2)
            v.tensor_tensor(yh, yh, along(rs[:, 28:32].rearrange("p (t g) -> p t g", t=NT), SEQ), ALU.mult) \
                .then_inc(*y_ready.up())
            dve.wait_ge(*a_free(L, A_KV))
            head_squares(kvt[:, :, 0:D_ATT], HD, 20, hn_ss, tmp_at=cacc)
            for tt in range(NT):
                softmax_out(tt, P * (tt + 1), tt + 1)
            dve.wait_ge(*hn_rstd(L, 1))
            kh = kvt[:, :, 0:D_ATT].rearrange("p t (h d) -> p t h d", d=HD)
            v.tensor_tensor(kh, kh, along(rs[:, 20:28].rearrange("p (t h) -> p t h", t=NT), HD), ALU.mult) \
                .then_inc(*hn_ready.up())
            dve.wait_ge(in_ffn, 32)
            v.tensor_copy(ffn_g[:, :], ffn_g2[:, L, :]).then_inc(*ffn_g_ready.up())
            for tt in range(NT):
                for item in range(12, 15):
                    c0 = (item - 12) * WIDE
                    width = min(WIDE, D_MODEL - c0)
                    bank = group()
                    x = X[:, tt, c0:c0 + width]
                    v.tensor_tensor(x, x, bank[:, 0:width], ALU.add).then_inc(*v_free.up())
                x_done(0, tt)
                normalise(1, tt)
            take_normed(col("memx_g", 0, KT))
            dve.wait_ge(*a_free(L, A_MQ))
            head_squares(mq[:, :, :], HD, 20, hn_ss)
            dve.wait_ge(*hn_rstd(L, 2))
            for tt in range(NT):
                softmax_in(tt, SEQ, None)
            for tt in range(NT):
                softmax_out(tt, SEQ, NT + tt + 1)
            rest_gu(first_block(L), 0)
            for tt in range(NT):
                for half in range(2):
                    bank = group()
                    x = X[:, tt, half * 512:(half + 1) * 512]
                    v.tensor_tensor(x, x, bank[:, :], ALU.add).then_inc(*v_free.up())
                x_done(1, tt)
                normalise(2, tt)
            take_normed(ffn_g)
            if L % 2:
                rest_gu(first_block(L), 1)

            def activate(g, t, n, src, dst):
                i = t % 2
                dve.wait_ge(*silu_ready(g, t + 1))
                v.tensor_tensor(dst[:, i, :], src[:, i, :], GU[i][0:dst.shape[0], n:2 * n], ALU.mult) \
                    .then_inc(act_ready.sem, 1)

            def rest_d(g, t):
                if t >= FT:
                    g, t = g + 1, t - FT
                w, low = (x[:, slot_of(t), GU_COLS:SLOT] for x in (W, W_R))
                dve.wait_ge(*high_d(g, t + 1))
                less(low, w, WHd[t % 2]).then_inc(low_d.sem, 1)

            if L % 2 == 0:
                g = first_block(L)
                for i in range(4):
                    ks = slice(i * 2, i * 2 + 2)
                    dve.wait_ge(*x_high(0, i + 1))
                    less(HTL[:, ks, :], HT[:, ks, :], HTH[:, ks, :]).then_inc(*x_low.up())
                rest_gu(g, 1)

                def act_rest(t):
                    dve.wait_ge(*act_high(g, t + 1))
                    less(ald[:, t % 2, :], atd[:, t % 2, :], ahd[:, t % 2, :]) \
                        .then_inc(act_low.sem, 1)

                for t in range(FT):
                    if t:
                        activate(g, t - 1, SEQ, sgd, atd)
                    if 0 < t < FT - 1:
                        rest_gu(g, t + 1)
                    if t:
                        act_rest(t - 1)
                    rest_d(g, t)
                activate(g, FT - 1, SEQ, sgd, atd)
                act_rest(FT - 1)
                dve.wait_ge(*chunk_done(g, FT - 1))
                for i, bank in enumerate((PA[2], PA[3], PV[0], PV[1])):
                    x = X[:, i // 2, (i % 2) * 512:(i % 2 + 1) * 512]
                    v.tensor_tensor(x, x, bank[:, :], ALU.add).then_inc(*dense_added.up())
                dve.wait_ge(*dense_added(0, 4))
                return
            M = L // 2

            def step(ins):
                ins.then_inc(*router_step.up())
                dve.wait_ge(*router_step(M, router_step.count(M)))

            def note(ins):
                ins.then_inc(*router_step.up())

            def noted():
                dve.wait_ge(*router_step(M, router_step.count(M)))

            dve.wait_ge(*router_full(M, 1))
            step(v.tensor_copy(rin[:, :, 0:N_EXP], PV[2][:, 0:NT * N_EXP].rearrange("p (t e) -> p t e", t=NT)))
            for tt in range(NT):
                note(v.max(m8[:, tt, :], rin[:, tt, 0:N_EXP]))
            noted()
            note(v.tensor_tensor(rsc[:, 0, :], m8[:, :, 1], m8[:, :, 0], ALU.subtract))
            step(v.tensor_copy(tr[:, :, 0:2], m8[:, :, 0:2]))
            for tt in range(NT):
                note(v.tensor_scalar(rel[:, tt, :], rin[:, tt, 0:N_EXP], m8[:, tt, 0:1], None, ALU.subtract))
                note(v.match_replace(mr[:, tt, :], tr[:, tt, :], rin[:, tt, :], PICKED))
            noted()
            v.tensor_scalar(rmask[:, :, :], mr[:, :, 0:N_EXP], PICKED, None, ALU.is_equal).then_inc(*mask_ready.up())
            v.tensor_copy(tabf[:, 7:8], one[:, :]).then_inc(*top2_ready.up())
            dve.wait_ge(*top2_exp(M, 1))
            dve.wait_ge(*mask_ready(M, 1))
            note(v.tensor_scalar(rsc[:, 2, :], rsc[:, 1, :], 1.0, None, ALU.add))
            step(v.tensor_tensor(gate[:, :, 0:N_EXP], rel[:, :, :], rmask[:, :, :], ALU.mult))
            step(v.reciprocal(rsc[:, 3, :], rsc[:, 2, :]))
            step(v.tensor_tensor(gate[:, :, 0:N_EXP], gate[:, :, 0:N_EXP], along(rsc[:, 3, :], N_EXP), ALU.mult))
            dve.wait_ge(*router_full(M, 2))
            bank = PV[3]
            step(v.scalar_tensor_tensor(out=posm[:, :, 0:N_EXP], in0=bank[:, 0:NT * N_EXP]
                                        .rearrange("p (t e) -> p t e", t=NT), scalar=1.0, in1=rmask[:, :, :],
                                        op0=ALU.add, op1=ALU.mult))
            step(v.tensor_scalar(posm[:, :, 0:N_EXP], posm[:, :, 0:N_EXP], -1.0, None, ALU.add))

            def place(dst, b, gates, done):
                for tt in range(NT):
                    col_b = BT[:, tt, bass.ds(b, 1)]
                    if gates:
                        ins = v.tensor_scalar(dst[:, tt, :], iota_j[:, 0:BLOCK], col_b, GT[:, tt, bass.ds(b, 1)],
                                              ALU.is_equal, ALU.mult)
                    else:
                        ins = v.tensor_scalar(dst[:, tt, :], iota_j[:, 0:BLOCK], col_b, None, ALU.is_equal)
                ins.then_inc(done.sem, 1)

            step(v.tensor_copy(BT[:, :, 0:N_EXP], posm[:, :, 0:N_EXP]))
            place(PM, 0, False, pm_ready)
            note(v.tensor_copy(GT[:, :, 0:N_EXP], gate[:, :, 0:N_EXP]))
            for i in range(FURTHER):
                c = slice(i * N_EXP, (i + 1) * N_EXP)
                if i:
                    note(v.tensor_scalar(posm[:, :, c], posm[:, :, 0:N_EXP], -float(i * BLOCK), None, ALU.add))
                    note(v.tensor_copy(gate[:, :, c], gate[:, :, 0:N_EXP]))
                ins = v.tensor_scalar(cnt[:, 0, c], bank[:, 16:24], (i + 1) * BLOCK + 0.5, None, ALU.is_gt)
                if i < FURTHER - 1:
                    note(ins)
                else:
                    ins.then_inc(*router_read.up())
            noted()
            dve.wait_ge(*router_read(M, 1))
            step(v.tensor_tensor_scan(cnt[:, 1, :], ones[:, 0:N_CAND], cnt[:, 0, :], 0.0, ALU.mult, ALU.add))
            for k in range(MAX_OVER):
                note(v.scalar_tensor_tensor(out=oh[:, k, :], in0=cnt[:, 1, :], scalar=float(k + 1), in1=cnt[:, 0, :],
                                            op0=ALU.is_equal, op1=ALU.mult))
            note(v.tensor_scalar(tabf[:, 0:1], cnt[:, 1, N_CAND - 1:N_CAND], 1.0, None, ALU.add))
            noted()
            for k in range(MAX_OVER):
                for i, (x, at, dst) in enumerate(((erow[:, :], 0.0, tabf[:, 2 + k:3 + k]),
                                   (posm[:, 0, :], -float(BLOCK), BT[:, 0, N_EXP + k:N_EXP + k + 1]),
                                   (posm[:, 1, :], -float(BLOCK), BT[:, 1, N_EXP + k:N_EXP + k + 1]),
                                   (gate[:, 0, :], 0.0, GT[:, 0, N_EXP + k:N_EXP + k + 1]),
                                   (gate[:, 1, :], 0.0, GT[:, 1, N_EXP + k:N_EXP + k + 1]))):
                    note(v.tensor_tensor_reduce(rtmp[:, 5 * k + i, :], oh[:, k, :], x, 1.0, at, ALU.mult, ALU.add, dst))
            noted()
            v.tensor_copy(tabi[:, :], tabf[:, :]).then_inc(*table_ready.up())
            dve.wait_ge(*table_ready(M, 1))

            more = dve.value_load(tabi[0:1, 0:1], min_val=1, max_val=MAX_OVER + 1)

            def add(q, i):
                dve.wait_ge(*sc_full(q, i + 1))
                x = X[:, i % 2, (i // 2) * 512:(i // 2 + 1) * 512]
                v.tensor_tensor(x, x, PV[i % 2][:, :], ALU.add).then_inc(moe_added.sem, 1)

            v.memset(yc, 0.0).then_inc(yc_ready.sem, 1)
            v.memset(PGT[:, :, :], 0.0).then_inc(pgt_ready.sem, 1)

            def tokens_low(b):
                dve.wait_ge(*hc_high(b, 1))
                less(hcL[:, :, :], hcT[:, :, :], hcH[:, :, :]).then_inc(hc_low.sem, 1)

            tokens_low(0)
            rest_d(first_block(L), 0)
            with dve.Fori(0, N_EXP - 1 + more) as b:
                g = first_block(L) + b

                def act_rest(t):
                    dve.wait_ge(*act_high(g, t + 1))
                    less(aL[:, t % 2, :], PV[3][:, 0:BLOCK], aH[:, t % 2, :]) \
                        .then_inc(act_low.sem, 1)

                for t in range(FT):
                    if t:
                        activate(g, t - 1, P, sg, at_)
                        rest_gu(g, t + 1)
                        act_rest(t - 1)
                        rest_d(g, t)
                    if t in (2, 4, 6, 8):
                        add(b, t // 2 - 1)
                    if t == 3:
                        place(PM, b + 1, False, pm_ready)
                    if t == 9:
                        place(PG, b, True, pg_ready)
                activate(g, FT - 1, P, sg, at_)
                tokens_low(b + 1)
                act_rest(FT - 1)
                rest_gu(g, FT + 1)
                rest_d(g, FT)
            for i in range(4):
                add(N_EXP - 1 + more, i)

        @block.vector
        def _(dve):
            for j in range(8):
                nc.vector.memset(inv[:, j:j + 1], ROPE_THETA ** (-2.0 * j / ROT))
            nc.vector.memset(rin[:, :, :], PAD)
            nc.vector.memset(tr[:, :, :], PAD).then_inc(act_ready.sem, 1)
            nc.vector.memset(BT[:, :, :], -1.0)
            nc.vector.memset(tabf[:, :], float(N_EXP)).then_inc(set_up, 1)
            dve.wait_ge(set_up, 1)
            dve.wait_ge(in_small, 16)
            n = [0]

            def link(ins):
                n[0] += 1
                ins.then_inc(trig_step, 1)
                dve.wait_ge(trig_step, n[0])
            link(nc.vector.tensor_copy(pos_f[:, :], pos_i[:, :]))
            for t in range(NT):
                link(nc.vector.tensor_scalar(ang[:, t, :], inv[:, :], pos_f[:, t:t + 1], None, ALU.mult))
            link(nc.vector.tensor_scalar(kay[:, :, :], ang[:, :, :], 1.0 / TWO_PI, ROUND_BIG, ALU.mult, ALU.add))
            link(nc.vector.tensor_scalar(kay[:, :, :], kay[:, :, :], -ROUND_BIG, None, ALU.add))
            for part in TURN_PARTS:
                link(nc.vector.scalar_tensor_tensor(out=ang[:, :, :], in0=kay[:, :, :], scalar=-part,
                                                    in1=ang[:, :, :], op0=ALU.mult, op1=ALU.add))
            for L in range(DEPTH):
                dve_layer(dve, L)


def kernel(**inputs):
    import numpy as np
    import concourse.bacc as bacc
    from concourse.bass_utils import run_bass_kernel_spmd

    a = {k: np.asarray(v) for k, v in inputs.items()}

    def tiles(w):
        return w.reshape(-1, P, w.shape[-1]).transpose(1, 0, 2).reshape(P, -1)

    def column(v):
        return v.reshape(-1, P).T

    cols, rows, wmix = [], [], np.zeros((DEPTH * MIX_ITEMS, P, SLOT), np.float32)
    for l in range(DEPTH):
        w_in, w_out, w_kv = a["w_in"][l], a["w_out"][l], a["memx_w_kv"][l]
        dw = a["conv_dw_w"][l].T.reshape(2, P, CONV_W).transpose(1, 0, 2).reshape(P, -1)
        sw = a["ssd_conv_w"][l].T.reshape(KT, P, SSD_CONV).transpose(1, 0, 2).reshape(P, -1)
        twice = [np.concatenate([a[n][l]] * 2)[:, None] for n in ("memx_q_norm_g", "memx_k_norm_g")]
        cols.append(np.concatenate([column(a["mix_norm_g"][l]), column(a["memx_norm_g"][l]),
                                    column(a["mem_norm_g"][l]), dw, column(a["conv_ln_g"][l]),
                                    column(a["conv_ln_b"][l]), sw, column(a["ssd_conv_b"][l]),
                                    column(a["ssd_norm_g"][l])] + twice, axis=1))
        rows.append(np.concatenate([a["att_q_norm_g"][l], a["att_k_norm_g"][l], a["ssd_dt_bias"][l],
                                    a["ssd_a_log"][l], a["ssd_d"][l]]))
        xbc_conv = np.concatenate([w_in[:, 1024:2048], w_in[:, 0:512]], axis=1)
        u = np.concatenate([w_in[:, 2056:3408], w_in[:, 2048:2056]], axis=1)
        items = [tiles(xbc_conv[:, i * WIDE:(i + 1) * WIDE]) for i in range(4)]
        items += [tiles(u[:, i * WIDE:(i + 1) * WIDE]) for i in range(4)]
        items += [tiles(w_in[:, 512:512 + WIDE]),
                  np.concatenate([tiles(w_in[:, 512 + WIDE:1024]), tiles(a["conv_pw_w"][l])], axis=1)]
        items += [tiles(w_kv[:, 0:WIDE]), tiles(w_kv[:, WIDE:])]
        w_o = a["memx_w_o"][l]
        items += [tiles(w_out[:, 0:WIDE]), tiles(w_out[:, WIDE:2 * WIDE]),
                  np.concatenate([tiles(w_out[:, 2 * WIDE:]), w_o[0:P]], axis=1),
                  np.concatenate([tiles(a["memx_w_q"][l]), w_o[P:2 * P]], axis=1)]
        for i, item in enumerate(items):
            wmix[l * MIX_ITEMS + i, :, 0:item.shape[1]] = item
    wffn = np.empty(((1 + N_EXP) * FT, P, SLOT), np.float32)
    for kind, at in (("w_gate", 0), ("w_up", KT * P)):
        for e in range(1 + N_EXP):
            w = a["ffn_" + kind][0] if e == 0 else a["moe_" + kind][0][e - 1]
            wffn[e * FT:(e + 1) * FT, :, at:at + KT * P] = \
                w.reshape(KT, P, FT, P).transpose(2, 1, 0, 3).reshape(FT, P, KT * P)
    for e in range(1 + N_EXP):
        w = a["ffn_w_down"][0] if e == 0 else a["moe_w_down"][0][e - 1]
        wffn[e * FT:(e + 1) * FT, :, 2 * KT * P:] = w.reshape(FT, P, D_MODEL)

    arrays = {
        "x_dram": a["x"], "mem_dram": a["mem"],
        "positions_dram": np.ascontiguousarray(a["positions"].reshape(NT, P).T),
        "cols_dram": np.stack(cols), "rows_dram": np.stack(rows),
        "ffn_g_dram": np.ascontiguousarray(a["ffn_norm_g"].reshape(DEPTH, KT, P).transpose(2, 0, 1)),
        "router_dram": np.ascontiguousarray(tiles(a["moe_w_router"][0]).reshape(P, KT, N_EXP)),
        "wmix_dram": wmix, "wffn_dram": wffn,
    }
    nc = bacc.Bacc("TRN2", target_bir_lowering=False, num_devices=1)
    args = [nc.dram_tensor(n, v.shape, mybir.dt.from_np(v.dtype), kind="ExternalInput").ap()
            for n, v in arrays.items()]
    args.append(nc.dram_tensor("out_dram", (1, SEQ, D_MODEL), F32, kind="ExternalOutput").ap())
    trunk_kernel(nc, *args)
    r = run_bass_kernel_spmd(nc, [arrays], core_ids=[0])
    return r.results[0]["out_dram"]
```
